# Optimizing a Trainium2 kernel written in Bass

```python
import jax, jax.numpy as jnp
from jax import lax
import numpy as np

D_MODEL = 1024
BATCH = 1
SEQ = 512
DEPTH = 1
DEC_BATCH = 1
DEC_SEQ = 32
PAST_LEN = 512

CHUNK = 64
GLA_HEADS = 4
GLA_DV = D_MODEL // 2 // GLA_HEADS
GLA_DK = GLA_DV // 2
GLA_GATE_RANK = 16
GLA_TAU = 16.0
GLA_WIDTH = GLA_HEADS * GLA_DV
SWA_HEAD_DIM = 64
SWA_Q_HEADS = D_MODEL // 2 // SWA_HEAD_DIM
SWA_KV_HEADS = 2
SWA_GROUP = SWA_Q_HEADS // SWA_KV_HEADS
SWA_WIDTH = SWA_Q_HEADS * SWA_HEAD_DIM
WINDOW = 128
WINDOW_CHUNKS = WINDOW // CHUNK
MIX_WIDTH = GLA_WIDTH + SWA_WIDTH
N_GROUPS = 4
EXPERTS_PER_GROUP = 8
EXPERT_FF = 256
TOP_K_INNER = 2
DEEPNORM_ALPHA = (2.0 * DEPTH) ** 0.25
DEEPNORM_BETA = (8.0 * DEPTH) ** -0.25
LN_EPS = 1e-5
NEG_INF = -1e30
IN_SPLITS = (GLA_HEADS * GLA_DK, GLA_HEADS * GLA_DK, GLA_WIDTH, GLA_WIDTH, GLA_GATE_RANK,
             SWA_WIDTH, SWA_KV_HEADS * SWA_HEAD_DIM, SWA_KV_HEADS * SWA_HEAD_DIM)
IN_WIDTH = sum(IN_SPLITS)

kernel_name = "hymba_gla_swa_sink_hmoe_deepnorm_adaln_stream_step"

def layer_norm(x, g, b):
    xf = x.astype(jnp.float32)
    mu = jnp.mean(xf, -1, keepdims=True)
    var = jnp.mean(jnp.square(xf - mu), -1, keepdims=True)
    return ((xf - mu) * lax.rsqrt(var + LN_EPS) * g + b).astype(x.dtype)

def alibi_slopes():
    s = 2.0 ** (-(8.0 / SWA_Q_HEADS) * np.arange(1, SWA_Q_HEADS + 1))
    return jnp.asarray(s.astype(np.float32).reshape(SWA_KV_HEADS, SWA_GROUP))

def adaln(c, ada_w, ada_b):
    mod = jax.nn.silu(c) @ ada_w + ada_b
    return [m[:, None, :] for m in jnp.split(mod, 6, axis=-1)]

def in_proj(h, w_in, a2_w, a2_b):
    B, L, _ = h.shape
    cuts = [int(i) for i in np.cumsum(IN_SPLITS)[:-1]]
    gq, gk, gv, gr, ga, sq, sk, sv = jnp.split(h @ w_in, cuts, axis=-1)
    loga = jax.nn.log_sigmoid((ga @ a2_w + a2_b).astype(jnp.float32)) / GLA_TAU
    return (gq.reshape(B, L, GLA_HEADS, GLA_DK) * GLA_DK ** -0.5,
            gk.reshape(B, L, GLA_HEADS, GLA_DK),
            gv.reshape(B, L, GLA_HEADS, GLA_DV),
            gr.reshape(B, L, GLA_HEADS, GLA_DV),
            loga.reshape(B, L, GLA_HEADS, GLA_DK),
            sq.reshape(B, L, SWA_KV_HEADS, SWA_GROUP, SWA_HEAD_DIM),
            sk.reshape(B, L, SWA_KV_HEADS, SWA_HEAD_DIM),
            sv.reshape(B, L, SWA_KV_HEADS, SWA_HEAD_DIM))

def gla_chunk_causal(q, k, v, loga, s0, chunk):
    f32 = jnp.float32
    B, L, H, _ = q.shape
    N = L // chunk
    q = q.astype(f32).reshape(B, N, chunk, H, GLA_DK)
    k = k.astype(f32).reshape(B, N, chunk, H, GLA_DK)
    v = v.astype(f32).reshape(B, N, chunk, H, GLA_DV)
    b = jnp.cumsum(loga.reshape(B, N, chunk, H, GLA_DK), axis=2)
    eb, ebn = jnp.exp(b), jnp.exp(-b)
    a_lo = jnp.einsum('bnthk,bnshk->bnhts', q * eb, k * ebn)
    a_up = jnp.einsum('bnthk,bnshk->bnhts', q * ebn, k * eb)
    pos = jnp.arange(chunk)
    a = jnp.where(pos[:, None] >= pos[None, :], a_lo, a_up)
    o = jnp.einsum('bnhts,bnshv->bnthv', a, v)
    b_end = b[:, :, -1]
    u = jnp.einsum('bnshk,bnshv->bnhkv', k * jnp.exp(b_end[:, :, None] - b), v)

    def step(s, gu):
        g, uc = gu
        return g[..., None] * s + uc, s

    s_fin, s_prev = lax.scan(step, s0.astype(f32),
                             (jnp.moveaxis(jnp.exp(b_end), 1, 0), jnp.moveaxis(u, 1, 0)))
    s_prev = jnp.moveaxis(s_prev, 0, 1)
    o = o + jnp.einsum('bnthk,bnhkv->bnthv', q * eb, s_prev)
    return o.reshape(B, L, H, GLA_DV), s_fin

def sink_attention(q, k, v, dist, valid, slopes, sinks):
    s = jnp.einsum('bnqhgd,bnkhd->bnhgqk', q, k).astype(jnp.float32) * SWA_HEAD_DIM ** -0.5
    s = s - slopes[:, :, None, None] * dist[None, None]
    s = jnp.where(valid[None, :, None, None], s, NEG_INF)
    sink = jnp.broadcast_to(sinks[:, :, None, None], s.shape[:-1] + (1,))
    p = jax.nn.softmax(jnp.concatenate([s, sink], axis=-1), axis=-1)[..., :-1]
    return jnp.einsum('bnhgqk,bnkhd->bnqhgd', p.astype(v.dtype), v)

def swa_prompt(sq, sk, sv, slopes, sinks):
    B, L = sq.shape[:2]
    N = L // CHUNK
    pad = WINDOW_CHUNKS * CHUNK
    kp = jnp.pad(sk, ((0, 0), (pad, 0), (0, 0), (0, 0))).reshape(B, N + WINDOW_CHUNKS, CHUNK, SWA_KV_HEADS, SWA_HEAD_DIM)
    vp = jnp.pad(sv, ((0, 0), (pad, 0), (0, 0), (0, 0))).reshape(B, N + WINDOW_CHUNKS, CHUNK, SWA_KV_HEADS, SWA_HEAD_DIM)
    kband = jnp.concatenate([kp[:, w:w + N] for w in range(WINDOW_CHUNKS + 1)], axis=2)
    vband = jnp.concatenate([vp[:, w:w + N] for w in range(WINDOW_CHUNKS + 1)], axis=2)
    qi = jnp.arange(CHUNK)[:, None]
    kj = jnp.arange((WINDOW_CHUNKS + 1) * CHUNK)[None, :]
    dist = jnp.abs(qi + pad - kj).astype(jnp.float32)
    valid = (jnp.arange(N)[:, None, None] * CHUNK - pad + kj[None]) >= 0
    qb = sq.reshape(B, N, CHUNK, SWA_KV_HEADS, SWA_GROUP, SWA_HEAD_DIM)
    o = sink_attention(qb, kband, vband, dist, valid, slopes, sinks)
    return o.reshape(B, L, SWA_KV_HEADS, SWA_GROUP, SWA_HEAD_DIM)

def swa_sample(sq, sk, sv, k_cache, v_cache, slopes, sinks):
    S = sq.shape[1]
    Lc = k_cache.shape[1]
    k_all = jnp.concatenate([k_cache.astype(sk.dtype), sk], axis=1)
    v_all = jnp.concatenate([v_cache.astype(sv.dtype), sv], axis=1)
    dist = jnp.abs(jnp.arange(S)[:, None] + Lc - jnp.arange(Lc + S)[None, :]).astype(jnp.float32)
    valid = jnp.ones((1, 1, Lc + S), dtype=bool)
    o = sink_attention(sq[:, None], k_all[:, None], v_all[:, None], dist, valid, slopes, sinks)[:, 0]
    return o, k_all[:, -Lc:], v_all[:, -Lc:]

def mixer_out(o_gla, gr, gla_norm_w, o_swa, w_o, dtype):
    B, L = o_gla.shape[:2]
    og = o_gla * lax.rsqrt(jnp.mean(jnp.square(o_gla), -1, keepdims=True) + LN_EPS) * gla_norm_w
    og = og * jax.nn.silu(gr.astype(jnp.float32))
    mixed = jnp.concatenate([og.reshape(B, L, GLA_WIDTH).astype(dtype),
                             o_swa.reshape(B, L, SWA_WIDTH).astype(dtype)], axis=-1)
    return mixed @ w_o

def hier_moe(h, rg_w, rg_b, re_w, re_b, w_gate, w_up, w_down):
    B, L, D = h.shape
    t = h.reshape(-1, D)
    g_logits = (t @ rg_w + rg_b).astype(jnp.float32)
    g_prob = jax.nn.softmax(g_logits, axis=-1)
    grp = jnp.argmax(g_logits, axis=-1)
    p_grp = jnp.take_along_axis(g_prob, grp[:, None], axis=-1)
    e_logits = (jnp.einsum('td,gde->tge', t, re_w) + re_b).astype(jnp.float32)
    e_sel = jnp.take_along_axis(e_logits, grp[:, None, None], axis=1)[:, 0]
    top_v, top_i = lax.top_k(e_sel, TOP_K_INNER)
    top_w = jax.nn.softmax(top_v, axis=-1) * p_grp
    exp_w = jnp.sum(jax.nn.one_hot(top_i, EXPERTS_PER_GROUP, dtype=jnp.float32) * top_w[..., None], axis=1)
    combine = (jax.nn.one_hot(grp, N_GROUPS, dtype=jnp.float32)[:, :, None] * exp_w[:, None, :]).astype(t.dtype)
    y = jnp.zeros_like(t)
    for g in range(N_GROUPS):
        hid = jax.nn.silu(jnp.einsum('td,edf->tef', t, w_gate[g])) * jnp.einsum('td,edf->tef', t, w_up[g])
        y = y + jnp.einsum('tef,efd->td', hid * combine[:, g, :, None], w_down[g])
    return y.reshape(B, L, D)

def trunk_layer(x, c, gla_s0, k_cache, v_cache, slopes, p):
    (ada_w, ada_b, w_in, a2_w, a2_b, gla_norm_w, sinks, w_o, ln1_g, ln1_b,
     rg_w, rg_b, re_w, re_b, w_gate, w_up, w_down, ln2_g, ln2_b) = p
    sh1, sc1, gt1, sh2, sc2, gt2 = adaln(c, ada_w, ada_b)
    h = x * (1 + sc1) + sh1
    gq, gk, gv, gr, loga, sq, sk, sv = in_proj(h, w_in, a2_w, a2_b)
    sinks = sinks.reshape(SWA_KV_HEADS, SWA_GROUP).astype(jnp.float32)
    if k_cache is None:
        s0 = jnp.zeros((x.shape[0], GLA_HEADS, GLA_DK, GLA_DV), jnp.float32)
        o_gla, s_new = gla_chunk_causal(gq, gk, gv, loga, s0, CHUNK)
        o_swa = swa_prompt(sq, sk, sv, slopes, sinks)
        k_new, v_new = sk[:, -WINDOW:], sv[:, -WINDOW:]
    else:
        o_gla, s_new = gla_chunk_causal(gq, gk, gv, loga, gla_s0, x.shape[1])
        o_swa, k_new, v_new = swa_sample(sq, sk, sv, k_cache, v_cache, slopes, sinks)
    mix = mixer_out(o_gla, gr, gla_norm_w, o_swa, w_o, x.dtype)
    x = layer_norm(DEEPNORM_ALPHA * x + gt1 * mix, ln1_g, ln1_b)
    h2 = x * (1 + sc2) + sh2
    x = layer_norm(DEEPNORM_ALPHA * x + gt2 * hier_moe(h2, rg_w, rg_b, re_w, re_b, w_gate, w_up, w_down), ln2_g, ln2_b)
    return x, s_new.astype(x.dtype), k_new, v_new

def setup_inputs(seed: int = 0) -> dict:
    key = jax.random.key(seed)
    ks = iter(jax.random.split(key, 40))
    nrm = lambda shape, scale=1.0: jax.random.normal(next(ks), shape, jnp.float32) * scale
    D = D_MODEL
    Lc = min(WINDOW, PAST_LEN)
    col_scale = np.concatenate([np.full(n, s, np.float32) for n, s in zip(
        IN_SPLITS, (1.0, 1.0, DEEPNORM_BETA, 1.0, 1.0, 1.0, 1.0, DEEPNORM_BETA))])
    return {
        "x_prompt": nrm((BATCH, SEQ, D)),
        "x_sample": nrm((DEC_BATCH, DEC_SEQ, D)),
        "c_prompt": nrm((BATCH, D)),
        "c_sample": nrm((DEC_BATCH, D)),
        "state_gla": nrm((DEPTH, DEC_BATCH, GLA_HEADS, GLA_DK, GLA_DV)),
        "cache_swa_k": nrm((DEPTH, DEC_BATCH, Lc, SWA_KV_HEADS, SWA_HEAD_DIM)),
        "cache_swa_v": nrm((DEPTH, DEC_BATCH, Lc, SWA_KV_HEADS, SWA_HEAD_DIM), DEEPNORM_BETA),
        "ada_w": nrm((DEPTH, D, 6 * D), D ** -0.5),
        "ada_b": nrm((DEPTH, 6 * D), 0.02),
        "w_in": nrm((DEPTH, D, IN_WIDTH), D ** -0.5) * jnp.asarray(col_scale),
        "gla_a2_w": nrm((DEPTH, GLA_GATE_RANK, GLA_HEADS * GLA_DK), GLA_GATE_RANK ** -0.5),
        "gla_a2_b": nrm((DEPTH, GLA_HEADS * GLA_DK), 0.1),
        "gla_norm_w": 1.0 + nrm((DEPTH, GLA_DV), 0.02),
        "swa_sinks": nrm((DEPTH, SWA_Q_HEADS), 0.5),
        "w_o": nrm((DEPTH, MIX_WIDTH, D), MIX_WIDTH ** -0.5 * DEEPNORM_BETA),
        "ln1_g": 1.0 + nrm((DEPTH, D), 0.02),
        "ln1_b": nrm((DEPTH, D), 0.02),
        "router_g_w": nrm((DEPTH, D, N_GROUPS), D ** -0.5),
        "router_g_b": nrm((DEPTH, N_GROUPS), 0.01),
        "router_e_w": nrm((DEPTH, N_GROUPS, D, EXPERTS_PER_GROUP), D ** -0.5),
        "router_e_b": nrm((DEPTH, N_GROUPS, EXPERTS_PER_GROUP), 0.01),
        "moe_w_gate": nrm((DEPTH, N_GROUPS, EXPERTS_PER_GROUP, D, EXPERT_FF), D ** -0.5 * DEEPNORM_BETA),
        "moe_w_up": nrm((DEPTH, N_GROUPS, EXPERTS_PER_GROUP, D, EXPERT_FF), D ** -0.5 * DEEPNORM_BETA),
        "moe_w_down": nrm((DEPTH, N_GROUPS, EXPERTS_PER_GROUP, EXPERT_FF, D), EXPERT_FF ** -0.5 * DEEPNORM_BETA),
        "ln2_g": 1.0 + nrm((DEPTH, D), 0.02),
        "ln2_b": nrm((DEPTH, D), 0.02),
    }

def reference(x_prompt, x_sample, c_prompt, c_sample, state_gla, cache_swa_k, cache_swa_v,
              ada_w, ada_b, w_in, gla_a2_w, gla_a2_b, gla_norm_w, swa_sinks, w_o, ln1_g, ln1_b,
              router_g_w, router_g_b, router_e_w, router_e_b, moe_w_gate, moe_w_up, moe_w_down,
              ln2_g, ln2_b):
    slopes = alibi_slopes()
    xp, xs = x_prompt, x_sample
    gla_p, kp, vp, gla_s, ksn, vsn = [], [], [], [], [], []
    for l in range(DEPTH):
        p = (ada_w[l], ada_b[l], w_in[l], gla_a2_w[l], gla_a2_b[l], gla_norm_w[l], swa_sinks[l], w_o[l],
             ln1_g[l], ln1_b[l], router_g_w[l], router_g_b[l], router_e_w[l], router_e_b[l],
             moe_w_gate[l], moe_w_up[l], moe_w_down[l], ln2_g[l], ln2_b[l])
        xp, s_p, k_p, v_p = trunk_layer(xp, c_prompt, None, None, None, slopes, p)
        xs, s_s, k_s, v_s = trunk_layer(xs, c_sample, state_gla[l], cache_swa_k[l], cache_swa_v[l], slopes, p)
        gla_p.append(s_p); kp.append(k_p); vp.append(v_p)
        gla_s.append(s_s); ksn.append(k_s); vsn.append(v_s)
    return (xp, xs, jnp.stack(gla_p), jnp.stack(kp), jnp.stack(vp),
            jnp.stack(gla_s), jnp.stack(ksn), jnp.stack(vsn))


_drawn_inputs = setup_inputs


def setup_inputs(seed=0):
    import zlib

    import numpy as np

    out = dict(_drawn_inputs(seed))
    spreads = {}
    factors = {'gla_norm_w': 8.0,
     'swa_sinks': 24.221,
     'ln1_g': 2.73,
     'ln1_b': 2.751,
     'router_g_b': 23.557,
     'router_e_b': 26.754,
     'ln2_g': 7.997,
     'ln2_b': 8.012}
    for name, (base, spread) in spreads.items():
        noise = np.random.default_rng([zlib.crc32(name.encode()), seed]).standard_normal(out[name].shape)
        drawn = base * np.exp(spread * noise) if base else spread * noise
        out[name] = __import__('jax').numpy.asarray(drawn.astype(out[name].dtype))
    for name, factor in factors.items():
        out[name] = (out[name] * factor).astype(out[name].dtype)
    return out
```

```python
import concourse.bass as bass
from concourse import mybir
from contextlib import ExitStack


def hymba_stream_step(nc, x_prompt, x_sample, c_prompt, c_sample, state_gla, cache_swa_k, cache_swa_v,
                      ada_w, ada_b, w_in, gla_a2_w, gla_a2_b, gla_norm_w, swa_sinks, w_o, ln1_g, ln1_b,
                      router_g_w, router_g_b, router_e_w, router_e_b, moe_w_gate, moe_w_up, moe_w_down,
                      ln2_g, ln2_b,
                      y_prompt, y_sample, state_prompt, k_prompt, v_prompt, state_sample, k_sample, v_sample):
    f32, i32 = mybir.dt.float32, mybir.dt.int32
    ALU = mybir.AluOpType
    ACT = mybir.ActivationFunctionType
    AX = mybir.AxisListType

    P = 128
    D = x_prompt.shape[2]
    KD = D // P
    LP, LS = x_prompt.shape[1], x_sample.shape[1]
    T = LP + LS
    NP = LP // P
    NT = NP + 1
    ROWS = [P] * NP + [LS]
    CH = 64
    NCH = LP // CH
    H, DK, DV = state_gla.shape[2:]
    HD = cache_swa_k.shape[4]
    NQ = swa_sinks.shape[1]
    WIN = cache_swa_k.shape[2]
    KW = WIN + P
    NG, NE = router_g_w.shape[2], router_e_w.shape[3]
    E = NG * NE
    FF = moe_w_gate.shape[4]
    NF = FF // P
    ALPHA = 2.0 ** 0.25
    EPS = 1e-5
    O_GQ, O_GK, O_GV, O_GR, O_GA = 0, H * DK, 2 * H * DK, 2 * H * DK + H * DV, 2 * H * DK + 2 * H * DV
    RANK = gla_a2_w.shape[1]
    O_SQ = O_GA + RANK
    O_SK = O_SQ + NQ * HD
    O_SV = O_SK + 2 * HD
    UC = 256

    PAIRS = 2 * T
    NOV = PAIRS // (P + 1)
    OVT = (T - 1) // P
    NBLK = E + NOV
    KSTEP = 1024
    EMPTY = 4096

    mod_d = nc.dram_tensor("mod_scratch", [2, 6 * D], f32).ap()
    h2_d = nc.dram_tensor("h2_scratch", [T, D], f32).ap()
    tbl_d = nc.dram_tensor("slot_table", [NBLK * P, 1], f32).ap()
    yb_d = nc.dram_tensor("expert_rows", [2 * KSTEP, D], f32).ap()

    def cols(w, c, n):
        return w[:, c:c + n].rearrange("(k p) n -> p k n", p=P)

    NR = 6
    units = []
    NA1 = 2 * D // UC
    NA = 6 * D // UC
    for u in range(NA1):
        units.append(("ada", u))
    WIN_UNITS = ["gq", "gk", "sq0", "sq1", "kv", "gv0", "gv1", "gr0", "gr1"]
    for w in WIN_UNITS:
        units.append((w, 0))
    for u in range(NA1, NA):
        units.append(("ada", u))
    for u in range(KD // 2):
        units.append(("wo", u))
    N0 = len(units)
    number = {u: n for n, u in enumerate(units)}

    ctx = ExitStack()
    with ctx:
        def sb(name, shape, dt=f32):
            return ctx.enter_context(nc.sbuf_tensor(name, shape, dt))

        def sem(name):
            return ctx.enter_context(nc.semaphore(name))

        bank = [ctx.enter_context(nc.psum_tensor(f"bank{i}", [P, 512], f32)) for i in range(8)]

        ring = sb("ring", [P, NR, KD * UC])
        x_tok = sb("x_tok", [P, NT, D])
        areaA = sb("areaA", [P, KD, T])
        hT, mixT = areaA, areaA
        areaB = sb("areaB", [P, 8 * T * 2])
        GW = 2 * T

        def area_b(i, n=1):
            return areaB[:, i * GW:(i + n) * GW]
        gq, gk, bc, eb, ebn, ed = (area_b(i).rearrange("p (a t) -> p a t", a=2) for i in range(6))
        sqT = area_b(6, 2).rearrange("p (a t) -> p a t", a=4)
        modP = areaB[:, 0:4 * D].rearrange("p (a n) -> p a n", a=4)
        modS = areaB[0:LS, 4 * D:8 * D].rearrange("p (a n) -> p a n", a=4)
        areaC = sb("areaC", [P, 9 * D + 256])
        gv = areaC[:, 0:NT * H * DV].rearrange("p (j n) -> p j n", j=NT)
        grg = areaC[:, NT * 512:2 * NT * 512].rearrange("p (j n) -> p j n", j=NT)
        Ssc = areaC[:, 5 * D:7 * D].rearrange("p (h n) -> p h n", h=NQ)
        PT = areaC[:, 7 * D:9 * D].rearrange("p (h b q) -> p h b q", h=NQ, b=2)
        z = areaC[:, 5 * D:5 * D + NT * 256].rearrange("p (j n) -> p j n", j=NT)
        zt = areaC[:, 7 * D:7 * D + NT * 256].rearrange("p (j n) -> p j n", j=NT)
        xg = areaC[:, 0:2 * D].rearrange("p (a n) -> p a n", a=2)
        xTe = areaC[:, 2 * D:4 * D].rearrange("p (a k t) -> p a k t", a=2, k=KD)
        ye = areaC[:, 4 * D:6 * D].rearrange("p (a n) -> p a n", a=2)
        hid = areaC[:, 6 * D:6 * D + 2 * FF].rearrange("p (a n) -> p a n", a=2)
        sgl = areaC[:, 6 * D + 2 * FF:7 * D].rearrange("p (a n) -> p a n", a=2)
        hidT = areaC[:, 7 * D:7 * D + 2 * FF].rearrange("p (a k t) -> p a k t", a=2, k=NF)
        h2Tt = areaC[:, 0:D].rearrange("p (k t) -> p k t", k=KD)
        ln1 = areaC[:, 1 * D:3 * D].rearrange("p (a n) -> p a n", a=2)
        h2 = areaC[:, 3 * D:5 * D].rearrange("p (a n) -> p a n", a=2)
        ytmp = areaC[:, 5 * D:6 * D]
        biasH = sb("biasH", [P, NQ, KW])
        ln2 = biasH[:, :, :].rearrange("p h n -> p (h n)").rearrange("p (a n) -> p a n", a=2)
        skT = sb("skT", [P, LP + WIN + LS])
        gaT = sb("gaT", [RANK, T])
        svt = sb("svt", [P, NT + 1, 2 * HD])
        skt = sb("skt", [P, 2, 2 * HD])
        S = sb("S", [P, NCH + 3, 2, DV])
        gend = sb("gend", [P, 2, NCH + 1])
        osb = areaC[:, 5 * D:6 * D].rearrange("p (a n) -> p a n", a=2)
        gex = areaC[:, 6 * D:7 * D].rearrange("p (a n) -> p a n", a=2)
        kdT = areaC[:, 7 * D:7 * D + 4 * P].rearrange("p (a n) -> p a n", a=2)
        og = areaC[:, 7 * D + 4 * P:7 * D + 8 * P]
        At = areaC[:, 8 * D + 256:9 * D + 256].rearrange("p (a h t) -> p a h t", a=2, h=H)
        modrt = sb("modrt", [P, 2 * D])
        modst = modrt[0:2, :]
        adab = sb("adab", [NA, UC])
        crow = sb("crow", [2 * KD, P])
        cT = sb("cT", [P, 2 * KD])
        cx = sb("cx", [P, 2 * KD])
        csT = sb("csT", [P, 2 * KD])
        shsc = sb("shsc", [P, 4 * KD])
        wga = sb("wga", [P, KD, RANK])
        a2w = sb("a2w", [RANK, H * DK])
        a2b = sb("a2b", [P, H * DK])
        nw = sb("nw", [P, DV])
        sinks = sb("sinks", [P, NQ])
        rw = sb("rw", [P, KD, NG + E])
        rb = sb("rb", [P, NG + E])
        kc = sb("kc", [P, 2 * HD])
        ident = sb("ident", [P, P])
        tri = sb("tri", [P, P])
        tup = sb("tup", [P, P])
        before = sb("before", [P, P])
        ones = sb("ones", [P, P])
        dist = sb("dist", [P, KW])
        epst = sb("epst", [P, 1])
        iow = sb("iow", [P, 40])
        fl = sb("fl", [P, NBLK])
        small = sb("small", [P, 64])
        stat = sb("stat", [P, 2, 16])
        lg = sb("lg", [P, NT, NG + E])
        rt = modrt[:, 0:10 * NT * E].rearrange("p (i n) -> p i n", i=10)
        rs = sb("rs", [P, 12, NT])
        ov = sb("ov", [P, 6, E])
        wts = sb("wts", [P, 2, NT])
        posi = sb("posi", [P, 2, NT], i32)
        tokv = sb("tokv", [P, 2, NT])
        trow = sb("trow", [NBLK, P])
        srci = sb("srci", [P, NBLK], i32)
        dsti = sb("dsti", [P, NBLK], i32)
        ovi = sb("ovi", [1, 2 + NOV], i32)

        s_c, s_x, s_adab, s_misc, s_misc2 = sem("c_loaded"), sem("x_loaded"), sem("adab_loaded"), sem("misc_loaded"), sem("router_loaded")
        full = [sem(f"ring_full{i}") for i in range(NR)]
        pe_mod = sem("mod_units_done")
        wo_used, pe_g = sem("wo_units_used"), sem("gate_done")
        dv = sem("dve_chain")
        ac = sem("act_chain")
        pl = sem("pool_chain")
        pe_c, c_ex, cs_ready = sem("c_transposed"), sem("c_exp"), sem("cs_ready")
        pe_xt, xt_ev = sem("x_transposed"), sem("xT_evacuated")
        ada_ev, pe_sc, h_ready = sem("mod_evacuated"), sem("mod_transposed"), sem("h_ready")
        pe_t, t_ev = sem("proj_T_done"), sem("proj_T_evacuated")
        pe_z, z_ev, z_abs, z_ln, l_ready = sem("gate_psum"), sem("gate_evacuated"), sem("z_abs"), sem("z_ln"), sem("loga_ready")
        b_ready, e_ready, gla_ready = sem("b_ready"), sem("exps_ready"), sem("gla_operands_ready")
        pe_tok, tok_ev = sem("proj_tok_done"), sem("proj_tok_evacuated")
        pe_kd, kd_ev, pe_u, u_ev = sem("kd_transposed"), sem("kd_evacuated"), sem("u_done"), sem("state_updated")
        pe_a, a_ev, pe_o, o_ev, o_sq, og_ready, pe_og, mg_ev = (sem(n) for n in (
            "A_done", "A_masked", "o_done", "o_evacuated", "o_stats", "og_ready", "og_transposed", "mixT_gla"))
        pe_qk, s_ev, m_ready, p_exp, p_ready, pe_pt, pt_ev, pe_pv, pv_ev = (sem(n) for n in (
            "qk_done", "scores_ready", "max_ready", "probs_exp", "probs_ready", "P_transposed", "PT_evacuated",
            "pv_done", "mixT_swa"))
        s_mod, s_modb, s_ln1, s_ln2, s_kc = sem("mod_stored"), sem("mod_rows"), sem("ln1_rows"), sem("ln2_rows"), sem("cache_loaded")
        pe_y, y_ev, v_ready, v_ln, h2_ready, h2_st = (sem(n) for n in (
            "out_proj_done", "out_proj_read", "var_ready", "rstd_ready", "h2_ready", "h2_stored"))
        h2_st = [h2_st, sem("h2_stored1")]
        pe_ht, ht_ev, pe_rt, rt_ev = sem("h2_transposed"), sem("h2T_evacuated"), sem("logits_done"), sem("logits_read")
        r_ex0, r_ex, oh_ready, pe_rank, pos_ready = (sem(n) for n in (
            "router_diffs", "router_exps", "onehots_ready", "ranks_done", "slots_ready"))
        s_tbl0, s_scat, s_trow, pe_tbl, tbl_ready, ov_ready = (sem(n) for n in (
            "table_empty", "table_filled", "table_loaded", "table_transposed", "table_ready", "overflow_ready"))
        s_g = [sem("rows_gathered0"), sem("rows_gathered1")]
        s_sc = [sem("rows_scattered0"), sem("rows_scattered1")]
        pe_xe, xe_a, xe_d, pe_gu, sg_done, hid_done, pe_hT, hT_ev, pe_dn, y_a, y_d = (sem(n) for n in (
            "xe_transposed", "xe_evac_act", "xe_evac_dve", "gate_up_done", "silu_done", "hid_done",
            "hid_transposed", "hidT_evacuated", "down_done", "ye_act", "ye_dve"))
        o_w = sem("overflow_weights")
        s_fin = [sem(f"final_rows{j}") for j in range(NT)]
        f_a, f_v, f_l, f_o = sem("final_scaled"), sem("final_var"), sem("final_rstd"), sem("final_out")
        s_out, s_kv = sem("outputs_stored"), sem("caches_stored")
        moe_over = sem("moe_over")

        block = ctx.enter_context(nc.Block())

        def tok(j):
            return slice(P * j, P * j + ROWS[j])

        def slot(n):
            return ring[:, n % NR, :]

        def unit_src(kind, u):
            if kind == "ada":
                return [(slice(0, KD * UC), cols(ada_w[0], u * UC, UC))]
            if kind == "wo":
                half = D * 2
                if u < KD // 4:
                    return [(None, w_o[0, 2 * P * u:2 * P * (u + 1), :].rearrange("(k p) n -> p k n", p=P))]
                i0 = 2 * (u - KD // 4)
                return [(g, w_o[0, H * DV + g * 4 * HD + i0 * HD:H * DV + g * 4 * HD + (i0 + 2) * HD, :]
                         .rearrange("(k p) n -> p k n", p=HD)) for g in range(2)]
            if kind in ("sq0", "sq1"):
                a = O_SQ + (0 if kind == "sq0" else 2 * HD)
                return [(2 * i + g, cols(w_in[0], a + g * 4 * HD + i * HD, HD)) for i in range(2) for g in range(2)]
            c = {"gq": O_GQ, "gk": O_GK, "kv": O_SK, "gv0": O_GV, "gv1": O_GV + UC, "gr0": O_GR, "gr1": O_GR + UC}[kind]
            return [(None, cols(w_in[0], c, UC))]

        NDMA = [len(unit_src(*u)) for u in units]

        def full_count(n):
            return sum(16 * NDMA[m] for m in range(n % NR, n + 1, NR))

        FULL0 = [0] * NR
        for n in range(N0):
            FULL0[n % NR] += 16 * NDMA[n]

        def expert_count(n):
            first = N0 + (n - N0) % NR
            return FULL0[n % NR] + 16 * ((n - first) // NR + 1)

        W3 = [moe_w_gate, moe_w_up, moe_w_down]

        def expert_src(e, r):
            w = W3[r][0].rearrange("g e a b -> (g e) a b")
            w = w[e] if isinstance(e, int) else w[bass.ds(e, 1)].rearrange("o a b -> (o a) b")
            return w.rearrange("(k p) n -> p k n", p=P)

        def slot_view(n, kd):
            return slot(n).rearrange("p (k n) -> p k n", k=kd)

        LAST = {"gq": (pe_t, 3), "gk": (pe_t, 5), "sq0": (pe_t, 7), "sq1": (pe_t, 9), "kv": (pe_tok, NT),
                "gv0": (pe_tok, 2 * NT), "gv1": (pe_tok, 3 * NT), "gr0": (pe_tok, 4 * NT), "gr1": (pe_tok, 5 * NT)}

        def freed(n):
            kind, u = units[n]
            if kind == "ada":
                return pe_mod, u + 1
            if kind == "wo":
                return (wo_used, u + 1) if u < KD // 2 - 1 else (pe_y, NT)
            return LAST[kind]

        def at(base, step, i):
            return base if i is None else i * step + base

        @block.sync
        def _(sp):
            sp.dma_start(crow[0:KD, :], c_prompt[0, :].rearrange("(k p) -> k p", p=P)).then_inc(s_c, 16)
            sp.dma_start(crow[KD:2 * KD, :], c_sample[0, :].rearrange("(k p) -> k p", p=P)).then_inc(s_c, 16)
            sp.dma_start(adab[:, :], ada_b[0, :].rearrange("(u n) -> u n", n=UC)).then_inc(s_adab, 16)
            sp.dma_start(x_tok[:, 0:NP, :], x_prompt[0].rearrange("(j p) n -> p j n", p=P)).then_inc(s_x, 16)
            sp.dma_start(x_tok[0:LS, NP, :], x_sample[0]).then_inc(s_x, 16)
            for n, (kind, u) in enumerate(units):
                if n >= NR:
                    sp.wait_ge(*freed(n - NR))
                for g, src in unit_src(kind, u):
                    if kind == "wo":
                        v = slot_view(n, 2)
                        dst = v if g is None else v[g * HD:(g + 1) * HD, :, :]
                    elif kind in ("sq0", "sq1"):
                        dst = slot_view(n, KD)[:, :, g * HD:(g + 1) * HD]
                    else:
                        dst = slot_view(n, KD)
                    sp.dma_start(dst, src).then_inc(full[n % NR], 16)

            for e in range(2):
                for r in range(3):
                    n = N0 + 3 * e + r
                    sp.wait_ge(*freed(n - NR))
                    sp.dma_start(slot_view(n, KD if r < 2 else NF), expert_src(e, r)).then_inc(full[n % NR], 16)
            with sp.Fori(1, E // 2) as i:
                for b in range(2):
                    for r, done in enumerate((pe_g, pe_gu, pe_dn)):
                        n = N0 + 3 * b + r
                        sp.wait_ge(done, i * 2 + b - 1)
                        sp.dma_start(slot_view(n, KD if r < 2 else NF), expert_src(i * 2 + b, r)).then_inc(full[n % NR], 16)

            sp.wait_ge(moe_over, 1)
            sp.wait_ge(ov_ready, 1)
            nov = sp.value_load(ovi[0:1, 0:1], min_val=0, max_val=NOV)
            with sp.If(nov > 0):
                with sp.Fori(0, nov) as i:
                    e = sp.value_load(ovi[0:1, bass.ds(i + 1, 1)], min_val=0, max_val=E - 1)
                    sp.wait_ge(y_d, i + E)
                    for r in range(3):
                        sp.dma_start(ring[:, r, :].rearrange("p (k n) -> p k n", k=KD if r < 2 else NF),
                                     expert_src(e, r)).then_inc(o_w, 16)

            sp.wait_ge(moe_over, 2)
            rows3 = yb_d.rearrange("(k t) n -> t k n", k=2)
            for j in range(NT):
                sp.dma_start(ring[0:ROWS[j], j, :].rearrange("p (k n) -> p k n", k=2),
                             rows3[P * j:P * j + ROWS[j], :, :]).then_inc(s_fin[j], 16)
            for j in range(NT):
                sp.wait_ge(f_o, j + 1)
                dst = y_prompt[0, P * j:P * (j + 1), :] if j < NP else y_sample[0]
                sp.dma_start(dst, x_tok[0:ROWS[j], j, :]).then_inc(s_out, 16)
            sp.wait_ge(s_out, 16 * NT)

        NCONST = 21

        @block.gpsimd
        def _(pool):
            chain = [0]

            def link(ins):
                chain[0] += 1
                ins.then_inc(pl, 1)
                pool.wait_ge(pl, chain[0])

            link(pool.memset(epst[:, :], EPS))
            link(pool.memset(ident[:, :], 0.0))
            link(pool.affine_select(out=ident[:, :], in_=ident[:, :], compare_op=ALU.not_equal, fill=1.0, base=0,
                               pattern=[[-1, P]], channel_multiplier=1))
            link(pool.memset(ones[:, :], 1.0))
            link(pool.memset(tri[:, :], 1.0 / 16.0))
            link(pool.affine_select(out=tri[:, :], in_=tri[:, :], compare_op=ALU.is_ge, fill=0.0, base=0,
                                    pattern=[[1, P]], channel_multiplier=-1))
            link(pool.memset(tri[0:CH, CH:P], 0.0))
            link(pool.memset(tup[:, :], 1.0))
            link(pool.affine_select(out=tup[:, :], in_=tup[:, :], compare_op=ALU.is_ge, fill=0.0, base=-1,
                                    pattern=[[-1, P]], channel_multiplier=1))
            link(pool.memset(tup[CH:P, 0:CH], 0.0))
            link(pool.memset(before[:, :], 1.0))
            link(pool.affine_select(out=before[:, :], in_=before[:, :], compare_op=ALU.is_ge, fill=0.0, base=-1,
                               pattern=[[1, P]], channel_multiplier=-1))
            link(pool.iota(dist[:, :], pattern=[[1, KW]], base=-WIN, channel_multiplier=-1,
                      allow_small_or_imprecise_dtypes=True))
            link(pool.memset(z[:, NP, :], 0.0))
            link(pool.memset(At[:, :, :, :], 0.0))
            link(pool.memset(S[:, 0, :, :], 0.0))
            link(pool.memset(lg[:, :, :], 0.0))
            link(pool.iota(ov[:, 0, :], pattern=[[P, E]], base=0, channel_multiplier=0,
                      allow_small_or_imprecise_dtypes=True))
            link(pool.iota(iow[:, 0:E], pattern=[[-1, E]], base=E, channel_multiplier=0,
                      allow_small_or_imprecise_dtypes=True))
            for k in range(2):
                link(pool.iota(tokv[:, k, :], pattern=[[P, NT]], base=k * KSTEP, channel_multiplier=1,
                          allow_small_or_imprecise_dtypes=True))
            link(pool.memset(fl[:, :], float(EMPTY)))
            pool.dma_start(tbl_d.rearrange("(p b) o -> p (b o)", p=P), fl[:, :]).then_inc(s_tbl0, 16)

            pool.wait_ge(tok_ev, NT)
            pool.dma_start(k_prompt[0, 0].rearrange("t h d -> t (h d)"), skt[:, 0, :]).then_inc(s_kv, 16)
            pool.dma_start(v_prompt[0, 0].rearrange("t h d -> t (h d)"), svt[:, NP - 1, :]).then_inc(s_kv, 16)
            for dst, old, new in ((k_sample, kc[LS:P, :], skt[0:LS, 1, :]), (v_sample, svt[LS:P, NP, :], svt[0:LS, NP + 1, :])):
                d = dst[0, 0].rearrange("t h d -> t (h d)")
                pool.dma_start(d[0:WIN - LS, :], old).then_inc(s_kv, 16)
                pool.dma_start(d[WIN - LS:WIN, :], new).then_inc(s_kv, 16)
            pool.wait_ge(u_ev, NT)
            for dst, n in ((state_prompt, NCH), (state_sample, NCH + 2)):
                pool.dma_start(dst[0, 0].rearrange("(a h) k v -> (h k) a v", a=2), S[:, n, :, :]).then_inc(s_kv, 16)
            pool.wait_ge(s_kv, 16 * 8)
            for h in range(2):
                pool.wait_ge(ada_ev, NA1 * (h + 2))
                pool.dma_start(mod_d[:, 2 * D * (h + 1):2 * D * (h + 2)], modst[:, :]).then_inc(s_mod, 16)
            pool.wait_ge(s_mod, 32)
            pool.wait_ge(pe_qk, 4 * NT)
            pool.wait_ge(pe_o, NT)
            pool.dma_start(modP[:, :, :].rearrange("p a n -> p (a n)"), mod_d[0:1, 2 * D:6 * D].to_broadcast([P, 4 * D])).then_inc(s_modb, 16)
            pool.dma_start(modS[:, :, :].rearrange("p a n -> p (a n)"), mod_d[1:2, 2 * D:6 * D].to_broadcast([LS, 4 * D])).then_inc(s_modb, 16)
            pool.wait_ge(og_ready, NT)
            pool.dma_start(ln1[:, 0, :], ln1_g.to_broadcast([P, D])).then_inc(s_ln1, 16)
            pool.dma_start(ln1[:, 1, :], ln1_b.to_broadcast([P, D])).then_inc(s_ln1, 16)
            pool.wait_ge(s_ev, 4 * NT)
            pool.dma_start(ln2[:, 0, :], ln2_g.to_broadcast([P, D])).then_inc(s_ln2, 16)
            pool.dma_start(ln2[:, 1, :], ln2_b.to_broadcast([P, D])).then_inc(s_ln2, 16)

            pool.wait_ge(pos_ready, 1)
            pool.wait_ge(s_tbl0, 16)
            for k in range(2):
                for j in range(NT):
                    pool.indirect_dma_start(
                        out=tbl_d[:, :], out_offset=bass.IndirectOffsetOnAxis(ap=posi[0:ROWS[j], k, j:j + 1], axis=0),
                        in_=tokv[0:ROWS[j], k, j:j + 1], in_offset=None,
                        bounds_check=NBLK * P - 1, oob_is_err=False).then_inc(s_scat, 16)
            pool.wait_ge(s_scat, 16 * 2 * NT)
            pool.dma_start(trow[:, :], tbl_d.rearrange("(b p) o -> b (p o)", p=P)).then_inc(s_trow, 16)
            pool.wait_ge(mg_ev, NT)
            pool.wait_ge(pe_rt, NT)
            pool.wait_ge(h2_st[0], 16 * ((NT + 1) // 2))
            pool.wait_ge(h2_st[1], 16 * (NT // 2))
            link(pool.memset(xg[:, :, :], 0.0))
            pool.wait_ge(tbl_ready, 1)

            def gather(b, a):
                pool.indirect_dma_start(
                    out=xg[:, a, :], out_offset=None, in_=h2_d[:, :],
                    in_offset=bass.IndirectOffsetOnAxis(ap=srci[:, b:b + 1], axis=0),
                    bounds_check=T - 1, oob_is_err=False).then_inc(s_g[a], 16)

            def scatter(b, a):
                pool.wait_ge(y_a, b + 1)
                pool.wait_ge(y_d, b + 1)
                pool.indirect_dma_start(
                    out=yb_d[:, :], out_offset=bass.IndirectOffsetOnAxis(ap=dsti[:, b:b + 1], axis=0),
                    in_=ye[:, a, :], in_offset=None,
                    bounds_check=2 * KSTEP - 1, oob_is_err=False).then_inc(s_sc[a], 16)

            gather(0, 0)
            gather(1, 1)
            for e in range(E):
                if e + 2 < E:
                    pool.wait_ge(pe_xe, e + 1)
                    gather(e + 2, e % 2)
                scatter(e, e % 2)
            pool.wait_ge(s_sc[0], 16 * (E // 2))
            pool.wait_ge(s_sc[1], 16 * (E // 2))
            pool.wait_ge(pe_dn, E)
            pool.engine_nop().then_inc(moe_over, 1)
            pool.wait_ge(ov_ready, 1)
            nov = pool.value_load(ovi[0:1, 0:1], min_val=0, max_val=NOV)
            for b in range(NOV):
                with pool.If(nov > b):
                    gather(E + b, 0)
                    scatter(E + b, 0)
                    pool.wait_ge(s_sc[0], 16 * (E // 2 + b + 1))
            pool.engine_nop().then_inc(moe_over, 1)

        @block.scalar
        def _(act):
            chain = [0]

            def link(ins):
                chain[0] += 1
                ins.then_inc(ac, 1)
                act.wait_ge(ac, chain[0])

            act.dma_start(wga[:, :, :], cols(w_in[0], O_GA, RANK)).then_inc(s_misc, 16)
            act.dma_start(a2w[:, :], gla_a2_w[0]).then_inc(s_misc, 16)
            act.dma_start(a2b[:, :], gla_a2_b.to_broadcast([P, H * DK])).then_inc(s_misc, 16)
            act.dma_start(nw[:, :], gla_norm_w.to_broadcast([P, DV])).then_inc(s_misc, 16)
            act.dma_start(sinks[:, :], swa_sinks.to_broadcast([P, NQ])).then_inc(s_misc, 16)
            act.dma_start(kc[:, :], cache_swa_k[0, 0].rearrange("t h d -> t (h d)")).then_inc(s_kc, 16)
            act.dma_start(svt[:, NP, :], cache_swa_v[0, 0].rearrange("t h d -> t (h d)")).then_inc(s_misc, 16)
            act.dma_start(S[:, NCH + 1, :, :], state_gla[0, 0].rearrange("(a h) k v -> (h k) a v", a=2)).then_inc(s_misc, 16)
            act.dma_start(rw[:, :, 0:NG], cols(router_g_w[0], 0, NG)).then_inc(s_misc2, 16)
            for g in range(NG):
                act.dma_start(rw[:, :, NG + g * NE:NG + (g + 1) * NE], cols(router_e_w[0, g], 0, NE)).then_inc(s_misc2, 16)
            act.dma_start(rb[:, 0:NG], router_g_b.to_broadcast([P, NG])).then_inc(s_misc2, 16)
            act.dma_start(rb[:, NG:NG + E], router_e_b.rearrange("o g e -> o (g e)").to_broadcast([P, E])).then_inc(s_misc2, 16)

            act.wait_ge(pl, NCONST)
            act.wait_ge(pe_c, 1)
            act.activation(cx[:, :], bank[0][:, 0:2 * KD], ACT.Exp, scale=-1.0).then_inc(c_ex, 1)
            for q in range(2 * NT):
                j, half = q // 2, q % 2
                act.wait_ge(pe_xt, q + 1)
                r = ROWS[j]
                act.activation(hT[:, 4 * half:4 * half + 4, tok(j)],
                               bank[1 + q % 2][:, 0:4 * r].rearrange("p (k t) -> p k t", k=4), ACT.Copy).then_inc(xt_ev, 1)
            dests = [gaT] + [gq[:, 0], gq[:, 1], gk[:, 0], gk[:, 1]] + [sqT[:, i] for i in range(4)] + [skT]

            def evac_t(tb):
                act.wait_ge(pe_t, tb + 1)
                d = dests[tb]
                m = RANK if tb == 0 else P
                s = DK ** -0.5 if tb in (1, 2) else 1.0
                off = LP + WIN if tb == 9 else LP
                act.activation(d[0:m, 0:LP], bank[1 + tb % 2][0:m, 0:LP], ACT.Copy, scale=s).then_inc(t_ev, 1)
                act.activation(d[0:m, off:off + LS], bank[5 + tb % 2][0:m, 0:LS], ACT.Copy, scale=s).then_inc(t_ev, 1)

            for tb in range(4):
                evac_t(tb)
            act.wait_ge(z_abs, 1)
            link(act.activation(zt, zt, ACT.Exp, scale=-1.0))
            act.activation(zt, zt, ACT.Ln, bias=1.0).then_inc(z_ln, 1)
            for tb in range(4, 7):
                evac_t(tb)
            act.wait_ge(b_ready, 2)
            act.activation(eb, bc, ACT.Exp).then_inc(e_ready, 1)
            act.activation(ebn, bc, ACT.Exp, scale=-1.0).then_inc(e_ready, 1)
            act.activation(ed, ed, ACT.Exp).then_inc(e_ready, 1)
            for tb in range(7, 10):
                evac_t(tb)
            act.wait_ge(pe_t, 11)
            act.activation(skT[:, LP:LP + WIN], bank[1][:, 0:WIN], ACT.Copy).then_inc(t_ev, 1)

            for j in range(NT):
                act.wait_ge(pe_kd, j + 1)
                if j >= 2:
                    act.wait_ge(pe_u, j - 1)
                act.activation(kdT[0:ROWS[j], j % 2, :], bank[0][0:ROWS[j], 0:2 * P], ACT.Copy).then_inc(kd_ev, 1)

            def mix_stats(j):
                r = ROWS[j]
                act.wait_ge(pe_o, j + 1)
                if j >= 2:
                    act.wait_ge(og_ready, j - 1)
                o4 = osb[0:r, j % 2, :].rearrange("p (a b v) -> p a b v", a=2, b=2)
                for par in range(2):
                    act.activation(o4[:, :, par, :], bank[3 + par][0:r, 0:2 * DV].rearrange("p (a v) -> p a v", a=2),
                                   ACT.Copy).then_inc(o_ev, 1)
                act.wait_ge(o_ev, 2 * (j + 1))
                for h in range(H):
                    link(act.activation(gex[0:r, j % 2, h * DV:(h + 1) * DV], osb[0:r, j % 2, h * DV:(h + 1) * DV], ACT.Square,
                                        accum_out=small[0:r, 8 * (j % 2) + h:8 * (j % 2) + h + 1]))
                ss = small[0:r, 8 * (j % 2):8 * (j % 2) + H]
                link(act.activation(ss, ss, ACT.Ln, scale=1.0 / DV, bias=epst[0:r, 0:1]))
                link(act.activation(ss, ss, ACT.Exp, scale=-0.5))
                act.wait_ge(tok_ev, 25)
                act.activation(gex[0:r, j % 2, :], grg[0:r, j, :], ACT.Exp, scale=-1.0).then_inc(o_sq, 1)

            def evac_og(j):
                act.wait_ge(pe_og, j + 1)
                act.activation(mixT[:, 0:4, tok(j)], bank[5][:, 0:4 * ROWS[j]].rearrange("p (k t) -> p k t", k=4),
                               ACT.Copy).then_inc(mg_ev, 1)

            for j in range(NT + 2):
                if 1 <= j <= NT:
                    mix_stats(j - 1)
                if j >= 2:
                    evac_og(j - 2)

            def win(j):
                return (P, KW) if j == 0 else (0, KW) if j < NP else (0, WIN + LS)

            def probs(j):
                r = ROWS[j]
                lo, hi = win(j)
                act.wait_ge(m_ready, j + 1)
                for h in range(NQ):
                    link(act.activation(Ssc[0:r, h, 0:hi - lo], Ssc[0:r, h, 0:hi - lo], ACT.Exp,
                                        bias=small[0:r, 24 + h:25 + h], accum_out=small[0:r, 32 + h:33 + h]))
                act.activation(small[0:r, 40:40 + NQ], small[0:r, 40:40 + NQ], ACT.Exp).then_inc(p_exp, 1)

            def evac_pt(j):
                r = ROWS[j]
                nb = 1 if j == 0 else 2
                for f in range(4):
                    act.wait_ge(pe_pt, 4 * j + f + 1)
                    if f == 0:
                        act.wait_ge(pe_pv, j)
                    src = bank[5 + f % 2][:, 0:2 * nb * r].rearrange("p (h b q) -> p h b q", h=2, b=nb)
                    if j < NP:
                        act.activation(PT[:, 2 * f:2 * f + 2, 0:nb, 0:r], src, ACT.Copy).then_inc(pt_ev, 1)
                    else:
                        link(act.activation(PT[:, 2 * f:2 * f + 2, 0, 0:r], src[:, :, 0, :], ACT.Copy))
                        act.activation(PT[0:LS, 2 * f:2 * f + 2, 1, 0:r], src[0:LS, :, 1, :], ACT.Copy).then_inc(pt_ev, 1)

            def evac_pv(j):
                act.wait_ge(pe_pv, j + 1)
                act.activation(mixT[:, 4:8, tok(j)], bank[7][:, 0:4 * ROWS[j]].rearrange("p (k t) -> p k t", k=4),
                               ACT.Copy).then_inc(pv_ev, 1)

            for j in range(NT):
                probs(j)
                evac_pt(j)
                evac_pv(j)

            def rstd(j):
                act.wait_ge(v_ready, j + 1)
                v = stat[0:ROWS[j], j % 2, 13:14]
                link(act.activation(v, v, ACT.Ln, bias=epst[0:ROWS[j], 0:1]))
                act.activation(v, v, ACT.Exp, scale=-0.5).then_inc(v_ln, 1)

            def evac_h2(j):
                r = ROWS[j]
                act.wait_ge(h2_ready, j + 1)
                act.dma_start(h2_d[P * j:P * j + r, :], h2[0:r, j % 2, :]).then_inc(h2_st[j % 2], 16)
                for half in range(2):
                    act.wait_ge(pe_ht, 2 * j + half + 1)
                    if half == 0:
                        act.wait_ge(pe_rt, j)
                    act.activation(h2Tt[:, 4 * half:4 * half + 4, 0:r],
                                   bank[5 + half][:, 0:4 * r].rearrange("p (k t) -> p k t", k=4), ACT.Copy).then_inc(ht_ev, 1)

            for j in range(NT + 1):
                if j < NT:
                    rstd(j)
                if j >= 1:
                    evac_h2(j - 1)
            act.wait_ge(r_ex0, 1)
            link(act.activation(rt[:, 0, 0:NT * NG], rt[:, 0, 0:NT * NG], ACT.Exp))
            act.activation(rs[:, 5, :], rs[:, 5, :], ACT.Exp).then_inc(r_ex, 1)

            def evac_xe(a, w):
                act.wait_ge(pe_xe, w)
                act.activation(xTe[:, a, 0:4, :], bank[0][:, :].rearrange("p (k t) -> p k t", k=4), ACT.Copy).then_inc(xe_a, 1)

            def silu(a, w):
                act.wait_ge(pe_gu, w)
                act.activation(sgl[:, a, :], bank[2 + a][:, 0:FF], ACT.Silu).then_inc(sg_done, 1)

            def evac_hT(a, w):
                act.wait_ge(pe_hT, w)
                act.activation(hidT[:, a, :, :], bank[4][:, 0:FF].rearrange("p (k t) -> p k t", k=NF), ACT.Copy).then_inc(hT_ev, 1)

            def evac_y(a, w, free):
                act.wait_ge(pe_dn, w)
                if free is not None:
                    act.wait_ge(s_sc[a], free)
                act.activation(ye[:, a, 0:512], bank[5][:, :], ACT.Copy).then_inc(y_a, 1)

            def step(e, i, last=False):
                a, b = e % 2, (e - 1) % 2
                silu(a, at(e + 1, 2, i))
                evac_hT(b, at(e, 2, i))
                if not last:
                    evac_xe(b, at(e + 2, 2, i))
                evac_y(b, at(e, 2, i), at(16 * ((e - 1) // 2), 16, i) if e >= 3 or i is not None else None)

            act.wait_ge(tbl_ready, 1)
            evac_xe(0, 1)
            silu(0, 1)
            evac_xe(1, 2)
            step(1, None)
            step(2, None)
            with act.Fori(1, E // 2 - 1) as i:
                step(1, i)
                step(2, i)
            step(E - 1, None, last=True)
            evac_hT(1, E)
            evac_y(1, E, 16 * (E // 2 - 1))
            act.wait_ge(ov_ready, 1)
            nov = act.value_load(ovi[0:1, 0:1], min_val=0, max_val=NOV)
            with act.If(nov > 0):
                with act.Fori(0, nov) as i:
                    evac_xe(0, i + E + 1)
                    silu(0, i + E + 1)
                    evac_hT(0, i + E + 1)
                    evac_y(0, i + E + 1, i * 16 + 16 * (E // 2))

            for j in range(NT):
                r = ROWS[j]
                act.wait_ge(s_fin[j], 16)
                act.activation(ring[0:r, j, 0:D], ring[0:r, j, 0:D], ACT.Copy, scale=wts[0:r, 0, j:j + 1]).then_inc(f_a, 1)
            for j in range(NT):
                r = ROWS[j]
                act.wait_ge(f_v, j + 1)
                v = stat[0:r, j % 2, 13:14]
                link(act.activation(v, v, ACT.Ln, bias=epst[0:r, 0:1]))
                act.activation(v, v, ACT.Exp, scale=-0.5).then_inc(f_l, 1)

        @block.tensor
        def _(pe):
            pe.wait_ge(pl, NCONST)
            pe.wait_ge(s_c, 32)
            pe.transpose(bank[0][:, 0:2 * KD], crow[:, :], ident[0:2 * KD, 0:2 * KD]).then_inc(pe_c, 1)
            pe.wait_ge(s_x, 32)
            for q in range(2 * NT):
                j, half = q // 2, q % 2
                r = ROWS[j]
                if q >= 2:
                    pe.wait_ge(xt_ev, q - 1)
                for k in range(4):
                    kk = 4 * half + k
                    mm = pe.transpose(bank[1 + q % 2][:, k * r:(k + 1) * r], x_tok[0:r, j, kk * P:(kk + 1) * P], ident[0:r, 0:r])
                mm.then_inc(pe_xt, 1)
            pe.wait_ge(cs_ready, 1)
            pe.wait_ge(s_adab, 16)
            cs3 = csT[:, :].rearrange("p (b k) -> p b k", b=2)

            def wait_unit(n):
                pe.wait_ge(full[n % NR], full_count(n))

            def ada(u, bk):
                n = number[("ada", u)]
                wait_unit(n)
                w = slot_view(n, KD)
                pe.matmul(bank[bk][0:2, 0:UC], ident[0:NA, u:u + 1].to_broadcast([NA, 2]), adab[:, :], start=True, stop=False)
                for k in range(KD):
                    mm = pe.matmul(bank[bk][0:2, 0:UC], cs3[:, :, k], w[:, k, :], start=False, stop=(k == KD - 1))
                mm.then_inc(pe_mod, 1)

            for u in range(NA1):
                if u >= 2:
                    pe.wait_ge(ada_ev, u - 1)
                ada(u, 3 + u % 2)
            pe.wait_ge(ada_ev, NA1)
            for i in range(2 * KD):
                mm = pe.transpose(bank[0][:, 32 + 2 * i:34 + 2 * i], modst[:, i * P:(i + 1) * P], ident[0:2, 0:2])
            mm.then_inc(pe_sc, 1)

            def proj_t(tb, lhs):
                m = RANK if tb == 0 else P
                if tb >= 2:
                    pe.wait_ge(t_ev, 2 * (tb - 1))
                for k in range(KD):
                    pe.matmul(bank[1 + tb % 2][0:m, 0:LP], lhs(k), hT[:, k, 0:LP], start=(k == 0), stop=(k == KD - 1))
                for k in range(KD):
                    mm = pe.matmul(bank[5 + tb % 2][0:m, 0:LS], lhs(k), hT[:, k, LP:T], start=(k == 0), stop=(k == KD - 1))
                return mm

            pe.wait_ge(s_misc, 16 * 7)
            pe.wait_ge(h_ready, 2 * KD)
            proj_t(0, lambda k: wga[:, k, :]).then_inc(pe_t, 1)
            tb = 1
            for kind in ("gq", "gk"):
                n = number[(kind, 0)]
                wait_unit(n)
                v = slot_view(n, KD)
                for b in range(2):
                    proj_t(tb, lambda k: v[:, k, b * P:(b + 1) * P]).then_inc(pe_t, 1)
                    tb += 1
                if kind == "gq":
                    pe.wait_ge(t_ev, 2)
                    for j in range(NT):
                        if j >= 2:
                            pe.wait_ge(z_ev, j - 1)
                        pe.matmul(bank[7 if j % 2 == 0 else 0][0:ROWS[j], 0:H * DK], gaT[:, tok(j)], a2w[:, :],
                                  start=True, stop=True).then_inc(pe_z, 1)
            pe.wait_ge(l_ready, 1)
            for j in range(NT):
                r = ROWS[j]
                pe.wait_ge(z_ev, 5 + j - 1 if j >= 1 else 5)
                for half in range(2):
                    mm = pe.matmul(bank[7 if j % 2 == 0 else 0][:, half * r:(half + 1) * r], z[0:r, j, half * P:(half + 1) * P],
                                   tri[0:r, 0:r], start=True, stop=True)
                mm.then_inc(pe_z, 1)
            for kind in ("sq0", "sq1"):
                n = number[(kind, 0)]
                wait_unit(n)
                v = slot_view(n, KD)
                for b in range(2):
                    proj_t(tb, lambda k: v[:, k, b * P:(b + 1) * P]).then_inc(pe_t, 1)
                    tb += 1
            n = number[("kv", 0)]
            wait_unit(n)
            v = slot_view(n, KD)
            proj_t(tb, lambda k: v[:, k, 0:2 * HD]).then_inc(pe_t, 1)
            pe.wait_ge(s_kc, 16)
            pe.wait_ge(t_ev, 18)
            pe.transpose(bank[1][:, 0:WIN], kc[:, :], ident[:, :]).then_inc(pe_t, 1)

            m = 0
            for kind in ("kv", "gv0", "gv1", "gr0", "gr1"):
                n = number[(kind, 0)]
                wait_unit(n)
                v = slot_view(n, KD)
                for j in range(NT):
                    r = ROWS[j]
                    c0 = 0 if kind != "kv" or j >= NP - 1 else 2 * HD
                    if m >= 2:
                        pe.wait_ge(tok_ev, m - 1)
                    for k in range(KD):
                        mm = pe.matmul(bank[3 + m % 2][0:r, 0:UC - c0], hT[:, k, tok(j)], v[:, k, c0:UC],
                                       start=(k == 0), stop=(k == KD - 1))
                    mm.then_inc(pe_tok, 1)
                    m += 1

            pe.wait_ge(gla_ready, 1)
            for j in range(NT + 1):
                if j < NT:
                    r = ROWS[j]
                    pe.wait_ge(kd_ev, j) if j >= 1 else pe.wait_ge(z_ev, 10)
                    for half in range(2):
                        mm = pe.transpose(bank[0][0:r, half * P:(half + 1) * P], ed[:, half, tok(j)], ident[:, :])
                    mm.then_inc(pe_kd, 1)
                if j >= 1:
                    i = j - 1
                    pe.wait_ge(kd_ev, i + 1)
                    pe.wait_ge(tok_ev, 15)
                    if i >= 1:
                        pe.wait_ge(u_ev, i)
                    else:
                        pe.wait_ge(t_ev, 21)
                    for c in range(2 if i < NP else 1):
                        r0 = c * CH
                        r1 = r0 + min(CH, ROWS[i])
                        for h in range(H):
                            mm = pe.matmul(bank[6 + c][(h % 2) * DK:(h % 2 + 1) * DK, (h // 2) * DV:(h // 2 + 1) * DV],
                                           kdT[r0:r1, i % 2, h * DK:(h + 1) * DK], gv[r0:r1, i, h * DV:(h + 1) * DV],
                                           start=True, stop=True)
                    mm.then_inc(pe_u, 1)

            def gla_scores(j):
                r = ROWS[j]
                if j >= 1:
                    pe.wait_ge(a_ev, j)
                for par in range(2):
                    q0 = par * DK
                    for a in range(2):
                        for up in range(2):
                            ks, qs = (ebn, eb) if up == 0 else (bc, gq)
                            mm = pe.matmul(bank[1 + par][0:r, (2 * up + a) * P:(2 * up + a) * P + r],
                                           ks[q0:q0 + DK, a, tok(j)], qs[q0:q0 + DK, a, tok(j)], start=True, stop=True)
                mm.then_inc(pe_a, 1)

            def gla_out(j):
                r = ROWS[j]
                pe.wait_ge(a_ev, j + 1)
                pe.wait_ge(u_ev, j + 1)
                if j >= 1:
                    pe.wait_ge(o_sq, j)
                else:
                    pe.wait_ge(tok_ev, 25)
                for par in range(2):
                    for a in range(2):
                        h = 2 * a + par
                        out = bank[3 + par][:, a * DV:(a + 1) * DV]
                        pe.matmul(out[0:r, :], At[0:r, j % 2, h, 0:r], gv[0:r, j, h * DV:(h + 1) * DV], start=True, stop=False)
                        for c in range(2 if j < NP else 1):
                            n = 2 * j + c if j < NP else NCH + 1
                            c0, cn = c * CH, min(CH, r)
                            mm = pe.matmul(out[c0:c0 + cn, :], eb[par * DK:(par + 1) * DK, a, P * j + c0:P * j + c0 + cn],
                                           S[par * DK:(par + 1) * DK, n, a, :], start=False, stop=True)
                mm.then_inc(pe_o, 1)

            def gla_turn(j):
                r = ROWS[j]
                pe.wait_ge(og_ready, j + 1)
                if j >= 1:
                    pe.wait_ge(mg_ev, j)
                for k in range(4):
                    mm = pe.transpose(bank[5][:, k * r:(k + 1) * r], og[0:r, k * P:(k + 1) * P], ident[0:r, 0:r])
                mm.then_inc(pe_og, 1)

            for j in range(NT + 2):
                if j < NT:
                    gla_scores(j)
                if 1 <= j <= NT:
                    gla_out(j - 1)
                if j >= 2:
                    gla_turn(j - 2)

            def qk(j):
                r = ROWS[j]
                if j >= 1:
                    pe.wait_ge(s_ev, 4 * j)
                k0, k1 = (0, P) if j == 0 else (P * (j - 1), P * (j + 1)) if j < NP else (LP, LP + WIN + LS)
                n = k1 - k0
                for g in range(2):
                    for par in range(2):
                        q0 = par * HD
                        for a in range(2):
                            mm = pe.matmul(bank[1 + 2 * g + par][0:r, a * KW:a * KW + n], sqT[q0:q0 + HD, 2 * g + a, tok(j)],
                                           skT[q0:q0 + HD, k0:k1], start=True, stop=True)
                        mm.then_inc(pe_qk, 1)

            def key_blocks(j):
                return [(0, P)] if j == 0 else [(0, P), (P, P)] if j < NP else [(0, P), (P, LS)]

            def pt(j):
                r = ROWS[j]
                pe.wait_ge(p_ready, j + 1)
                nb = len(key_blocks(j))
                for f in range(4):
                    fill = 4 * j + f
                    if fill >= 2:
                        pe.wait_ge(pt_ev, fill - 1)
                    for h in range(2):
                        for b, (kb, kn) in enumerate(key_blocks(j)):
                            c = (h * nb + b) * r
                            mm = pe.transpose(bank[5 + f % 2][0:kn, c:c + r], Ssc[0:r, 2 * f + h, kb:kb + kn], ident[0:r, 0:r])
                    mm.then_inc(pe_pt, 1)

            def pv(j):
                r = ROWS[j]
                pe.wait_ge(pt_ev, 4 * (j + 1))
                if j >= 1:
                    pe.wait_ge(pv_ev, j)
                tiles = [0] if j == 0 else [j - 1, j] if j < NP else [NP, NP + 1]
                for i in range(4):
                    for g in range(2):
                        for b, (kb, kn) in enumerate(key_blocks(j)):
                            mm = pe.matmul(bank[7][g * HD:(g + 1) * HD, i * r:(i + 1) * r], svt[0:kn, tiles[b], g * HD:(g + 1) * HD],
                                           PT[0:kn, 4 * g + i, b, 0:r], start=(b == 0), stop=(b == len(tiles) - 1))
                mm.then_inc(pe_pv, 1)

            rest = list(range(NA1, NA))
            for j in range(NT + 1):
                if j < NT:
                    qk(j)
                if j >= 1:
                    pt(j - 1)
                for u in (rest[4 * j:4 * j + 4] if j < 4 else []):
                    pe.wait_ge(ada_ev, u)
                    ada(u, 0)
                if j >= 1:
                    pv(j - 1)

            def out_proj(j):
                r = ROWS[j]
                if j >= 2:
                    pe.wait_ge(y_ev, j - 1)
                for u in range(KD // 2):
                    n = number[("wo", u)]
                    wait_unit(n)
                    v = slot_view(n, 2)
                    for kk in range(2):
                        k = 2 * u + kk
                        for half in range(2):
                            mm = pe.matmul(bank[1 + 2 * (j % 2) + half][0:r, :], mixT[:, k, tok(j)], v[:, kk, half * 512:(half + 1) * 512],
                                           start=(k == 0), stop=(k == KD - 1))
                    if j == NT - 1 and u < KD // 2 - 1:
                        mm.then_inc(wo_used, 1)
                mm.then_inc(pe_y, 1)

            def route(j):
                r = ROWS[j]
                pe.wait_ge(h2_ready, j + 1)
                for half in range(2):
                    if j >= 1:
                        pe.wait_ge(ht_ev, 2 * j)
                    for k in range(4):
                        kk = 4 * half + k
                        mm = pe.transpose(bank[5 + half][:, k * r:(k + 1) * r], h2[0:r, j % 2, kk * P:(kk + 1) * P], ident[0:r, 0:r])
                    mm.then_inc(pe_ht, 1)
                pe.wait_ge(ht_ev, 2 * (j + 1))
                if j >= 1:
                    pe.wait_ge(rt_ev, j)
                for k in range(KD):
                    mm = pe.matmul(bank[7][0:r, 0:NG + E], h2Tt[:, k, 0:r], rw[:, k, :], start=(k == 0), stop=(k == KD - 1))
                mm.then_inc(pe_rt, 1)

            pe.wait_ge(mg_ev, NT)
            pe.wait_ge(pv_ev, NT)
            pe.wait_ge(s_misc2, 16 * (NG + 3))
            for j in range(NT + 2):
                if j < NT:
                    out_proj(j)
                if j >= 2:
                    route(j - 2)

            pe.wait_ge(oh_ready, 1)
            M = rt[:, 3, :].rearrange("p (j e) -> p j e", j=NT)
            for j in range(NT):
                for i in range(j + 1):
                    lhs = before if i == j else ones
                    mm = pe.matmul(bank[0][:, j * E:(j + 1) * E], lhs[0:ROWS[i], :], M[0:ROWS[i], i, :], start=(i == 0), stop=(i == j))
            for i in range(NT):
                mm = pe.matmul(bank[0][:, NT * E:(NT + 1) * E], ones[0:ROWS[i], :], M[0:ROWS[i], i, :], start=(i == 0), stop=(i == NT - 1))
            mm.then_inc(pe_rank, 1)
            pe.wait_ge(s_trow, 16)
            pe.transpose(bank[7][:, 0:NBLK], trow[:, :], ident[0:NBLK, 0:NBLK]).then_inc(pe_tbl, 1)

            def turn_x(a, gw):
                pe.wait_ge(s_g[a], gw)
                for k in range(KD):
                    mm = pe.transpose(bank[k // 4][:, (k % 4) * P:(k % 4 + 1) * P], xg[:, a, k * P:(k + 1) * P], ident[:, :])
                mm.then_inc(pe_xe, 1)

            def gate_up(a, wg, wu):
                for out, w, done in ((0, wg, pe_g), (FF, wu, pe_gu)):
                    for k in range(KD):
                        mm = pe.matmul(bank[2 + a][:, out:out + FF], xTe[:, a, k, :], w[:, k, :], start=(k == 0), stop=(k == KD - 1))
                    mm.then_inc(done, 1)

            def turn_h(a):
                for k in range(NF):
                    mm = pe.transpose(bank[4][:, k * P:(k + 1) * P], hid[:, a, k * P:(k + 1) * P], ident[:, :])
                mm.then_inc(pe_hT, 1)

            def down(a, w):
                for k in range(NF):
                    for half in range(2):
                        mm = pe.matmul(bank[5 + half][:, :], hidT[:, a, k, :], w[:, k, half * 512:(half + 1) * 512],
                                       start=(k == 0), stop=(k == NF - 1))
                return mm

            def expert_up(e, i):
                n = N0 + 3 * e
                pe.wait_ge(xe_a, at(e + 1, 2, i))
                pe.wait_ge(xe_d, at(e + 1, 2, i))
                if e >= 2 or i is not None:
                    pe.wait_ge(hid_done, at(e - 1, 2, i))
                pe.wait_ge(full[n % NR], at(expert_count(n), 16, i))
                pe.wait_ge(full[(n + 1) % NR], at(expert_count(n + 1), 16, i))
                gate_up(e % 2, slot_view(n, KD), slot_view(n + 1, KD))

            def expert_turn(e, i):
                pe.wait_ge(hid_done, at(e + 1, 2, i))
                if e >= 1:
                    pe.wait_ge(hT_ev, at(e, 2, i))
                turn_h(e % 2)

            def rows_turn(e, i):
                pe.wait_ge(xe_a, at(e, 2, i))
                pe.wait_ge(xe_d, at(e, 2, i))
                turn_x(e % 2, at(16 * (e // 2 + 1), 16, i))

            def expert_down(e, i):
                n = N0 + 3 * e + 2
                pe.wait_ge(hT_ev, at(e + 1, 2, i))
                if e >= 1 or i is not None:
                    pe.wait_ge(y_a, at(e, 2, i))
                    pe.wait_ge(y_d, at(e, 2, i))
                pe.wait_ge(full[n % NR], at(expert_count(n), 16, i))
                down(e % 2, slot_view(n, NF)).then_inc(pe_dn, 1)

            def step(e, i):
                expert_up(e, i)
                expert_turn(e - 1, i)
                rows_turn(e + 1, i)
                expert_down(e - 1, i)

            pe.wait_ge(tbl_ready, 1)
            turn_x(0, 16)
            expert_up(0, None)
            rows_turn(1, None)
            step(1, None)
            step(2, None)
            with pe.Fori(1, E // 2 - 1) as i:
                step(1, i)
                step(2, i)
            expert_up(E - 1, None)
            expert_turn(E - 2, None)
            expert_down(E - 2, None)
            expert_turn(E - 1, None)
            expert_down(E - 1, None)
            pe.wait_ge(ov_ready, 1)
            nov = pe.value_load(ovi[0:1, 0:1], min_val=0, max_val=NOV)
            with pe.If(nov > 0):
                with pe.Fori(0, nov) as i:
                    turn_x(0, i * 16 + 16 * (E // 2) + 16)
                    pe.wait_ge(xe_a, i + E + 1)
                    pe.wait_ge(xe_d, i + E + 1)
                    pe.wait_ge(o_w, i * 48 + 48)
                    gate_up(0, ring[:, 0, :].rearrange("p (k n) -> p k n", k=KD), ring[:, 1, :].rearrange("p (k n) -> p k n", k=KD))
                    pe.wait_ge(hid_done, i + E + 1)
                    turn_h(0)
                    pe.wait_ge(hT_ev, i + E + 1)
                    down(0, ring[:, 2, :].rearrange("p (k n) -> p k n", k=NF)).then_inc(pe_dn, 1)

        @block.vector
        def _(dve):
            chain = [0]

            def link(ins):
                chain[0] += 1
                ins.then_inc(dv, 1)
                dve.wait_ge(dv, chain[0])

            def bcast(ap, shape):
                return ap.broadcast_to(shape)

            dve.wait_ge(pl, NCONST)
            link(dve.scalar_tensor_tensor(dist[:, :], dist[:, :], -1.0, dist[:, :], ALU.mult, ALU.max))
            link(dve.memset(dist[0:CH, WIN + CH:KW], 1e32))
            link(dve.memset(dist[CH:P, 0:CH], 1e32))
            for h in range(NQ):
                dve.tensor_scalar(biasH[:, h, :], dist[:, :], -(2.0 ** (-(8.0 / NQ) * (h + 1))), None, ALU.mult)
            dve.wait_ge(c_ex, 1)
            link(dve.tensor_scalar(cx[:, :], cx[:, :], 1.0, None, ALU.add))
            link(dve.reciprocal(cx[:, :], cx[:, :]))
            dve.tensor_tensor(csT[:, :], bank[0][:, 0:2 * KD], cx[:, :], ALU.mult).then_inc(cs_ready, 1)

            def mod_evac(u, bk):
                dve.wait_ge(pe_mod, u + 1)
                if u >= 2 * NA1:
                    dve.wait_ge(s_mod, 16)
                dve.tensor_copy(modst[:, (u % NA1) * UC:(u % NA1 + 1) * UC], bank[bk][0:2, 0:UC]).then_inc(ada_ev, 1)

            for u in range(NA1):
                mod_evac(u, 3 + u % 2)
            dve.wait_ge(pe_sc, 1)
            link(dve.tensor_copy(shsc[:, 0:2 * KD], bank[0][:, 32:32 + 2 * KD]))
            link(dve.tensor_scalar(shsc[:, 2 * KD:4 * KD], bank[0][:, 32 + 2 * KD:32 + 4 * KD], 1.0, None, ALU.add))
            dve.wait_ge(xt_ev, 2 * NT)
            for k in range(KD):
                for b, cs in ((0, slice(0, LP)), (1, slice(LP, T))):
                    dve.tensor_scalar(hT[:, k, cs], hT[:, k, cs], shsc[:, 2 * KD + 2 * k + b:2 * KD + 2 * k + b + 1],
                                      shsc[:, 2 * k + b:2 * k + b + 1], ALU.mult, ALU.add).then_inc(h_ready, 1)
            dve.wait_ge(s_misc, 16 * 7)
            for j in range(NT):
                r = ROWS[j]
                dve.wait_ge(pe_z, j + 1)
                dve.tensor_tensor(z[0:r, j, :], bank[7 if j % 2 == 0 else 0][0:r, 0:H * DK], a2b[0:r, :], ALU.add).then_inc(z_ev, 1)
            dve.wait_ge(z_ev, NT)
            dve.scalar_tensor_tensor(zt, z, -1.0, z, ALU.mult, ALU.max).then_inc(z_abs, 1)
            dve.wait_ge(z_ln, 1)
            dve.scalar_tensor_tensor(z, z, 0.0, zt, ALU.min, ALU.subtract).then_inc(l_ready, 1)
            for j in range(NT):
                r = ROWS[j]
                dve.wait_ge(pe_z, NT + j + 1)
                dve.tensor_copy(bc[:, :, tok(j)], bank[7 if j % 2 == 0 else 0][:, 0:2 * r].rearrange("p (a t) -> p a t", a=2)).then_inc(z_ev, 1)
            dve.wait_ge(z_ev, 2 * NT)
            for a in range(2):
                bp = bc[:, a, 0:LP].rearrange("p (n t) -> p n t", t=CH)
                link(dve.tensor_tensor(ed[:, a, 0:LP].rearrange("p (n t) -> p n t", t=CH),
                                       bcast(bp[:, :, CH - 1:CH], [P, NCH, CH]), bp, ALU.subtract))
                dve.tensor_tensor(ed[:, a, LP:T], bcast(bc[:, a, T - 1:T], [P, LS]), bc[:, a, LP:T], ALU.subtract).then_inc(b_ready, 1)
            dve.wait_ge(e_ready, 3)
            dve.wait_ge(t_ev, 10)
            for a in range(2):
                dve.tensor_copy(gend[:, a, 0:NCH], eb[:, a, 0:LP].rearrange("p (n t) -> p n t", t=CH)[:, :, CH - 1])
                link(dve.tensor_copy(gend[:, a, NCH:NCH + 1], eb[:, a, T - 1:T]))
            link(dve.tensor_tensor(bc, gk, eb, ALU.mult))
            link(dve.tensor_tensor(eb, gq, eb, ALU.mult))
            link(dve.tensor_tensor(gq, gq, ebn, ALU.mult))
            link(dve.tensor_tensor(ebn, gk, ebn, ALU.mult))
            dve.tensor_tensor(ed, gk, ed, ALU.mult).then_inc(gla_ready, 1)
            m = 0
            for kind in range(5):
                for j in range(NT):
                    r = ROWS[j]
                    dve.wait_ge(pe_tok, m + 1)
                    src = bank[3 + m % 2]
                    if kind == 0:
                        i = NP + 1 if j == NP else j
                        if j >= NP - 1:
                            link(dve.tensor_copy(skt[0:r, j - NP + 1, :], src[0:r, 0:2 * HD]))
                            dve.tensor_copy(svt[0:r, i, :], src[0:r, 2 * HD:4 * HD]).then_inc(tok_ev, 1)
                        else:
                            dve.tensor_copy(svt[0:r, i, :], src[0:r, 0:2 * HD]).then_inc(tok_ev, 1)
                    else:
                        dst = gv if kind < 3 else grg
                        c = UC * ((kind - 1) % 2)
                        dve.tensor_copy(dst[0:r, j, c:c + UC], src[0:r, 0:UC]).then_inc(tok_ev, 1)
                    m += 1
            for j in range(NT):
                dve.wait_ge(pe_u, j + 1)
                for c in range(2 if j < NP else 1):
                    n = 2 * j + c
                    s0, s1 = (n, n + 1) if j < NP else (NCH + 1, NCH + 2)
                    for a in range(2):
                        last = dve.scalar_tensor_tensor(S[:, s1, a, :], S[:, s0, a, :], gend[:, a, n:n + 1],
                                                        bank[6 + c][:, a * DV:(a + 1) * DV], ALU.mult, ALU.add)
                        if a == 0 or c == 0 and j < NP:
                            link(last)
                        else:
                            last.then_inc(u_ev, 1)
                            dve.wait_ge(u_ev, j + 1)

            def mask(j):
                r = ROWS[j]
                dve.wait_ge(pe_a, j + 1)
                if j >= 2:
                    dve.wait_ge(pe_o, j - 1)
                for par in range(2):
                    a4 = At[0:r, j % 2, :, 0:r].rearrange("p (a b) t -> p a b t", b=2)[:, :, par, :]
                    for up, mk in ((0, tri), (1, tup)):
                        src = bank[1 + par][0:r, 2 * up * P:2 * (up + 1) * P].rearrange("p (a t) -> p a t", a=2)[:, :, 0:r]
                        last = dve.copy_predicated(a4, bcast(mk[0:r, 0:r].bitcast(i32).unsqueeze(1), [r, 2, r]), src)
                        if up == 0 or par == 0:
                            link(last)
                last.then_inc(a_ev, 1)

            def gated(j):
                r = ROWS[j]
                dve.wait_ge(o_sq, j + 1)
                gx = gex[0:r, j % 2, :]
                o = osb[0:r, j % 2, :]
                link(dve.tensor_scalar(gx, gx, 1.0, None, ALU.add))
                link(dve.reciprocal(gx, gx))
                link(dve.tensor_tensor(gx, gx, grg[0:r, j, :], ALU.mult))
                h3 = [r, H, DV]
                gx3, o3 = gx.rearrange("p (h v) -> p h v", h=H), o.rearrange("p (h v) -> p h v", h=H)
                link(dve.tensor_tensor(gx3, gx3, bcast(nw[0:r, :].unsqueeze(1), h3), ALU.mult))
                link(dve.tensor_tensor(o3, o3, bcast(small[0:r, 8 * (j % 2):8 * (j % 2) + H].unsqueeze(2), h3), ALU.mult))
                if j >= 1:
                    dve.wait_ge(pe_og, j)
                dve.tensor_tensor(og[0:r, :], o, gx, ALU.mult).then_inc(og_ready, 1)

            for j in range(NT + 1):
                if j < NT:
                    mask(j)
                if j >= 1:
                    gated(j - 1)

            rest = list(range(NA1, NA))
            for j in range(NT):
                r = ROWS[j]
                w0, w1 = (P, KW) if j == 0 else (0, KW) if j < NP else (0, WIN + LS)
                n = w1 - w0
                if j >= 1:
                    dve.wait_ge(pe_pt, 4 * j)
                for g in range(2):
                    for par in range(2):
                        dve.wait_ge(pe_qk, 4 * j + 2 * g + par + 1)
                        h0 = 4 * par + 2 * g
                        dve.scalar_tensor_tensor(Ssc[0:r, h0:h0 + 2, 0:n],
                                                 bank[1 + 2 * g + par][0:r, :].rearrange("p (a n) -> p a n", a=2)[:, :, 0:n],
                                                 HD ** -0.5, biasH[0:r, h0:h0 + 2, w0:w1], ALU.mult, ALU.add).then_inc(s_ev, 1)
                dve.wait_ge(s_ev, 4 * (j + 1))
                mx, nm, rsum, es = (small[0:r, 8 * i + 16:8 * i + 24] for i in range(4))
                link(dve.tensor_reduce(mx, Ssc[0:r, :, 0:n], AX.X, ALU.max))
                link(dve.tensor_tensor(mx, mx, sinks[0:r, :], ALU.max))
                link(dve.tensor_tensor(es, sinks[0:r, :], mx, ALU.subtract))
                dve.tensor_scalar(nm, mx, -1.0, None, ALU.mult).then_inc(m_ready, 1)
                for u in (rest[4 * j:4 * j + 4] if j < 4 else []):
                    mod_evac(u, 0)
                dve.wait_ge(p_exp, j + 1)
                link(dve.tensor_tensor(rsum, rsum, es, ALU.add))
                link(dve.reciprocal(rsum, rsum))
                dve.tensor_tensor(Ssc[0:r, :, 0:n], Ssc[0:r, :, 0:n], bcast(rsum.unsqueeze(2), [r, NQ, n]), ALU.mult).then_inc(p_ready, 1)

            dve.wait_ge(s_modb, 32)
            dve.wait_ge(s_ln1, 32)

            def ln_stats(x, j, done):
                r = ROWS[j]
                st = stat[0:r, j % 2, :]
                link(dve.bn_stats(st[:, 0:6], x[:, 0:512]))
                link(dve.bn_stats(st[:, 6:12], x[:, 512:D]))
                dve.bn_aggr(st[:, 12:14], st[:, 0:12]).then_inc(done, 1)

            def ln_finish(x, j, rows):
                r = ROWS[j]
                st = stat[0:r, j % 2, :]
                link(dve.tensor_scalar(x, x, st[:, 12:13], st[:, 13:14], ALU.subtract, ALU.mult))
                link(dve.tensor_tensor(x, x, rows[0:r, 0, :], ALU.mult))

            def logits(j):
                r = ROWS[j]
                dve.wait_ge(pe_rt, j + 1)
                dve.tensor_tensor(lg[0:r, j, :], bank[7][0:r, 0:NG + E], rb[0:r, :], ALU.add).then_inc(rt_ev, 1)

            for j in range(NT):
                r = ROWS[j]
                md = modP if j < NP else modS
                x = x_tok[0:r, j, :]
                dve.wait_ge(pe_y, j + 1)
                for half in range(2):
                    c = slice(512 * half, 512 * (half + 1))
                    last = dve.tensor_tensor(ytmp[0:r, c], bank[1 + 2 * (j % 2) + half][0:r, :], md[0:r, 0, c], ALU.mult)
                    if half == 0:
                        link(last)
                last.then_inc(y_ev, 1)
                dve.wait_ge(y_ev, j + 1)
                link(dve.scalar_tensor_tensor(x, x, ALPHA, ytmp[0:r, :], ALU.mult, ALU.add))
                ln_stats(x, j, v_ready)
                dve.wait_ge(v_ln, j + 1)
                ln_finish(x, j, ln1)
                link(dve.tensor_tensor(x, x, ln1[0:r, 1, :], ALU.add))
                if j >= 2:
                    dve.wait_ge(h2_st[j % 2], 16 * (j // 2))
                    dve.wait_ge(pe_ht, 2 * (j - 1))
                link(dve.scalar_tensor_tensor(h2[0:r, j % 2, :], md[0:r, 2, :], 1.0, x, ALU.add, ALU.mult))
                dve.tensor_tensor(h2[0:r, j % 2, :], h2[0:r, j % 2, :], md[0:r, 1, :], ALU.add).then_inc(h2_ready, 1)
                if j >= 1:
                    logits(j - 1)
            logits(NT - 1)

            R5, R4 = [P, NT, E], [P, NT, NG]
            g, ex = lg[:, :, 0:NG], lg[:, :, NG:NG + E]

            def q5(i):
                return rt[:, i, :].rearrange("p (j e) -> p j e", j=NT)

            def q4(i):
                return rt[:, i, 0:NT * NG].rearrange("p (j e) -> p j e", j=NT)

            def over(i, shape):
                return bcast(rs[:, i, :].unsqueeze(2), shape)

            def first_max(v, mxi, eq, out, n, shape):
                link(dve.tensor_tensor(eq, v, over(mxi, shape), ALU.is_equal))
                link(dve.tensor_tensor(eq, eq, bcast(iow[:, 0:n].unsqueeze(1), shape), ALU.mult))
                link(dve.tensor_reduce(rs[:, 9, :], eq, AX.X, ALU.max))
                link(dve.tensor_tensor(out, eq, over(9, shape), ALU.is_equal))

            dve.wait_ge(rt_ev, NT)
            link(dve.tensor_reduce(rs[:, 0, :], g, AX.X, ALU.max))
            link(dve.tensor_tensor(q4(0), g, over(0, R4), ALU.subtract))
            first_max(g, 0, q4(1), q4(2), NG, R4)
            link(dve.tensor_scalar(q4(2), q4(2), 1e30, -1e30, ALU.mult, ALU.add))
            link(dve.tensor_tensor(ex.rearrange("p j (g e) -> p j g e", g=NG), ex.rearrange("p j (g e) -> p j g e", g=NG),
                                   bcast(q4(2).unsqueeze(3), [P, NT, NG, NE]), ALU.add))
            link(dve.tensor_reduce(rs[:, 3, :], ex, AX.X, ALU.max))
            first_max(ex, 3, q5(6), q5(4), E, R5)
            link(dve.scalar_tensor_tensor(q5(6), q5(4), -2e30, ex, ALU.mult, ALU.add))
            link(dve.tensor_reduce(rs[:, 4, :], q5(6), AX.X, ALU.max))
            first_max(q5(6), 4, q5(7), q5(5), E, R5)
            dve.tensor_tensor(q5(3), q5(4), q5(5), ALU.add).then_inc(oh_ready, 1)
            dve.tensor_tensor(rs[:, 5, :], rs[:, 4, :], rs[:, 3, :], ALU.subtract).then_inc(r_ex0, 1)

            dve.wait_ge(pe_rank, 1)
            cnt = bank[0][:, NT * E:(NT + 1) * E]
            link(dve.tensor_scalar(ov[:, 1, :], cnt, float(P), None, ALU.is_gt))
            for m in range(2, OVT + 1):
                link(dve.scalar_tensor_tensor(ov[:, 1, :], cnt, float(m * P), ov[:, 1, :], ALU.is_gt, ALU.add))
            link(dve.tensor_copy(ov[:, 2, :], ov[:, 1, :]))
            a, sh = 2, 1
            while sh < E:
                link(dve.tensor_copy(ov[:, 5 - a, 0:sh], ov[:, a, 0:sh]))
                link(dve.tensor_tensor(ov[:, 5 - a, sh:E], ov[:, a, sh:E], ov[:, a, 0:E - sh], ALU.add))
                a, sh = 5 - a, 2 * sh
            link(dve.tensor_tensor(ov[:, 4, :], ov[:, a, :], ov[:, 1, :], ALU.subtract))
            link(dve.tensor_scalar(ov[:, 4, :], ov[:, 4, :], float(P), float(E * P - P), ALU.mult, ALU.add))
            link(dve.tensor_tensor(ov[:, 4, :], ov[:, 4, :], ov[:, 0, :], ALU.subtract))
            rank = bank[0][:, 0:NT * E].rearrange("p (j e) -> p j e", j=NT)
            link(dve.scalar_tensor_tensor(q5(6), rank, float(P), bcast(ov[:, 4, :].unsqueeze(1), R5), ALU.is_ge, ALU.mult))
            link(dve.tensor_tensor(q5(7), rank, bcast(ov[:, 0, :].unsqueeze(1), R5), ALU.add))
            link(dve.tensor_tensor(q5(6), q5(6), q5(7), ALU.add))
            for k in range(2):
                link(dve.tensor_tensor(q5(7), q5(6), q5(4 + k), ALU.mult))
                link(dve.tensor_reduce(rs[:, 6 + k, :], q5(7), AX.X, ALU.add))
                last = dve.tensor_copy(posi[:, k, :], rs[:, 6 + k, :])
                if k == 0:
                    link(last)
            last.then_inc(pos_ready, 1)
            dve.wait_ge(r_ex, 1)
            link(dve.tensor_reduce(rs[:, 1, :], q4(0), AX.X, ALU.add))
            link(dve.tensor_scalar(rs[:, 2, :], rs[:, 5, :], 1.0, None, ALU.add))
            link(dve.tensor_tensor(rs[:, 1, :], rs[:, 1, :], rs[:, 2, :], ALU.mult))
            link(dve.reciprocal(wts[:, 0, :], rs[:, 1, :]))
            link(dve.tensor_tensor(wts[:, 1, :], wts[:, 0, :], rs[:, 5, :], ALU.mult))
            link(dve.tensor_copy(ovi[0:1, 0:1], ov[0:1, a, E - 1:E]))
            for b in range(NOV):
                link(dve.tensor_scalar(ov[0:1, 1, :], ov[0:1, a, :], float(b), None, ALU.is_le))
                link(dve.tensor_reduce(rs[0:1, 8, 0:1], ov[0:1, 1, :], AX.X, ALU.add))
                link(dve.tensor_scalar(rs[0:1, 8, 0:1], rs[0:1, 8, 0:1], float(E - 1), None, ALU.min))
                last = dve.tensor_copy(ovi[0:1, b + 1:b + 2], rs[0:1, 8, 0:1])
                if b < NOV - 1:
                    link(last)
            last.then_inc(ov_ready, 1)
            dve.wait_ge(pe_tbl, 1)
            ent = bank[7][:, 0:NBLK]
            link(dve.tensor_copy(dsti[:, :], ent))
            link(dve.tensor_scalar(fl[:, :], ent, float(KSTEP), -float(KSTEP), ALU.is_ge, ALU.mult))
            dve.tensor_tensor(srci[:, :], ent, fl[:, :], ALU.add).then_inc(tbl_ready, 1)

            def evac_xe(a, w):
                dve.wait_ge(pe_xe, w)
                dve.tensor_copy(xTe[:, a, 4:8, :], bank[1][:, :].rearrange("p (k t) -> p k t", k=4)).then_inc(xe_d, 1)

            def hidden(a, w):
                dve.wait_ge(sg_done, w)
                dve.tensor_tensor(hid[:, a, :], bank[2 + a][:, FF:2 * FF], sgl[:, a, :], ALU.mult).then_inc(hid_done, 1)

            def evac_y(a, w, free):
                dve.wait_ge(pe_dn, w)
                if free is not None:
                    dve.wait_ge(s_sc[a], free)
                dve.tensor_copy(ye[:, a, 512:D], bank[6][:, :]).then_inc(y_d, 1)

            def step(e, i, last=False):
                x, b = e % 2, (e - 1) % 2
                hidden(x, at(e + 1, 2, i))
                if not last:
                    evac_xe(b, at(e + 2, 2, i))
                evac_y(b, at(e, 2, i), at(16 * ((e - 1) // 2), 16, i) if e >= 3 or i is not None else None)

            evac_xe(0, 1)
            hidden(0, 1)
            evac_xe(1, 2)
            step(1, None)
            step(2, None)
            with dve.Fori(1, E // 2 - 1) as i:
                step(1, i)
                step(2, i)
            step(E - 1, None, last=True)
            evac_y(1, E, 16 * (E // 2 - 1))
            nov = dve.value_load(ovi[0:1, 0:1], min_val=0, max_val=NOV)
            with dve.If(nov > 0):
                with dve.Fori(0, nov) as i:
                    evac_xe(0, i + E + 1)
                    hidden(0, i + E + 1)
                    evac_y(0, i + E + 1, i * 16 + 16 * (E // 2))

            dve.wait_ge(s_ln2, 32)
            for j in range(NT):
                r = ROWS[j]
                md = modP if j < NP else modS
                x = x_tok[0:r, j, :]
                y = ring[0:r, j, 0:D]
                dve.wait_ge(f_a, j + 1)
                link(dve.scalar_tensor_tensor(y, ring[0:r, j, D:2 * D], wts[0:r, 1, j:j + 1], y, ALU.mult, ALU.add))
                link(dve.tensor_tensor(y, y, md[0:r, 3, :], ALU.mult))
                link(dve.scalar_tensor_tensor(x, x, ALPHA, y, ALU.mult, ALU.add))
                ln_stats(x, j, f_v)
                dve.wait_ge(f_l, j + 1)
                ln_finish(x, j, ln2)
                dve.tensor_tensor(x, x, ln2[0:r, 1, :], ALU.add).then_inc(f_o, 1)


_INS = ["x_prompt", "x_sample", "c_prompt", "c_sample", "state_gla", "cache_swa_k", "cache_swa_v",
        "ada_w", "ada_b", "w_in", "gla_a2_w", "gla_a2_b", "gla_norm_w", "swa_sinks", "w_o", "ln1_g", "ln1_b",
        "router_g_w", "router_g_b", "router_e_w", "router_e_b", "moe_w_gate", "moe_w_up", "moe_w_down",
        "ln2_g", "ln2_b"]
_OUTS = [(1, 512, 1024), (1, 32, 1024), (1, 1, 4, 64, 128), (1, 1, 128, 2, 64), (1, 1, 128, 2, 64),
         (1, 1, 4, 64, 128), (1, 1, 128, 2, 64), (1, 1, 128, 2, 64)]


def kernel(**inputs):
    import numpy as _np
    import concourse.bacc as _bacc
    from concourse import mybir as _mybir
    from concourse.bass_utils import run_bass_kernel_spmd as _run

    nc = _bacc.Bacc("TRN2", target_bir_lowering=False, num_devices=1)
    arrays, args = {}, []
    for name in _INS:
        a = _np.ascontiguousarray(inputs[name])
        arrays[f"in_{name}_dram"] = a
        args.append(nc.dram_tensor(f"in_{name}_dram", a.shape, _mybir.dt.from_np(a.dtype), kind="ExternalInput").ap())
    for i, shape in enumerate(_OUTS):
        args.append(nc.dram_tensor(f"out_{i}_dram", shape, _mybir.dt.float32, kind="ExternalOutput").ap())
    hymba_stream_step(nc, *args)
    r = _run(nc, [arrays], core_ids=[0])
    return tuple(r.results[0][f"out_{i}_dram"] for i in range(len(_OUTS)))
```

```python
import concourse.bass as bass
from concourse import mybir
from contextlib import ExitStack


def hymba_stream_step(nc, x_prompt, x_sample, c_prompt, c_sample, state_gla, cache_swa_k, cache_swa_v,
                      ada_w, ada_b, w_in, gla_a2_w, gla_a2_b, gla_norm_w, swa_sinks, w_o, ln1_g, ln1_b,
                      router_g_w, router_g_b, router_e_w, router_e_b, moe_w_gate, moe_w_up, moe_w_down,
                      ln2_g, ln2_b,
                      y_prompt, y_sample, state_prompt, k_prompt, v_prompt, state_sample, k_sample, v_sample):
    f32, i32 = mybir.dt.float32, mybir.dt.int32
    ALU = mybir.AluOpType
    ACT = mybir.ActivationFunctionType
    AX = mybir.AxisListType

    P = 128
    D = x_prompt.shape[2]
    KD = D // P
    LP, LS = x_prompt.shape[1], x_sample.shape[1]
    T = LP + LS
    NP = LP // P
    NT = NP + 1
    ROWS = [P] * NP + [LS]
    CH = 64
    NCH = LP // CH
    H, DK, DV = state_gla.shape[2:]
    HD = cache_swa_k.shape[4]
    NQ = swa_sinks.shape[1]
    WIN = cache_swa_k.shape[2]
    KW = WIN + P
    NG, NE = router_g_w.shape[2], router_e_w.shape[3]
    E = NG * NE
    FF = moe_w_gate.shape[4]
    NF = FF // P
    ALPHA = 2.0 ** 0.25
    EPS = 1e-5
    O_GQ, O_GK, O_GV, O_GR, O_GA = 0, H * DK, 2 * H * DK, 2 * H * DK + H * DV, 2 * H * DK + 2 * H * DV
    RANK = gla_a2_w.shape[1]
    O_SQ = O_GA + RANK
    O_SK = O_SQ + NQ * HD
    O_SV = O_SK + 2 * HD
    UC = 256

    PAIRS = 2 * T
    NOV = PAIRS // (P + 1)
    OVT = (T - 1) // P
    NBLK = E + NOV
    KSTEP = 1024
    EMPTY = 4096

    mod_d = nc.dram_tensor("mod_scratch", [2, 6 * D], f32).ap()
    h2_d = nc.dram_tensor("h2_scratch", [T, D], f32).ap()
    tbl_d = nc.dram_tensor("slot_table", [NBLK * P, 1], f32).ap()
    yb_d = nc.dram_tensor("expert_rows", [2 * KSTEP, D], f32).ap()

    def cols(w, c, n):
        return w[:, c:c + n].rearrange("(k p) n -> p k n", p=P)

    NR = 6
    units = []
    NA1 = 2 * D // UC
    NA = 6 * D // UC
    for u in range(NA1):
        units.append(("ada", u))
    WIN_UNITS = ["gq", "gk", "sq0", "sq1", "kv", "gv0", "gv1", "gr0", "gr1"]
    for w in WIN_UNITS:
        units.append((w, 0))
    for u in range(NA1, NA):
        units.append(("ada", u))
    for u in range(KD // 2):
        units.append(("wo", u))
    N0 = len(units)
    number = {u: n for n, u in enumerate(units)}

    ctx = ExitStack()
    with ctx:
        def sb(name, shape, dt=f32):
            return ctx.enter_context(nc.sbuf_tensor(name, shape, dt))

        def sem(name):
            return ctx.enter_context(nc.semaphore(name))

        bank = [ctx.enter_context(nc.psum_tensor(f"bank{i}", [P, 512], f32)) for i in range(8)]

        ring = sb("ring", [P, NR, KD * UC])
        x_tok = sb("x_tok", [P, NT, D])
        areaA = sb("areaA", [P, KD, T])
        hT, mixT = areaA, areaA
        areaB = sb("areaB", [P, 8 * T * 2])
        GW = 2 * T

        def area_b(i, n=1):
            return areaB[:, i * GW:(i + n) * GW]
        gq, gk, bc, eb, ebn, ed = (area_b(i).rearrange("p (a t) -> p a t", a=2) for i in range(6))
        sqT = area_b(6, 2).rearrange("p (a t) -> p a t", a=4)
        mixS = sqT
        areaC = sb("areaC", [P, 9 * D + 256])
        gv = areaC[:, 0:NT * H * DV].rearrange("p (j n) -> p j n", j=NT)
        grg = areaC[:, NT * 512:2 * NT * 512].rearrange("p (j n) -> p j n", j=NT)
        PT = areaC[:, 7 * D:9 * D].rearrange("p (h b q) -> p h b q", h=NQ, b=2)
        z = areaC[:, 5 * D:5 * D + NT * 256].rearrange("p (j n) -> p j n", j=NT)
        zt = areaC[:, 7 * D:7 * D + NT * 256].rearrange("p (j n) -> p j n", j=NT)
        xg = areaC[:, 0:2 * D].rearrange("p (a n) -> p a n", a=2)
        xTe = areaC[:, 2 * D:4 * D].rearrange("p (a k t) -> p a k t", a=2, k=KD)
        ye = areaC[:, 4 * D:6 * D].rearrange("p (a n) -> p a n", a=2)
        hid = areaC[:, 6 * D:6 * D + 2 * FF].rearrange("p (a n) -> p a n", a=2)
        sgl = areaC[:, 6 * D + 2 * FF:7 * D].rearrange("p (a n) -> p a n", a=2)
        hidT = areaC[:, 7 * D:7 * D + 2 * FF].rearrange("p (a k t) -> p a k t", a=2, k=NF)
        h2Tt = areaC[:, 0:D].rearrange("p (k t) -> p k t", k=KD)
        ytmp = areaC[:, D:2 * D]
        ln1 = areaC[:, 2 * D:4 * D].rearrange("p (a n) -> p a n", a=2)
        h2 = areaC[:, 5 * D:7 * D].rearrange("p (a n) -> p a n", a=2)
        biasH = sb("biasH", [P, NQ, KW])
        ln2 = biasH[:, :, :].rearrange("p h n -> p (h n)").rearrange("p (a n) -> p a n", a=2)
        skT = sb("skT", [P, LP + WIN + LS])
        gaT = sb("gaT", [RANK, T])
        svt = sb("svt", [P, NT + 1, 2 * HD])
        skt = sb("skt", [P, 2, 2 * HD])
        S = sb("S", [P, NCH + 3, 2, DV])
        gend = sb("gend", [P, 2, NCH + 1])
        osb = areaC[:, 5 * D:6 * D].rearrange("p (a n) -> p a n", a=2)
        gex = areaC[:, 6 * D:7 * D].rearrange("p (a n) -> p a n", a=2)
        kdT = areaC[:, 7 * D:7 * D + 4 * P].rearrange("p (a n) -> p a n", a=2)
        og = areaC[:, 7 * D + 4 * P:7 * D + 8 * P]
        At = areaC[:, 8 * D + 256:9 * D + 256].rearrange("p (a h t) -> p a h t", a=2, h=H)
        modrt = sb("modrt", [P, 2 * D])
        modst = modrt[0:2, :]
        Ssc = [t.rearrange("p (h n) -> p h n", h=NQ) for t in (areaC[:, 5 * D:7 * D], modrt[:, :])]
        modP = [area_b(5)[:, 0:D], area_b(0)[:, 0:D], area_b(2)[:, 0:D], modrt[:, 0:D]]
        modS = [area_b(1)[:, 0:D], area_b(3)[:, 0:D], area_b(4)[:, 0:D], modrt[:, D:2 * D]]
        adab = sb("adab", [NA, UC])
        crow = sb("crow", [2 * KD, P])
        cT = sb("cT", [P, 2 * KD])
        cx = sb("cx", [P, 2 * KD])
        csT = sb("csT", [P, 2 * KD])
        shsc = sb("shsc", [P, 4 * KD])
        wga = sb("wga", [P, KD, RANK])
        a2w = sb("a2w", [RANK, H * DK])
        a2b = sb("a2b", [P, H * DK])
        nw = sb("nw", [P, DV])
        sinks = sb("sinks", [P, NQ])
        rw = sb("rw", [P, KD, NG + E])
        rb = sb("rb", [P, NG + E])
        kc = sb("kc", [P, 2 * HD])
        ident = sb("ident", [P, P])
        tri = sb("tri", [P, P])
        tup = sb("tup", [P, P])
        before = sb("before", [P, P])
        ones = sb("ones", [P, P])
        dist = sb("dist", [P, KW])
        epst = sb("epst", [P, 1])
        iow = sb("iow", [P, 40])
        fl = sb("fl", [P, NBLK])
        small = sb("small", [P, 80])
        stat = sb("stat", [P, 2, 16])
        lg = sb("lg", [P, NT, NG + E])
        rt = modrt[:, 0:10 * NT * E].rearrange("p (i n) -> p i n", i=10)
        rs = sb("rs", [P, 12, NT])
        ov = sb("ov", [P, 6, E])
        wts = sb("wts", [P, 2, NT])
        posi = sb("posi", [P, 2, NT], i32)
        tokv = sb("tokv", [P, 2, NT])
        trow = sb("trow", [NBLK, P])
        srci = sb("srci", [P, NBLK], i32)
        dsti = sb("dsti", [P, NBLK], i32)
        ovi = sb("ovi", [1, 2 + NOV], i32)

        s_c, s_x, s_adab, s_misc, s_misc2 = sem("c_loaded"), sem("x_loaded"), sem("adab_loaded"), sem("misc_loaded"), sem("router_loaded")
        full = [sem(f"ring_full{i}") for i in range(NR)]
        pe_mod = sem("mod_units_done")
        wo_used, pe_g = sem("wo_units_used"), sem("gate_done")
        dv = sem("dve_chain")
        ac = sem("act_chain")
        pl = sem("pool_chain")
        pe_c, c_ex, cs_ready = sem("c_transposed"), sem("c_exp"), sem("cs_ready")
        pe_xt, xt_ev = sem("x_transposed"), sem("xT_evacuated")
        ada_ev, pe_sc, h_ready = sem("mod_evacuated"), sem("mod_transposed"), sem("h_ready")
        pe_t, t_ev = sem("proj_T_done"), sem("proj_T_evacuated")
        pe_z, z_ev, z_abs, z_ln, l_ready = sem("gate_psum"), sem("gate_evacuated"), sem("z_abs"), sem("z_ln"), sem("loga_ready")
        b_ready, e_ready, gla_ready = sem("b_ready"), sem("exps_ready"), sem("gla_operands_ready")
        pe_tok, tok_ev = sem("proj_tok_done"), sem("proj_tok_evacuated")
        pe_kd, kd_ev, pe_u, u_ev = sem("kd_transposed"), sem("kd_evacuated"), sem("u_done"), sem("state_updated")
        pe_a, a_ev, pe_o, o_ev, o_sq, og_ready, pe_og, mg_ev = (sem(n) for n in (
            "A_done", "A_masked", "o_done", "o_evacuated", "o_stats", "og_ready", "og_transposed", "mixT_gla"))
        pe_qk, s_ev, m_ready, p_exp, p_ready, pe_pt, pt_ev, pe_pv, pv_ev = (sem(n) for n in (
            "qk_done", "scores_ready", "max_ready", "probs_exp", "probs_ready", "P_transposed", "PT_evacuated",
            "pv_done", "mixT_swa"))
        s_mod, s_modb, s_ln1, s_ln2, s_kc = sem("mod_stored"), sem("mod_rows"), sem("ln1_rows"), sem("ln2_rows"), sem("cache_loaded")
        pe_y, y_ev, v_ready, v_ln, h2_ready, h2_st = (sem(n) for n in (
            "out_proj_done", "out_proj_read", "var_ready", "rstd_ready", "h2_ready", "h2_stored"))
        h2_st = [h2_st, sem("h2_stored1")]
        pe_ht, ht_ev, pe_rt, rt_ev = sem("h2_transposed"), sem("h2T_evacuated"), sem("logits_done"), sem("logits_read")
        r_ex0, r_ex, oh_ready, pe_rank, pos_ready = (sem(n) for n in (
            "router_diffs", "router_exps", "onehots_ready", "ranks_done", "slots_ready"))
        s_tbl0, s_scat, s_trow, pe_tbl, tbl_ready, ov_ready = (sem(n) for n in (
            "table_empty", "table_filled", "table_loaded", "table_transposed", "table_ready", "overflow_ready"))
        s_g = [sem("rows_gathered0"), sem("rows_gathered1")]
        s_sc = [sem("rows_scattered0"), sem("rows_scattered1")]
        pe_xe, xe_a, xe_d, pe_gu, sg_done, hid_done, pe_hT, hT_ev, pe_dn, y_a, y_d = (sem(n) for n in (
            "xe_transposed", "xe_evac_act", "xe_evac_dve", "gate_up_done", "silu_done", "hid_done",
            "hid_transposed", "hidT_evacuated", "down_done", "ye_act", "ye_dve"))
        o_w = sem("overflow_weights")
        s_fin = [sem(f"final_rows{j}") for j in range(NT)]
        f_a, f_v, f_l, f_o = sem("final_scaled"), sem("final_var"), sem("final_rstd"), sem("final_out")
        f_g = sem("final_gained")
        s_out, s_kv = sem("outputs_stored"), sem("caches_stored")
        moe_over = sem("moe_over")
        at_zero = sem("A_zeroed")
        s_gt1, s_gt2 = sem("gt1_rows"), sem("gt2_rows")

        block = ctx.enter_context(nc.Block())

        def tok(j):
            return slice(P * j, P * j + ROWS[j])

        def slot(n):
            return ring[:, n % NR, :]

        def unit_src(kind, u):
            if kind == "ada":
                return [(slice(0, KD * UC), cols(ada_w[0], u * UC, UC))]
            if kind == "wo":
                half = D * 2
                if u < KD // 4:
                    return [(None, w_o[0, 2 * P * u:2 * P * (u + 1), :].rearrange("(k p) n -> p k n", p=P))]
                i0 = 2 * (u - KD // 4)
                return [(g, w_o[0, H * DV + g * 4 * HD + i0 * HD:H * DV + g * 4 * HD + (i0 + 2) * HD, :]
                         .rearrange("(k p) n -> p k n", p=HD)) for g in range(2)]
            if kind in ("sq0", "sq1"):
                a = O_SQ + (0 if kind == "sq0" else 2 * HD)
                return [(2 * i + g, cols(w_in[0], a + g * 4 * HD + i * HD, HD)) for i in range(2) for g in range(2)]
            c = {"gq": O_GQ, "gk": O_GK, "kv": O_SK, "gv0": O_GV, "gv1": O_GV + UC, "gr0": O_GR, "gr1": O_GR + UC}[kind]
            return [(None, cols(w_in[0], c, UC))]

        NDMA = [len(unit_src(*u)) for u in units]

        def full_count(n):
            return sum(16 * NDMA[m] for m in range(n % NR, n + 1, NR))

        FULL0 = [0] * NR
        for n in range(N0):
            FULL0[n % NR] += 16 * NDMA[n]

        def expert_count(n):
            first = N0 + (n - N0) % NR
            return FULL0[n % NR] + 16 * ((n - first) // NR + 1)

        W3 = [moe_w_gate, moe_w_up, moe_w_down]

        def expert_src(e, r):
            w = W3[r][0].rearrange("g e a b -> (g e) a b")
            w = w[e] if isinstance(e, int) else w[bass.ds(e, 1)].rearrange("o a b -> (o a) b")
            return w.rearrange("(k p) n -> p k n", p=P)

        def slot_view(n, kd):
            return slot(n).rearrange("p (k n) -> p k n", k=kd)

        LAST = {"gq": (pe_t, 3), "gk": (pe_t, 5), "sq0": (pe_t, 7), "sq1": (pe_t, 9), "kv": (pe_tok, NT),
                "gv0": (pe_tok, 2 * NT), "gv1": (pe_tok, 3 * NT), "gr0": (pe_tok, 4 * NT), "gr1": (pe_tok, 5 * NT)}

        def freed(n):
            kind, u = units[n]
            if kind == "ada":
                return pe_mod, u + 1
            if kind == "wo":
                return (wo_used, u + 1) if u < KD // 2 - 1 else (pe_y, NT)
            return LAST[kind]

        ADA_AT = []
        for j in range(NT + 2):
            u = NA1 + 3 * j
            ADA_AT.append([[x for x in part if x < NA] for part in ([u, u + 1], [u + 2])])

        TOK = [(kind, j) for kind in ("kv", "gv0", "gv1", "gr0", "gr1") for j in range(NT)]
        places = [(j, f) for j in range(NT + 1) for f in range(4) if (j, f) not in ((0, 2), (0, 3), (NT, 0), (NT, 1))]
        TOK_AT = dict(zip(places, range(NT, len(TOK))))

        def at(base, step, i):
            return base if i is None else i * step + base

        @block.sync
        def _(sp):
            sp.dma_start(crow[0:KD, :], c_prompt[0, :].rearrange("(k p) -> k p", p=P)).then_inc(s_c, 16)
            sp.dma_start(crow[KD:2 * KD, :], c_sample[0, :].rearrange("(k p) -> k p", p=P)).then_inc(s_c, 16)
            sp.dma_start(adab[:, :], ada_b[0, :].rearrange("(u n) -> u n", n=UC)).then_inc(s_adab, 16)
            sp.dma_start(x_tok[:, 0:NP, :], x_prompt[0].rearrange("(j p) n -> p j n", p=P)).then_inc(s_x, 16)
            sp.dma_start(x_tok[0:LS, NP, :], x_sample[0]).then_inc(s_x, 16)
            for n, (kind, u) in enumerate(units):
                if n >= NR:
                    sp.wait_ge(*freed(n - NR))
                for g, src in unit_src(kind, u):
                    if kind == "wo":
                        v = slot_view(n, 2)
                        dst = v if g is None else v[g * HD:(g + 1) * HD, :, :]
                    elif kind in ("sq0", "sq1"):
                        dst = slot_view(n, KD)[:, :, g * HD:(g + 1) * HD]
                    else:
                        dst = slot_view(n, KD)
                    sp.dma_start(dst, src).then_inc(full[n % NR], 16)

            for e in range(2):
                for r in range(3):
                    n = N0 + 3 * e + r
                    sp.wait_ge(*freed(n - NR))
                    sp.dma_start(slot_view(n, KD if r < 2 else NF), expert_src(e, r)).then_inc(full[n % NR], 16)
            with sp.Fori(1, E // 2) as i:
                for b in range(2):
                    for r, done in enumerate((pe_g, pe_gu, pe_dn)):
                        n = N0 + 3 * b + r
                        sp.wait_ge(done, i * 2 + b - 1)
                        sp.dma_start(slot_view(n, KD if r < 2 else NF), expert_src(i * 2 + b, r)).then_inc(full[n % NR], 16)

            sp.wait_ge(moe_over, 1)
            sp.wait_ge(ov_ready, 1)
            nov = sp.value_load(ovi[0:1, 0:1], min_val=0, max_val=NOV)
            with sp.If(nov > 0):
                with sp.Fori(0, nov) as i:
                    e = sp.value_load(ovi[0:1, bass.ds(i + 1, 1)], min_val=0, max_val=E - 1)
                    sp.wait_ge(y_d, i + E)
                    for r in range(3):
                        sp.dma_start(ring[:, r, :].rearrange("p (k n) -> p k n", k=KD if r < 2 else NF),
                                     expert_src(e, r)).then_inc(o_w, 16)

            sp.wait_ge(moe_over, 2)
            rows3 = yb_d.rearrange("(k t) n -> t k n", k=2)
            for j in range(NT):
                sp.dma_start(ring[0:ROWS[j], j, :].rearrange("p (k n) -> p k n", k=2),
                             rows3[P * j:P * j + ROWS[j], :, :]).then_inc(s_fin[j], 16)
            for j in range(NT):
                sp.wait_ge(f_o, j + 1)
                dst = y_prompt[0, P * j:P * (j + 1), :] if j < NP else y_sample[0]
                sp.dma_start(dst, x_tok[0:ROWS[j], j, :]).then_inc(s_out, 16)
            sp.wait_ge(s_out, 16 * NT)

        NCONST = 20

        @block.gpsimd
        def _(pool):
            chain = [0]

            def link(ins):
                chain[0] += 1
                ins.then_inc(pl, 1)
                pool.wait_ge(pl, chain[0])

            link(pool.memset(epst[:, :], EPS))
            link(pool.memset(ident[:, :], 0.0))
            link(pool.affine_select(out=ident[:, :], in_=ident[:, :], compare_op=ALU.not_equal, fill=1.0, base=0,
                               pattern=[[-1, P]], channel_multiplier=1))
            link(pool.memset(ones[:, :], 1.0))
            link(pool.memset(tri[:, :], 1.0 / 16.0))
            link(pool.affine_select(out=tri[:, :], in_=tri[:, :], compare_op=ALU.is_ge, fill=0.0, base=0,
                                    pattern=[[1, P]], channel_multiplier=-1))
            link(pool.memset(tri[0:CH, CH:P], 0.0))
            link(pool.memset(tup[:, :], 1.0))
            link(pool.affine_select(out=tup[:, :], in_=tup[:, :], compare_op=ALU.is_ge, fill=0.0, base=-1,
                                    pattern=[[-1, P]], channel_multiplier=1))
            link(pool.memset(tup[CH:P, 0:CH], 0.0))
            link(pool.memset(before[:, :], 1.0))
            link(pool.affine_select(out=before[:, :], in_=before[:, :], compare_op=ALU.is_ge, fill=0.0, base=-1,
                               pattern=[[1, P]], channel_multiplier=-1))
            link(pool.iota(dist[:, :], pattern=[[1, KW]], base=-WIN, channel_multiplier=-1,
                      allow_small_or_imprecise_dtypes=True))
            link(pool.memset(z[:, NP, :], 0.0))
            link(pool.memset(S[:, 0, :, :], 0.0))
            link(pool.memset(lg[:, :, :], 0.0))
            link(pool.iota(ov[:, 0, :], pattern=[[P, E]], base=0, channel_multiplier=0,
                      allow_small_or_imprecise_dtypes=True))
            link(pool.iota(iow[:, 0:E], pattern=[[-1, E]], base=E, channel_multiplier=0,
                      allow_small_or_imprecise_dtypes=True))
            for k in range(2):
                link(pool.iota(tokv[:, k, :], pattern=[[P, NT]], base=k * KSTEP, channel_multiplier=1,
                          allow_small_or_imprecise_dtypes=True))
            link(pool.memset(fl[:, :], float(EMPTY)))
            pool.dma_start(tbl_d.rearrange("(p b) o -> p (b o)", p=P), fl[:, :]).then_inc(s_tbl0, 16)

            pool.wait_ge(tok_ev, NT)
            pool.dma_start(k_prompt[0, 0].rearrange("t h d -> t (h d)"), skt[:, 0, :]).then_inc(s_kv, 16)
            pool.dma_start(v_prompt[0, 0].rearrange("t h d -> t (h d)"), svt[:, NP - 1, :]).then_inc(s_kv, 16)
            for dst, old, new in ((k_sample, kc[LS:P, :], skt[0:LS, 1, :]), (v_sample, svt[LS:P, NP, :], svt[0:LS, NP + 1, :])):
                d = dst[0, 0].rearrange("t h d -> t (h d)")
                pool.dma_start(d[0:WIN - LS, :], old).then_inc(s_kv, 16)
                pool.dma_start(d[WIN - LS:WIN, :], new).then_inc(s_kv, 16)
            pool.wait_ge(pe_pv, NT)
            pool.memset(At[:, :, :, :], 0.0).then_inc(at_zero, 1)
            pool.wait_ge(s_ev, 4 * NT)
            pool.dma_start(ln2[:, 0, :], ln2_g.to_broadcast([P, D])).then_inc(s_ln2, 16)
            pool.dma_start(ln2[:, 1, :], ln2_b.to_broadcast([P, D])).then_inc(s_ln2, 16)
            pool.wait_ge(u_ev, NT)
            for dst, n in ((state_prompt, NCH), (state_sample, NCH + 2)):
                pool.dma_start(dst[0, 0].rearrange("(a h) k v -> (h k) a v", a=2), S[:, n, :, :]).then_inc(s_kv, 16)
            pool.wait_ge(s_kv, 16 * 8)
            def mod_rows(a, loaded):
                c = slice((a + 2) * D, (a + 3) * D)
                pool.dma_start(modP[a], mod_d[0:1, c].to_broadcast([P, D])).then_inc(loaded, 16)
                pool.dma_start(modS[a][0:LS, :], mod_d[1:2, c].to_broadcast([LS, D])).then_inc(loaded, 16)

            pool.wait_ge(ada_ev, NA1 * 2)
            pool.dma_start(mod_d[:, 2 * D:4 * D], modst[:, :]).then_inc(s_mod, 16)
            pool.wait_ge(s_mod, 16)
            mod_rows(0, s_gt1)
            pool.wait_ge(ada_ev, NA1 * 3)
            pool.dma_start(mod_d[:, 4 * D:6 * D], modst[:, :]).then_inc(s_mod, 16)
            pool.wait_ge(s_mod, 32)
            pool.wait_ge(pe_o, NT)
            mod_rows(1, s_modb)
            mod_rows(2, s_modb)
            pool.wait_ge(og_ready, NT)
            pool.dma_start(ln1[:, 0, :], ln1_g.to_broadcast([P, D])).then_inc(s_ln1, 16)
            pool.dma_start(ln1[:, 1, :], ln1_b.to_broadcast([P, D])).then_inc(s_ln1, 16)

            pool.wait_ge(pos_ready, 1)
            pool.wait_ge(s_tbl0, 16)
            for k in range(2):
                for j in range(NT):
                    pool.indirect_dma_start(
                        out=tbl_d[:, :], out_offset=bass.IndirectOffsetOnAxis(ap=posi[0:ROWS[j], k, j:j + 1], axis=0),
                        in_=tokv[0:ROWS[j], k, j:j + 1], in_offset=None,
                        bounds_check=NBLK * P - 1, oob_is_err=False).then_inc(s_scat, 16)
            pool.wait_ge(s_scat, 16 * 2 * NT)
            pool.dma_start(trow[:, :], tbl_d.rearrange("(b p) o -> b (p o)", p=P)).then_inc(s_trow, 16)
            pool.wait_ge(mg_ev, NT)
            pool.wait_ge(pe_rt, NT)
            pool.wait_ge(h2_st[0], 16 * ((NT + 1) // 2))
            pool.wait_ge(h2_st[1], 16 * (NT // 2))
            link(pool.memset(xg[:, :, :], 0.0))
            pool.wait_ge(tbl_ready, 1)

            def gather(b, a):
                pool.indirect_dma_start(
                    out=xg[:, a, :], out_offset=None, in_=h2_d[:, :],
                    in_offset=bass.IndirectOffsetOnAxis(ap=srci[:, b:b + 1], axis=0),
                    bounds_check=T - 1, oob_is_err=False).then_inc(s_g[a], 16)

            def scatter(b, a):
                pool.wait_ge(y_a, b + 1)
                pool.wait_ge(y_d, b + 1)
                pool.indirect_dma_start(
                    out=yb_d[:, :], out_offset=bass.IndirectOffsetOnAxis(ap=dsti[:, b:b + 1], axis=0),
                    in_=ye[:, a, :], in_offset=None,
                    bounds_check=2 * KSTEP - 1, oob_is_err=False).then_inc(s_sc[a], 16)

            gather(0, 0)
            gather(1, 1)
            pool.wait_ge(ov_ready, 1)
            mod_rows(3, s_gt2)
            for e in range(E + 2):
                if e + 2 < E:
                    pool.wait_ge(pe_xe, e + 1)
                    gather(e + 2, e % 2)
                if e >= 2:
                    scatter(e - 2, e % 2)
            pool.wait_ge(s_sc[0], 16 * (E // 2))
            pool.wait_ge(s_sc[1], 16 * (E // 2))
            pool.wait_ge(pe_dn, E)
            pool.engine_nop().then_inc(moe_over, 1)
            pool.wait_ge(ov_ready, 1)
            nov = pool.value_load(ovi[0:1, 0:1], min_val=0, max_val=NOV)
            for b in range(NOV):
                with pool.If(nov > b):
                    gather(E + b, 0)
                    scatter(E + b, 0)
                    pool.wait_ge(s_sc[0], 16 * (E // 2 + b + 1))
            pool.engine_nop().then_inc(moe_over, 1)
            for j in range(NT):
                x = x_tok[0:ROWS[j], j, :]
                pool.wait_ge(f_g, j + 1)
                pool.tensor_tensor(x, x, ln2[0:ROWS[j], 1, :], ALU.add).then_inc(f_o, 1)

        @block.scalar
        def _(act):
            chain = [0]

            def link(ins):
                chain[0] += 1
                ins.then_inc(ac, 1)
                act.wait_ge(ac, chain[0])

            act.dma_start(wga[:, :, :], cols(w_in[0], O_GA, RANK)).then_inc(s_misc, 16)
            act.dma_start(a2w[:, :], gla_a2_w[0]).then_inc(s_misc, 16)
            act.dma_start(a2b[:, :], gla_a2_b.to_broadcast([P, H * DK])).then_inc(s_misc, 16)
            act.dma_start(nw[:, :], gla_norm_w.to_broadcast([P, DV])).then_inc(s_misc, 16)
            act.dma_start(sinks[:, :], swa_sinks.to_broadcast([P, NQ])).then_inc(s_misc, 16)
            act.dma_start(kc[:, :], cache_swa_k[0, 0].rearrange("t h d -> t (h d)")).then_inc(s_kc, 16)
            act.dma_start(svt[:, NP, :], cache_swa_v[0, 0].rearrange("t h d -> t (h d)")).then_inc(s_misc, 16)
            act.dma_start(S[:, NCH + 1, :, :], state_gla[0, 0].rearrange("(a h) k v -> (h k) a v", a=2)).then_inc(s_misc, 16)
            act.dma_start(rw[:, :, 0:NG], cols(router_g_w[0], 0, NG)).then_inc(s_misc2, 16)
            for g in range(NG):
                act.dma_start(rw[:, :, NG + g * NE:NG + (g + 1) * NE], cols(router_e_w[0, g], 0, NE)).then_inc(s_misc2, 16)
            act.dma_start(rb[:, 0:NG], router_g_b.to_broadcast([P, NG])).then_inc(s_misc2, 16)
            act.dma_start(rb[:, NG:NG + E], router_e_b.rearrange("o g e -> o (g e)").to_broadcast([P, E])).then_inc(s_misc2, 16)

            act.wait_ge(pl, NCONST)
            act.wait_ge(pe_c, 1)
            act.activation(cx[:, :], bank[0][:, 0:2 * KD], ACT.Exp, scale=-1.0).then_inc(c_ex, 1)
            for q in range(2 * NT):
                j, half = q // 2, q % 2
                act.wait_ge(pe_xt, q + 1)
                r = ROWS[j]
                act.activation(hT[:, 4 * half:4 * half + 4, tok(j)],
                               bank[1 + q % 2][:, 0:4 * r].rearrange("p (k t) -> p k t", k=4), ACT.Copy).then_inc(xt_ev, 1)
            dests = [gaT] + [gq[:, 0], gq[:, 1], gk[:, 0], gk[:, 1]] + [sqT[:, i] for i in range(4)] + [skT]

            def evac_t(tb):
                act.wait_ge(pe_t, tb + 1)
                d = dests[tb]
                m = RANK if tb == 0 else P
                s = DK ** -0.5 if tb in (1, 2) else 1.0
                off = LP + WIN if tb == 9 else LP
                act.activation(d[0:m, 0:LP], bank[1 + tb % 2][0:m, 0:LP], ACT.Copy, scale=s).then_inc(t_ev, 1)
                act.activation(d[0:m, off:off + LS], bank[5 + tb % 2][0:m, 0:LS], ACT.Copy, scale=s).then_inc(t_ev, 1)

            for tb in range(4):
                evac_t(tb)
            act.wait_ge(z_abs, 1)
            link(act.activation(zt, zt, ACT.Exp, scale=-1.0))
            act.activation(zt, zt, ACT.Ln, bias=1.0).then_inc(z_ln, 1)
            for tb in range(4, 7):
                evac_t(tb)
            act.wait_ge(b_ready, 2)
            act.activation(eb, bc, ACT.Exp).then_inc(e_ready, 1)
            act.activation(ebn, bc, ACT.Exp, scale=-1.0).then_inc(e_ready, 1)
            act.activation(ed, ed, ACT.Exp).then_inc(e_ready, 1)
            for tb in range(7, 10):
                evac_t(tb)
            act.wait_ge(pe_t, 11)
            act.activation(skT[:, LP:LP + WIN], bank[1][:, 0:WIN], ACT.Copy).then_inc(t_ev, 1)

            def win(j):
                return (P, KW) if j == 0 else (0, KW) if j < NP else (0, WIN + LS)

            def probs(j):
                r = ROWS[j]
                lo, hi = win(j)
                act.wait_ge(m_ready, j + 1)
                c = 16 + 32 * (j % 2)
                for h in range(NQ):
                    sc = Ssc[j % 2][0:r, h, 0:hi - lo]
                    act.activation(sc, sc, ACT.Exp, bias=small[0:r, c + 8 + h:c + 9 + h],
                                   accum_out=small[0:r, c + 16 + h:c + 17 + h]).then_inc(p_exp, 1)
                act.activation(small[0:r, c + 24:c + 32], small[0:r, c + 24:c + 32], ACT.Exp).then_inc(p_exp, 1)

            def evac_pt(j):
                r = ROWS[j]
                nb = 1 if j == 0 else 2
                for f in range(4):
                    act.wait_ge(pe_pt, 4 * j + f + 1)
                    if f == 0:
                        act.wait_ge(pe_pv, j)
                    src = bank[5 + f % 2][:, 0:2 * nb * r].rearrange("p (h b q) -> p h b q", h=2, b=nb)
                    if j < NP:
                        act.activation(PT[:, 2 * f:2 * f + 2, 0:nb, 0:r], src, ACT.Copy).then_inc(pt_ev, 1)
                    else:
                        link(act.activation(PT[:, 2 * f:2 * f + 2, 0, 0:r], src[:, :, 0, :], ACT.Copy))
                        act.activation(PT[0:LS, 2 * f:2 * f + 2, 1, 0:r], src[0:LS, :, 1, :], ACT.Copy).then_inc(pt_ev, 1)

            def evac_pv(j):
                act.wait_ge(pe_pv, j + 1)
                act.activation(mixS[:, :, tok(j)], bank[7][:, 0:4 * ROWS[j]].rearrange("p (k t) -> p k t", k=4),
                               ACT.Copy).then_inc(pv_ev, 1)

            for j in range(NT + 1):
                if j >= 1:
                    evac_pt(j - 1)
                if j < NT:
                    probs(j)
                if j >= 1:
                    evac_pv(j - 1)

            for j in range(NT):
                act.wait_ge(pe_kd, j + 1)
                if j >= 2:
                    act.wait_ge(pe_u, j - 1)
                act.activation(kdT[0:ROWS[j], j % 2, :], bank[0][0:ROWS[j], 0:2 * P], ACT.Copy).then_inc(kd_ev, 1)

            def mix_stats(j):
                r = ROWS[j]
                act.wait_ge(pe_o, j + 1)
                if j >= 2:
                    act.wait_ge(og_ready, j - 1)
                o4 = osb[0:r, j % 2, :].rearrange("p (a b v) -> p a b v", a=2, b=2)
                for par in range(2):
                    act.activation(o4[:, :, par, :], bank[3 + par][0:r, 0:2 * DV].rearrange("p (a v) -> p a v", a=2),
                                   ACT.Copy).then_inc(o_ev, 1)
                act.wait_ge(o_ev, 2 * (j + 1))
                for h in range(H):
                    link(act.activation(gex[0:r, j % 2, h * DV:(h + 1) * DV], osb[0:r, j % 2, h * DV:(h + 1) * DV], ACT.Square,
                                        accum_out=small[0:r, 8 * (j % 2) + h:8 * (j % 2) + h + 1]))
                ss = small[0:r, 8 * (j % 2):8 * (j % 2) + H]
                link(act.activation(ss, ss, ACT.Ln, scale=1.0 / DV, bias=epst[0:r, 0:1]))
                link(act.activation(ss, ss, ACT.Exp, scale=-0.5))
                act.wait_ge(tok_ev, 25)
                act.activation(gex[0:r, j % 2, :], grg[0:r, j, :], ACT.Exp, scale=-1.0).then_inc(o_sq, 1)

            def evac_og(j):
                act.wait_ge(pe_og, j + 1)
                act.activation(mixT[:, 0:4, tok(j)], bank[5][:, 0:4 * ROWS[j]].rearrange("p (k t) -> p k t", k=4),
                               ACT.Copy).then_inc(mg_ev, 1)

            for j in range(NT + 2):
                if 1 <= j <= NT:
                    mix_stats(j - 1)
                if j >= 2:
                    evac_og(j - 2)

            def rstd(j):
                act.wait_ge(v_ready, j + 1)
                v = stat[0:ROWS[j], j % 2, 13:14]
                link(act.activation(v, v, ACT.Ln, bias=epst[0:ROWS[j], 0:1]))
                act.activation(v, v, ACT.Exp, scale=-0.5).then_inc(v_ln, 1)

            def evac_h2(j):
                r = ROWS[j]
                act.wait_ge(h2_ready, j + 1)
                act.dma_start(h2_d[P * j:P * j + r, :], h2[0:r, j % 2, :]).then_inc(h2_st[j % 2], 16)
                for half in range(2):
                    act.wait_ge(pe_ht, 2 * j + half + 1)
                    if half == 0:
                        act.wait_ge(pe_rt, j)
                    act.activation(h2Tt[:, 4 * half:4 * half + 4, 0:r],
                                   bank[5 + half][:, 0:4 * r].rearrange("p (k t) -> p k t", k=4), ACT.Copy).then_inc(ht_ev, 1)

            for j in range(NT + 1):
                if j < NT:
                    rstd(j)
                if j >= 1:
                    evac_h2(j - 1)
            act.wait_ge(r_ex0, 1)
            link(act.activation(rt[:, 0, 0:NT * NG], rt[:, 0, 0:NT * NG], ACT.Exp))
            act.activation(rs[:, 5, :], rs[:, 5, :], ACT.Exp).then_inc(r_ex, 1)

            def evac_xe(a, w):
                act.wait_ge(pe_xe, w)
                act.activation(xTe[:, a, 0:4, :], bank[0][:, :].rearrange("p (k t) -> p k t", k=4), ACT.Copy).then_inc(xe_a, 1)

            def silu(a, w):
                act.wait_ge(pe_gu, w)
                act.activation(sgl[:, a, :], bank[2 + a][:, 0:FF], ACT.Silu).then_inc(sg_done, 1)

            def evac_hT(a, w):
                act.wait_ge(pe_hT, w)
                act.activation(hidT[:, a, :, :], bank[4][:, 0:FF].rearrange("p (k t) -> p k t", k=NF), ACT.Copy).then_inc(hT_ev, 1)

            def evac_y(a, w, free):
                act.wait_ge(pe_dn, w)
                if free is not None:
                    act.wait_ge(s_sc[a], free)
                act.activation(ye[:, a, 0:512], bank[5][:, :], ACT.Copy).then_inc(y_a, 1)

            def step(e, i, last=False):
                a, b = e % 2, (e - 1) % 2
                silu(a, at(e + 1, 2, i))
                evac_hT(b, at(e, 2, i))
                if not last:
                    evac_xe(b, at(e + 2, 2, i))
                evac_y(b, at(e, 2, i), at(16 * ((e - 1) // 2), 16, i) if e >= 3 or i is not None else None)

            act.wait_ge(tbl_ready, 1)
            evac_xe(0, 1)
            silu(0, 1)
            evac_xe(1, 2)
            step(1, None)
            step(2, None)
            with act.Fori(1, E // 2 - 1) as i:
                step(1, i)
                step(2, i)
            step(E - 1, None, last=True)
            evac_hT(1, E)
            evac_y(1, E, 16 * (E // 2 - 1))
            act.wait_ge(ov_ready, 1)
            nov = act.value_load(ovi[0:1, 0:1], min_val=0, max_val=NOV)
            with act.If(nov > 0):
                with act.Fori(0, nov) as i:
                    evac_xe(0, i + E + 1)
                    silu(0, i + E + 1)
                    evac_hT(0, i + E + 1)
                    evac_y(0, i + E + 1, i * 16 + 16 * (E // 2))

            def scale_first(j):
                r = ROWS[j]
                act.wait_ge(s_fin[j], 16)
                act.activation(ring[0:r, j, 0:D], ring[0:r, j, 0:D], ACT.Copy, scale=wts[0:r, 0, j:j + 1]).then_inc(f_a, 1)

            def normalise(j):
                r = ROWS[j]
                act.wait_ge(f_v, j + 1)
                mean, v = stat[0:r, j % 2, 12:13], stat[0:r, j % 2, 13:14]
                link(act.activation(v, v, ACT.Ln, bias=epst[0:r, 0:1]))
                link(act.activation(v, v, ACT.Exp, scale=-0.5))
                link(act.activation(mean, mean, ACT.Copy, scale=v))
                link(act.mul(mean, mean, -1.0))
                act.activation(x_tok[0:r, j, :], x_tok[0:r, j, :], ACT.Identity, scale=v, bias=mean).then_inc(f_l, 1)

            scale_first(0)
            scale_first(1)
            for j in range(NT):
                if j + 2 < NT:
                    scale_first(j + 2)
                normalise(j)

        @block.tensor
        def _(pe):
            pe.wait_ge(pl, NCONST)
            pe.wait_ge(s_c, 32)
            pe.transpose(bank[0][:, 0:2 * KD], crow[:, :], ident[0:2 * KD, 0:2 * KD]).then_inc(pe_c, 1)
            pe.wait_ge(s_x, 32)
            for q in range(2 * NT):
                j, half = q // 2, q % 2
                r = ROWS[j]
                if q >= 2:
                    pe.wait_ge(xt_ev, q - 1)
                for k in range(4):
                    kk = 4 * half + k
                    mm = pe.transpose(bank[1 + q % 2][:, k * r:(k + 1) * r], x_tok[0:r, j, kk * P:(kk + 1) * P], ident[0:r, 0:r])
                mm.then_inc(pe_xt, 1)
            pe.wait_ge(cs_ready, 1)
            pe.wait_ge(s_adab, 16)
            cs3 = csT[:, :].rearrange("p (b k) -> p b k", b=2)

            def wait_unit(n):
                pe.wait_ge(full[n % NR], full_count(n))

            def ada(u, bk):
                n = number[("ada", u)]
                wait_unit(n)
                w = slot_view(n, KD)
                pe.matmul(bank[bk][0:2, 0:UC], ident[0:NA, u:u + 1].to_broadcast([NA, 2]), adab[:, :], start=True, stop=False)
                for k in range(KD):
                    mm = pe.matmul(bank[bk][0:2, 0:UC], cs3[:, :, k], w[:, k, :], start=False, stop=(k == KD - 1))
                mm.then_inc(pe_mod, 1)

            for u in range(NA1):
                if u >= 2:
                    pe.wait_ge(ada_ev, u - 1)
                ada(u, 3 + u % 2)
            pe.wait_ge(ada_ev, NA1)
            for i in range(2 * KD):
                mm = pe.transpose(bank[0][:, 32 + 2 * i:34 + 2 * i], modst[:, i * P:(i + 1) * P], ident[0:2, 0:2])
            mm.then_inc(pe_sc, 1)

            def proj_t(tb, lhs):
                m = RANK if tb == 0 else P
                if tb >= 2:
                    pe.wait_ge(t_ev, 2 * (tb - 1))
                for k in range(KD):
                    pe.matmul(bank[1 + tb % 2][0:m, 0:LP], lhs(k), hT[:, k, 0:LP], start=(k == 0), stop=(k == KD - 1))
                for k in range(KD):
                    mm = pe.matmul(bank[5 + tb % 2][0:m, 0:LS], lhs(k), hT[:, k, LP:T], start=(k == 0), stop=(k == KD - 1))
                return mm

            pe.wait_ge(s_misc, 16 * 7)
            pe.wait_ge(h_ready, 2 * KD)
            proj_t(0, lambda k: wga[:, k, :]).then_inc(pe_t, 1)
            tb = 1
            for kind in ("gq", "gk"):
                n = number[(kind, 0)]
                wait_unit(n)
                v = slot_view(n, KD)
                for b in range(2):
                    proj_t(tb, lambda k: v[:, k, b * P:(b + 1) * P]).then_inc(pe_t, 1)
                    tb += 1
                if kind == "gq":
                    pe.wait_ge(t_ev, 2)
                    for j in range(NT):
                        if j >= 2:
                            pe.wait_ge(z_ev, j - 1)
                        pe.matmul(bank[7 if j % 2 == 0 else 0][0:ROWS[j], 0:H * DK], gaT[:, tok(j)], a2w[:, :],
                                  start=True, stop=True).then_inc(pe_z, 1)
            pe.wait_ge(l_ready, 1)
            for j in range(NT):
                r = ROWS[j]
                pe.wait_ge(z_ev, 5 + j - 1 if j >= 1 else 5)
                for half in range(2):
                    mm = pe.matmul(bank[7 if j % 2 == 0 else 0][:, half * r:(half + 1) * r], z[0:r, j, half * P:(half + 1) * P],
                                   tri[0:r, 0:r], start=True, stop=True)
                mm.then_inc(pe_z, 1)
            for kind in ("sq0", "sq1"):
                n = number[(kind, 0)]
                wait_unit(n)
                v = slot_view(n, KD)
                for b in range(2):
                    proj_t(tb, lambda k: v[:, k, b * P:(b + 1) * P]).then_inc(pe_t, 1)
                    tb += 1
            n = number[("kv", 0)]
            wait_unit(n)
            v = slot_view(n, KD)
            proj_t(tb, lambda k: v[:, k, 0:2 * HD]).then_inc(pe_t, 1)
            pe.wait_ge(s_kc, 16)
            pe.wait_ge(t_ev, 18)
            pe.transpose(bank[1][:, 0:WIN], kc[:, :], ident[:, :]).then_inc(pe_t, 1)

            def proj_tok(m):
                kind, j = TOK[m]
                n = number[(kind, 0)]
                wait_unit(n)
                v = slot_view(n, KD)
                r = ROWS[j]
                c0 = 0 if kind != "kv" or j >= NP - 1 else 2 * HD
                if m >= 2:
                    pe.wait_ge(tok_ev, m - 1)
                for k in range(KD):
                    mm = pe.matmul(bank[3 + m % 2][0:r, 0:UC - c0], hT[:, k, tok(j)], v[:, k, c0:UC],
                                   start=(k == 0), stop=(k == KD - 1))
                mm.then_inc(pe_tok, 1)

            def fill(j, f):
                if (j, f) in TOK_AT:
                    proj_tok(TOK_AT[(j, f)])

            for m in range(NT):
                proj_tok(m)

            def qk(j, g):
                r = ROWS[j]
                k0, k1 = (0, P) if j == 0 else (P * (j - 1), P * (j + 1)) if j < NP else (LP, LP + WIN + LS)
                n = k1 - k0
                for par in range(2):
                    f = 4 * j + 2 * g + par
                    if f >= 2:
                        pe.wait_ge(s_ev, f - 1)
                    q0 = par * HD
                    for a in range(2):
                        mm = pe.matmul(bank[1 + par][0:r, a * KW:a * KW + n], sqT[q0:q0 + HD, 2 * g + a, tok(j)],
                                       skT[q0:q0 + HD, k0:k1], start=True, stop=True)
                    mm.then_inc(pe_qk, 1)

            def key_blocks(j):
                return [(0, P)] if j == 0 else [(0, P), (P, P)] if j < NP else [(0, P), (P, LS)]

            def pt(j, fs):
                r = ROWS[j]
                pe.wait_ge(p_ready, j + 1)
                nb = len(key_blocks(j))
                for f in fs:
                    if 4 * j + f >= 2:
                        pe.wait_ge(pt_ev, 4 * j + f - 1)
                    for h in range(2):
                        for b, (kb, kn) in enumerate(key_blocks(j)):
                            c = (h * nb + b) * r
                            mm = pe.transpose(bank[5 + f % 2][0:kn, c:c + r], Ssc[j % 2][0:r, 2 * f + h, kb:kb + kn], ident[0:r, 0:r])
                    mm.then_inc(pe_pt, 1)

            def pv(j):
                r = ROWS[j]
                pe.wait_ge(pt_ev, 4 * (j + 1))
                if j >= 1:
                    pe.wait_ge(pv_ev, j)
                tiles = [0] if j == 0 else [j - 1, j] if j < NP else [NP, NP + 1]
                for i in range(4):
                    for g in range(2):
                        for b, (kb, kn) in enumerate(key_blocks(j)):
                            mm = pe.matmul(bank[7][g * HD:(g + 1) * HD, i * r:(i + 1) * r], svt[0:kn, tiles[b], g * HD:(g + 1) * HD],
                                           PT[0:kn, 4 * g + i, b, 0:r], start=(b == 0), stop=(b == len(tiles) - 1))
                mm.then_inc(pe_pv, 1)

            pe.wait_ge(t_ev, 21)
            for j in range(NT + 1):
                if j < NT:
                    qk(j, 0)
                fill(j, 0)
                if j < NT:
                    qk(j, 1)
                fill(j, 1)
                if j >= 1:
                    pt(j - 1, (0, 1))
                fill(j, 2)
                if j >= 1:
                    pt(j - 1, (2, 3))
                fill(j, 3)
                if j >= 1:
                    pv(j - 1)

            pe.wait_ge(gla_ready, 1)
            pe.wait_ge(pv_ev, NT)
            for j in range(NT + 1):
                if j < NT:
                    r = ROWS[j]
                    pe.wait_ge(kd_ev, j) if j >= 1 else pe.wait_ge(z_ev, 10)
                    for half in range(2):
                        mm = pe.transpose(bank[0][0:r, half * P:(half + 1) * P], ed[:, half, tok(j)], ident[:, :])
                    mm.then_inc(pe_kd, 1)
                if j >= 1:
                    i = j - 1
                    pe.wait_ge(kd_ev, i + 1)
                    pe.wait_ge(tok_ev, 15)
                    if i >= 1:
                        pe.wait_ge(u_ev, i)
                    for c in range(2 if i < NP else 1):
                        r0 = c * CH
                        r1 = r0 + min(CH, ROWS[i])
                        for h in range(H):
                            mm = pe.matmul(bank[6 + c][(h % 2) * DK:(h % 2 + 1) * DK, (h // 2) * DV:(h // 2 + 1) * DV],
                                           kdT[r0:r1, i % 2, h * DK:(h + 1) * DK], gv[r0:r1, i, h * DV:(h + 1) * DV],
                                           start=True, stop=True)
                    mm.then_inc(pe_u, 1)

            def ada_rest(us):
                for u in us:
                    if u >= NA1 + 2:
                        pe.wait_ge(ada_ev, u - 1)
                    ada(u, 6 * (u % 2))

            def gla_scores(j):
                r = ROWS[j]
                if j >= 1:
                    pe.wait_ge(a_ev, j)
                for par in range(2):
                    q0 = par * DK
                    for a in range(2):
                        for up in range(2):
                            ks, qs = (ebn, eb) if up == 0 else (bc, gq)
                            mm = pe.matmul(bank[1 + par][0:r, (2 * up + a) * P:(2 * up + a) * P + r],
                                           ks[q0:q0 + DK, a, tok(j)], qs[q0:q0 + DK, a, tok(j)], start=True, stop=True)
                mm.then_inc(pe_a, 1)

            def gla_out(j):
                r = ROWS[j]
                pe.wait_ge(a_ev, j + 1)
                pe.wait_ge(u_ev, j + 1)
                if j >= 1:
                    pe.wait_ge(o_sq, j)
                else:
                    pe.wait_ge(tok_ev, 25)
                for par in range(2):
                    for a in range(2):
                        h = 2 * a + par
                        out = bank[3 + par][:, a * DV:(a + 1) * DV]
                        pe.matmul(out[0:r, :], At[0:r, j % 2, h, 0:r], gv[0:r, j, h * DV:(h + 1) * DV], start=True, stop=False)
                        for c in range(2 if j < NP else 1):
                            n = 2 * j + c if j < NP else NCH + 1
                            c0, cn = c * CH, min(CH, r)
                            mm = pe.matmul(out[c0:c0 + cn, :], eb[par * DK:(par + 1) * DK, a, P * j + c0:P * j + c0 + cn],
                                           S[par * DK:(par + 1) * DK, n, a, :], start=False, stop=True)
                mm.then_inc(pe_o, 1)

            def gla_turn(j):
                r = ROWS[j]
                pe.wait_ge(og_ready, j + 1)
                if j >= 1:
                    pe.wait_ge(mg_ev, j)
                for k in range(4):
                    mm = pe.transpose(bank[5][:, k * r:(k + 1) * r], og[0:r, k * P:(k + 1) * P], ident[0:r, 0:r])
                mm.then_inc(pe_og, 1)

            pe.wait_ge(kd_ev, NT)
            pe.wait_ge(u_ev, NT)
            for j in range(NT + 2):
                if j < NT:
                    gla_scores(j)
                ada_rest(ADA_AT[j][0])
                if 1 <= j <= NT:
                    gla_out(j - 1)
                ada_rest(ADA_AT[j][1])
                if j >= 2:
                    gla_turn(j - 2)

            def out_proj(j):
                r = ROWS[j]
                if j >= 2:
                    pe.wait_ge(y_ev, 2 * (j - 1))
                for u in range(KD // 2):
                    n = number[("wo", u)]
                    wait_unit(n)
                    v = slot_view(n, 2)
                    for kk in range(2):
                        k = 2 * u + kk
                        for half in range(2):
                            mix = mixT[:, k, tok(j)] if k < H else mixS[:, k - H, tok(j)]
                            mm = pe.matmul(bank[1 + 2 * (j % 2) + half][0:r, :], mix, v[:, kk, half * 512:(half + 1) * 512],
                                           start=(k == 0), stop=(k == KD - 1))
                    if j == NT - 1 and u < KD // 2 - 1:
                        mm.then_inc(wo_used, 1)
                mm.then_inc(pe_y, 1)

            def route(j):
                r = ROWS[j]
                pe.wait_ge(h2_ready, j + 1)
                for half in range(2):
                    if j >= 1:
                        pe.wait_ge(ht_ev, 2 * j)
                    for k in range(4):
                        kk = 4 * half + k
                        mm = pe.transpose(bank[5 + half][:, k * r:(k + 1) * r], h2[0:r, j % 2, kk * P:(kk + 1) * P], ident[0:r, 0:r])
                    mm.then_inc(pe_ht, 1)
                pe.wait_ge(ht_ev, 2 * (j + 1))
                if j >= 1:
                    pe.wait_ge(rt_ev, j)
                for k in range(KD):
                    mm = pe.matmul(bank[7][0:r, 0:NG + E], h2Tt[:, k, 0:r], rw[:, k, :], start=(k == 0), stop=(k == KD - 1))
                mm.then_inc(pe_rt, 1)

            pe.wait_ge(mg_ev, NT)
            pe.wait_ge(pv_ev, NT)
            pe.wait_ge(s_misc2, 16 * (NG + 3))
            for j in range(NT + 2):
                if j < NT:
                    out_proj(j)
                if j >= 2:
                    route(j - 2)

            pe.wait_ge(oh_ready, 1)
            M = rt[:, 3, :].rearrange("p (j e) -> p j e", j=NT)
            for j in range(NT):
                for i in range(j + 1):
                    lhs = before if i == j else ones
                    mm = pe.matmul(bank[0][:, j * E:(j + 1) * E], lhs[0:ROWS[i], :], M[0:ROWS[i], i, :], start=(i == 0), stop=(i == j))
            for i in range(NT):
                mm = pe.matmul(bank[0][:, NT * E:(NT + 1) * E], ones[0:ROWS[i], :], M[0:ROWS[i], i, :], start=(i == 0), stop=(i == NT - 1))
            mm.then_inc(pe_rank, 1)
            pe.wait_ge(s_trow, 16)
            pe.transpose(bank[7][:, 0:NBLK], trow[:, :], ident[0:NBLK, 0:NBLK]).then_inc(pe_tbl, 1)

            def turn_x(a, gw):
                pe.wait_ge(s_g[a], gw)
                for k in range(KD):
                    mm = pe.transpose(bank[k // 4][:, (k % 4) * P:(k % 4 + 1) * P], xg[:, a, k * P:(k + 1) * P], ident[:, :])
                mm.then_inc(pe_xe, 1)

            def gate_up(a, wg, wu):
                for out, w, done in ((0, wg, pe_g), (FF, wu, pe_gu)):
                    for k in range(KD):
                        mm = pe.matmul(bank[2 + a][:, out:out + FF], xTe[:, a, k, :], w[:, k, :], start=(k == 0), stop=(k == KD - 1))
                    mm.then_inc(done, 1)

            def turn_h(a):
                for k in range(NF):
                    mm = pe.transpose(bank[4][:, k * P:(k + 1) * P], hid[:, a, k * P:(k + 1) * P], ident[:, :])
                mm.then_inc(pe_hT, 1)

            def down(a, w):
                for k in range(NF):
                    for half in range(2):
                        mm = pe.matmul(bank[5 + half][:, :], hidT[:, a, k, :], w[:, k, half * 512:(half + 1) * 512],
                                       start=(k == 0), stop=(k == NF - 1))
                return mm

            def expert_up(e, i):
                n = N0 + 3 * e
                pe.wait_ge(xe_a, at(e + 1, 2, i))
                pe.wait_ge(xe_d, at(e + 1, 2, i))
                if e >= 2 or i is not None:
                    pe.wait_ge(hid_done, at(e - 1, 2, i))
                pe.wait_ge(full[n % NR], at(expert_count(n), 16, i))
                pe.wait_ge(full[(n + 1) % NR], at(expert_count(n + 1), 16, i))
                gate_up(e % 2, slot_view(n, KD), slot_view(n + 1, KD))

            def expert_turn(e, i):
                pe.wait_ge(hid_done, at(e + 1, 2, i))
                if e >= 1:
                    pe.wait_ge(hT_ev, at(e, 2, i))
                turn_h(e % 2)

            def rows_turn(e, i):
                pe.wait_ge(xe_a, at(e, 2, i))
                pe.wait_ge(xe_d, at(e, 2, i))
                turn_x(e % 2, at(16 * (e // 2 + 1), 16, i))

            def expert_down(e, i):
                n = N0 + 3 * e + 2
                pe.wait_ge(hT_ev, at(e + 1, 2, i))
                if e >= 1 or i is not None:
                    pe.wait_ge(y_a, at(e, 2, i))
                    pe.wait_ge(y_d, at(e, 2, i))
                pe.wait_ge(full[n % NR], at(expert_count(n), 16, i))
                down(e % 2, slot_view(n, NF)).then_inc(pe_dn, 1)

            def step(e, i):
                expert_up(e, i)
                expert_turn(e - 1, i)
                rows_turn(e + 1, i)
                expert_down(e - 1, i)

            pe.wait_ge(tbl_ready, 1)
            turn_x(0, 16)
            expert_up(0, None)
            rows_turn(1, None)
            step(1, None)
            step(2, None)
            with pe.Fori(1, E // 2 - 1) as i:
                step(1, i)
                step(2, i)
            expert_up(E - 1, None)
            expert_turn(E - 2, None)
            expert_down(E - 2, None)
            expert_turn(E - 1, None)
            expert_down(E - 1, None)
            pe.wait_ge(ov_ready, 1)
            nov = pe.value_load(ovi[0:1, 0:1], min_val=0, max_val=NOV)
            with pe.If(nov > 0):
                with pe.Fori(0, nov) as i:
                    turn_x(0, i * 16 + 16 * (E // 2) + 16)
                    pe.wait_ge(xe_a, i + E + 1)
                    pe.wait_ge(xe_d, i + E + 1)
                    pe.wait_ge(o_w, i * 48 + 48)
                    gate_up(0, ring[:, 0, :].rearrange("p (k n) -> p k n", k=KD), ring[:, 1, :].rearrange("p (k n) -> p k n", k=KD))
                    pe.wait_ge(hid_done, i + E + 1)
                    turn_h(0)
                    pe.wait_ge(hT_ev, i + E + 1)
                    down(0, ring[:, 2, :].rearrange("p (k n) -> p k n", k=NF)).then_inc(pe_dn, 1)

        @block.vector
        def _(dve):
            chain = [0]

            def link(ins):
                chain[0] += 1
                ins.then_inc(dv, 1)
                dve.wait_ge(dv, chain[0])

            def bcast(ap, shape):
                return ap.broadcast_to(shape)

            dve.wait_ge(pl, NCONST)
            link(dve.scalar_tensor_tensor(dist[:, :], dist[:, :], -1.0, dist[:, :], ALU.mult, ALU.max))
            link(dve.memset(dist[0:CH, WIN + CH:KW], 1e32))
            link(dve.memset(dist[CH:P, 0:CH], 1e32))
            for h in range(NQ):
                dve.tensor_scalar(biasH[:, h, :], dist[:, :], -(2.0 ** (-(8.0 / NQ) * (h + 1))), None, ALU.mult)
            dve.wait_ge(c_ex, 1)
            link(dve.tensor_scalar(cx[:, :], cx[:, :], 1.0, None, ALU.add))
            link(dve.reciprocal(cx[:, :], cx[:, :]))
            dve.tensor_tensor(csT[:, :], bank[0][:, 0:2 * KD], cx[:, :], ALU.mult).then_inc(cs_ready, 1)

            def mod_evac(u, bk):
                dve.wait_ge(pe_mod, u + 1)
                if u >= 2 * NA1:
                    dve.wait_ge(s_mod, 16)
                dve.tensor_copy(modst[:, (u % NA1) * UC:(u % NA1 + 1) * UC], bank[bk][0:2, 0:UC]).then_inc(ada_ev, 1)

            for u in range(NA1):
                mod_evac(u, 3 + u % 2)
            dve.wait_ge(pe_sc, 1)
            link(dve.tensor_copy(shsc[:, 0:2 * KD], bank[0][:, 32:32 + 2 * KD]))
            link(dve.tensor_scalar(shsc[:, 2 * KD:4 * KD], bank[0][:, 32 + 2 * KD:32 + 4 * KD], 1.0, None, ALU.add))
            dve.wait_ge(xt_ev, 2 * NT)
            for k in range(KD):
                for b, cs in ((0, slice(0, LP)), (1, slice(LP, T))):
                    dve.tensor_scalar(hT[:, k, cs], hT[:, k, cs], shsc[:, 2 * KD + 2 * k + b:2 * KD + 2 * k + b + 1],
                                      shsc[:, 2 * k + b:2 * k + b + 1], ALU.mult, ALU.add).then_inc(h_ready, 1)
            dve.wait_ge(s_misc, 16 * 7)
            for j in range(NT):
                r = ROWS[j]
                dve.wait_ge(pe_z, j + 1)
                dve.tensor_tensor(z[0:r, j, :], bank[7 if j % 2 == 0 else 0][0:r, 0:H * DK], a2b[0:r, :], ALU.add).then_inc(z_ev, 1)
            dve.wait_ge(z_ev, NT)
            dve.scalar_tensor_tensor(zt, z, -1.0, z, ALU.mult, ALU.max).then_inc(z_abs, 1)
            dve.wait_ge(z_ln, 1)
            dve.scalar_tensor_tensor(z, z, 0.0, zt, ALU.min, ALU.subtract).then_inc(l_ready, 1)
            for j in range(NT):
                r = ROWS[j]
                dve.wait_ge(pe_z, NT + j + 1)
                dve.tensor_copy(bc[:, :, tok(j)], bank[7 if j % 2 == 0 else 0][:, 0:2 * r].rearrange("p (a t) -> p a t", a=2)).then_inc(z_ev, 1)
            dve.wait_ge(z_ev, 2 * NT)
            for a in range(2):
                bp = bc[:, a, 0:LP].rearrange("p (n t) -> p n t", t=CH)
                link(dve.tensor_tensor(ed[:, a, 0:LP].rearrange("p (n t) -> p n t", t=CH),
                                       bcast(bp[:, :, CH - 1:CH], [P, NCH, CH]), bp, ALU.subtract))
                dve.tensor_tensor(ed[:, a, LP:T], bcast(bc[:, a, T - 1:T], [P, LS]), bc[:, a, LP:T], ALU.subtract).then_inc(b_ready, 1)
            dve.wait_ge(e_ready, 3)
            dve.wait_ge(t_ev, 10)
            for a in range(2):
                dve.tensor_copy(gend[:, a, 0:NCH], eb[:, a, 0:LP].rearrange("p (n t) -> p n t", t=CH)[:, :, CH - 1])
                link(dve.tensor_copy(gend[:, a, NCH:NCH + 1], eb[:, a, T - 1:T]))
            link(dve.tensor_tensor(bc, gk, eb, ALU.mult))
            link(dve.tensor_tensor(eb, gq, eb, ALU.mult))
            link(dve.tensor_tensor(gq, gq, ebn, ALU.mult))
            link(dve.tensor_tensor(ebn, gk, ebn, ALU.mult))
            dve.tensor_tensor(ed, gk, ed, ALU.mult).then_inc(gla_ready, 1)
            def evac_tok(m):
                kind, j = TOK[m]
                r = ROWS[j]
                dve.wait_ge(pe_tok, m + 1)
                src = bank[3 + m % 2]
                if kind == "kv":
                    i = NP + 1 if j == NP else j
                    if j >= NP - 1:
                        link(dve.tensor_copy(skt[0:r, j - NP + 1, :], src[0:r, 0:2 * HD]))
                        dve.tensor_copy(svt[0:r, i, :], src[0:r, 2 * HD:4 * HD]).then_inc(tok_ev, 1)
                    else:
                        dve.tensor_copy(svt[0:r, i, :], src[0:r, 0:2 * HD]).then_inc(tok_ev, 1)
                else:
                    dst = gv if kind in ("gv0", "gv1") else grg
                    c = UC * int(kind[-1])
                    dve.tensor_copy(dst[0:r, j, c:c + UC], src[0:r, 0:UC]).then_inc(tok_ev, 1)

            def fill(j, f):
                if (j, f) in TOK_AT:
                    evac_tok(TOK_AT[(j, f)])

            for m in range(NT):
                evac_tok(m)

            def stats_of(j):
                return (small[0:ROWS[j], 16 + 32 * (j % 2) + 8 * i:24 + 32 * (j % 2) + 8 * i] for i in range(4))

            def key_window(j):
                return (P, KW) if j == 0 else (0, KW) if j < NP else (0, WIN + LS)

            def scores(j, g):
                r = ROWS[j]
                w0, w1 = key_window(j)
                n = w1 - w0
                sc = Ssc[j % 2]
                if j >= 2 and g == 0:
                    dve.wait_ge(pe_pt, 4 * (j - 1))
                for par in range(2):
                    dve.wait_ge(pe_qk, 4 * j + 2 * g + par + 1)
                    h0 = 4 * par + 2 * g
                    dve.scalar_tensor_tensor(sc[0:r, h0:h0 + 2, 0:n],
                                             bank[1 + par][0:r, :].rearrange("p (a n) -> p a n", a=2)[:, :, 0:n],
                                             HD ** -0.5, biasH[0:r, h0:h0 + 2, w0:w1], ALU.mult, ALU.add).then_inc(s_ev, 1)

            def maxima(j):
                r = ROWS[j]
                w0, w1 = key_window(j)
                dve.wait_ge(s_ev, 4 * (j + 1))
                mx, nm, rsum, es = stats_of(j)
                link(dve.tensor_reduce(mx, Ssc[j % 2][0:r, :, 0:w1 - w0], AX.X, ALU.max))
                link(dve.tensor_tensor(mx, mx, sinks[0:r, :], ALU.max))
                link(dve.tensor_tensor(es, sinks[0:r, :], mx, ALU.subtract))
                dve.tensor_scalar(nm, mx, -1.0, None, ALU.mult).then_inc(m_ready, 1)

            def normalise(j):
                r = ROWS[j]
                n = P if j == 0 else KW if j < NP else WIN + LS
                mx, nm, rsum, es = stats_of(j)
                sc = Ssc[j % 2][0:r, :, 0:n]
                dve.wait_ge(p_exp, (NQ + 1) * (j + 1))
                link(dve.tensor_tensor(rsum, rsum, es, ALU.add))
                link(dve.reciprocal(rsum, rsum))
                dve.tensor_tensor(sc, sc, bcast(rsum.unsqueeze(2), [r, NQ, n]), ALU.mult).then_inc(p_ready, 1)

            for j in range(NT + 1):
                if j < NT:
                    scores(j, 0)
                fill(j, 0)
                if j < NT:
                    scores(j, 1)
                if j >= 1:
                    normalise(j - 1)
                fill(j, 1)
                if j < NT:
                    maxima(j)
                fill(j, 2)
                fill(j, 3)

            for j in range(NT):
                dve.wait_ge(pe_u, j + 1)
                for c in range(2 if j < NP else 1):
                    n = 2 * j + c
                    s0, s1 = (n, n + 1) if j < NP else (NCH + 1, NCH + 2)
                    for a in range(2):
                        last = dve.scalar_tensor_tensor(S[:, s1, a, :], S[:, s0, a, :], gend[:, a, n:n + 1],
                                                        bank[6 + c][:, a * DV:(a + 1) * DV], ALU.mult, ALU.add)
                        if a == 0 or c == 0 and j < NP:
                            link(last)
                        else:
                            last.then_inc(u_ev, 1)
                            dve.wait_ge(u_ev, j + 1)

            def mask(j):
                r = ROWS[j]
                dve.wait_ge(pe_a, j + 1)
                if j >= 2:
                    dve.wait_ge(pe_o, j - 1)
                for par in range(2):
                    a4 = At[0:r, j % 2, :, 0:r].rearrange("p (a b) t -> p a b t", b=2)[:, :, par, :]
                    for up, mk in ((0, tri), (1, tup)):
                        src = bank[1 + par][0:r, 2 * up * P:2 * (up + 1) * P].rearrange("p (a t) -> p a t", a=2)[:, :, 0:r]
                        last = dve.copy_predicated(a4, bcast(mk[0:r, 0:r].bitcast(i32).unsqueeze(1), [r, 2, r]), src)
                        if up == 0 or par == 0:
                            link(last)
                last.then_inc(a_ev, 1)

            def gated(j):
                r = ROWS[j]
                dve.wait_ge(o_sq, j + 1)
                gx = gex[0:r, j % 2, :]
                o = osb[0:r, j % 2, :]
                link(dve.tensor_scalar(gx, gx, 1.0, None, ALU.add))
                link(dve.reciprocal(gx, gx))
                link(dve.tensor_tensor(gx, gx, grg[0:r, j, :], ALU.mult))
                h3 = [r, H, DV]
                gx3, o3 = gx.rearrange("p (h v) -> p h v", h=H), o.rearrange("p (h v) -> p h v", h=H)
                link(dve.tensor_tensor(gx3, gx3, bcast(nw[0:r, :].unsqueeze(1), h3), ALU.mult))
                link(dve.tensor_tensor(o3, o3, bcast(small[0:r, 8 * (j % 2):8 * (j % 2) + H].unsqueeze(2), h3), ALU.mult))
                if j >= 1:
                    dve.wait_ge(pe_og, j)
                dve.tensor_tensor(og[0:r, :], o, gx, ALU.mult).then_inc(og_ready, 1)

            dve.wait_ge(at_zero, 1)
            for j in range(NT + 2):
                if j < NT:
                    mask(j)
                for u in ADA_AT[j][0]:
                    mod_evac(u, 6 * (u % 2))
                if 1 <= j <= NT:
                    gated(j - 1)
                for u in ADA_AT[j][1]:
                    mod_evac(u, 6 * (u % 2))

            dve.wait_ge(s_gt1, 32)

            def ln_stats(x, j, done):
                r = ROWS[j]
                st = stat[0:r, j % 2, :]
                link(dve.bn_stats(st[:, 0:6], x[:, 0:512]))
                link(dve.bn_stats(st[:, 6:12], x[:, 512:D]))
                dve.bn_aggr(st[:, 12:14], st[:, 0:12]).then_inc(done, 1)

            def ln_finish(x, j, rows):
                r = ROWS[j]
                st = stat[0:r, j % 2, :]
                link(dve.tensor_scalar(x, x, st[:, 12:13], st[:, 13:14], ALU.subtract, ALU.mult))
                link(dve.tensor_tensor(x, x, rows[0:r, 0, :], ALU.mult))

            def logits(j):
                r = ROWS[j]
                dve.wait_ge(pe_rt, j + 1)
                dve.tensor_tensor(lg[0:r, j, :], bank[7][0:r, 0:NG + E], rb[0:r, :], ALU.add).then_inc(rt_ev, 1)

            def residual(j):
                r = ROWS[j]
                md = modP if j < NP else modS
                x = x_tok[0:r, j, :]
                dve.wait_ge(pe_y, j + 1)
                for half in range(2):
                    c = slice(512 * half, 512 * (half + 1))
                    dve.tensor_tensor(ytmp[0:r, c], bank[1 + 2 * (j % 2) + half][0:r, :], md[0][0:r, c], ALU.mult).then_inc(y_ev, 1)
                dve.wait_ge(y_ev, 2 * (j + 1))
                link(dve.scalar_tensor_tensor(x, x, ALPHA, ytmp[0:r, :], ALU.mult, ALU.add))
                ln_stats(x, j, v_ready)

            def modulated(j):
                r = ROWS[j]
                md = modP if j < NP else modS
                x = x_tok[0:r, j, :]
                dve.wait_ge(v_ln, j + 1)
                if j == 0:
                    dve.wait_ge(s_ln1, 32)
                    dve.wait_ge(s_modb, 64)
                ln_finish(x, j, ln1)
                link(dve.tensor_tensor(x, x, ln1[0:r, 1, :], ALU.add))
                if j >= 2:
                    dve.wait_ge(h2_st[j % 2], 16 * (j // 2))
                    dve.wait_ge(pe_ht, 2 * (j - 1))
                link(dve.scalar_tensor_tensor(h2[0:r, j % 2, :], md[2][0:r, :], 1.0, x, ALU.add, ALU.mult))
                dve.tensor_tensor(h2[0:r, j % 2, :], h2[0:r, j % 2, :], md[1][0:r, :], ALU.add).then_inc(h2_ready, 1)

            for j in range(NT + 2):
                if j < NT:
                    residual(j)
                if 1 <= j <= NT:
                    modulated(j - 1)
                if j >= 2:
                    logits(j - 2)

            R5, R4 = [P, NT, E], [P, NT, NG]
            g, ex = lg[:, :, 0:NG], lg[:, :, NG:NG + E]

            def q5(i):
                return rt[:, i, :].rearrange("p (j e) -> p j e", j=NT)

            def q4(i):
                return rt[:, i, 0:NT * NG].rearrange("p (j e) -> p j e", j=NT)

            def over(i, shape):
                return bcast(rs[:, i, :].unsqueeze(2), shape)

            def first_max(v, mxi, eq, out, n, shape):
                link(dve.tensor_tensor(eq, v, over(mxi, shape), ALU.is_equal))
                link(dve.tensor_tensor(eq, eq, bcast(iow[:, 0:n].unsqueeze(1), shape), ALU.mult))
                link(dve.tensor_reduce(rs[:, 9, :], eq, AX.X, ALU.max))
                link(dve.tensor_tensor(out, eq, over(9, shape), ALU.is_equal))

            dve.wait_ge(rt_ev, NT)
            link(dve.tensor_reduce(rs[:, 0, :], g, AX.X, ALU.max))
            link(dve.tensor_tensor(q4(0), g, over(0, R4), ALU.subtract))
            first_max(g, 0, q4(1), q4(2), NG, R4)
            link(dve.tensor_scalar(q4(2), q4(2), 1e30, -1e30, ALU.mult, ALU.add))
            link(dve.tensor_tensor(ex.rearrange("p j (g e) -> p j g e", g=NG), ex.rearrange("p j (g e) -> p j g e", g=NG),
                                   bcast(q4(2).unsqueeze(3), [P, NT, NG, NE]), ALU.add))
            link(dve.tensor_reduce(rs[:, 3, :], ex, AX.X, ALU.max))
            first_max(ex, 3, q5(6), q5(4), E, R5)
            link(dve.scalar_tensor_tensor(q5(6), q5(4), -2e30, ex, ALU.mult, ALU.add))
            link(dve.tensor_reduce(rs[:, 4, :], q5(6), AX.X, ALU.max))
            first_max(q5(6), 4, q5(7), q5(5), E, R5)
            dve.tensor_tensor(q5(3), q5(4), q5(5), ALU.add).then_inc(oh_ready, 1)
            dve.tensor_tensor(rs[:, 5, :], rs[:, 4, :], rs[:, 3, :], ALU.subtract).then_inc(r_ex0, 1)

            dve.wait_ge(pe_rank, 1)
            cnt = bank[0][:, NT * E:(NT + 1) * E]
            link(dve.tensor_scalar(ov[:, 1, :], cnt, float(P), None, ALU.is_gt))
            for m in range(2, OVT + 1):
                link(dve.scalar_tensor_tensor(ov[:, 1, :], cnt, float(m * P), ov[:, 1, :], ALU.is_gt, ALU.add))
            link(dve.tensor_copy(ov[:, 2, :], ov[:, 1, :]))
            a, sh = 2, 1
            while sh < E:
                link(dve.tensor_copy(ov[:, 5 - a, 0:sh], ov[:, a, 0:sh]))
                link(dve.tensor_tensor(ov[:, 5 - a, sh:E], ov[:, a, sh:E], ov[:, a, 0:E - sh], ALU.add))
                a, sh = 5 - a, 2 * sh
            link(dve.tensor_tensor(ov[:, 4, :], ov[:, a, :], ov[:, 1, :], ALU.subtract))
            link(dve.tensor_scalar(ov[:, 4, :], ov[:, 4, :], float(P), float(E * P - P), ALU.mult, ALU.add))
            link(dve.tensor_tensor(ov[:, 4, :], ov[:, 4, :], ov[:, 0, :], ALU.subtract))
            rank = bank[0][:, 0:NT * E].rearrange("p (j e) -> p j e", j=NT)
            link(dve.scalar_tensor_tensor(q5(6), rank, float(P), bcast(ov[:, 4, :].unsqueeze(1), R5), ALU.is_ge, ALU.mult))
            link(dve.tensor_tensor(q5(7), rank, bcast(ov[:, 0, :].unsqueeze(1), R5), ALU.add))
            link(dve.tensor_tensor(q5(6), q5(6), q5(7), ALU.add))
            for k in range(2):
                link(dve.tensor_tensor(q5(7), q5(6), q5(4 + k), ALU.mult))
                link(dve.tensor_reduce(rs[:, 6 + k, :], q5(7), AX.X, ALU.add))
                last = dve.tensor_copy(posi[:, k, :], rs[:, 6 + k, :])
                if k == 0:
                    link(last)
            last.then_inc(pos_ready, 1)
            dve.wait_ge(r_ex, 1)
            link(dve.tensor_reduce(rs[:, 1, :], q4(0), AX.X, ALU.add))
            link(dve.tensor_scalar(rs[:, 2, :], rs[:, 5, :], 1.0, None, ALU.add))
            link(dve.tensor_tensor(rs[:, 1, :], rs[:, 1, :], rs[:, 2, :], ALU.mult))
            link(dve.reciprocal(wts[:, 0, :], rs[:, 1, :]))
            link(dve.tensor_tensor(wts[:, 1, :], wts[:, 0, :], rs[:, 5, :], ALU.mult))
            link(dve.tensor_copy(ovi[0:1, 0:1], ov[0:1, a, E - 1:E]))
            for b in range(NOV):
                link(dve.tensor_scalar(ov[0:1, 1, :], ov[0:1, a, :], float(b), None, ALU.is_le))
                link(dve.tensor_reduce(rs[0:1, 8, 0:1], ov[0:1, 1, :], AX.X, ALU.add))
                link(dve.tensor_scalar(rs[0:1, 8, 0:1], rs[0:1, 8, 0:1], float(E - 1), None, ALU.min))
                last = dve.tensor_copy(ovi[0:1, b + 1:b + 2], rs[0:1, 8, 0:1])
                if b < NOV - 1:
                    link(last)
            last.then_inc(ov_ready, 1)
            dve.wait_ge(pe_tbl, 1)
            ent = bank[7][:, 0:NBLK]
            link(dve.tensor_copy(dsti[:, :], ent))
            link(dve.tensor_scalar(fl[:, :], ent, float(KSTEP), -float(KSTEP), ALU.is_ge, ALU.mult))
            dve.tensor_tensor(srci[:, :], ent, fl[:, :], ALU.add).then_inc(tbl_ready, 1)

            def evac_xe(a, w):
                dve.wait_ge(pe_xe, w)
                dve.tensor_copy(xTe[:, a, 4:8, :], bank[1][:, :].rearrange("p (k t) -> p k t", k=4)).then_inc(xe_d, 1)

            def hidden(a, w):
                dve.wait_ge(sg_done, w)
                dve.tensor_tensor(hid[:, a, :], bank[2 + a][:, FF:2 * FF], sgl[:, a, :], ALU.mult).then_inc(hid_done, 1)

            def evac_y(a, w, free):
                dve.wait_ge(pe_dn, w)
                if free is not None:
                    dve.wait_ge(s_sc[a], free)
                dve.tensor_copy(ye[:, a, 512:D], bank[6][:, :]).then_inc(y_d, 1)

            def step(e, i, last=False):
                x, b = e % 2, (e - 1) % 2
                hidden(x, at(e + 1, 2, i))
                if not last:
                    evac_xe(b, at(e + 2, 2, i))
                evac_y(b, at(e, 2, i), at(16 * ((e - 1) // 2), 16, i) if e >= 3 or i is not None else None)

            evac_xe(0, 1)
            hidden(0, 1)
            evac_xe(1, 2)
            step(1, None)
            step(2, None)
            with dve.Fori(1, E // 2 - 1) as i:
                step(1, i)
                step(2, i)
            step(E - 1, None, last=True)
            evac_y(1, E, 16 * (E // 2 - 1))
            nov = dve.value_load(ovi[0:1, 0:1], min_val=0, max_val=NOV)
            with dve.If(nov > 0):
                with dve.Fori(0, nov) as i:
                    evac_xe(0, i + E + 1)
                    hidden(0, i + E + 1)
                    evac_y(0, i + E + 1, i * 16 + 16 * (E // 2))

            dve.wait_ge(s_ln2, 32)
            dve.wait_ge(s_gt2, 32)
            for j in range(NT + 1):
                if j < NT:
                    r = ROWS[j]
                    md = modP if j < NP else modS
                    x = x_tok[0:r, j, :]
                    y = ring[0:r, j, 0:D]
                    dve.wait_ge(f_a, j + 1)
                    link(dve.scalar_tensor_tensor(y, ring[0:r, j, D:2 * D], wts[0:r, 1, j:j + 1], y, ALU.mult, ALU.add))
                    link(dve.tensor_tensor(y, y, md[3][0:r, :], ALU.mult))
                    link(dve.scalar_tensor_tensor(x, x, ALPHA, y, ALU.mult, ALU.add))
                    if j >= 2:
                        dve.wait_ge(f_l, j - 1)
                    ln_stats(x, j, f_v)
                if j >= 1:
                    x = x_tok[0:ROWS[j - 1], j - 1, :]
                    dve.wait_ge(f_l, j)
                    dve.tensor_tensor(x, x, ln2[0:ROWS[j - 1], 0, :], ALU.mult).then_inc(f_g, 1)


_INS = ["x_prompt", "x_sample", "c_prompt", "c_sample", "state_gla", "cache_swa_k", "cache_swa_v",
        "ada_w", "ada_b", "w_in", "gla_a2_w", "gla_a2_b", "gla_norm_w", "swa_sinks", "w_o", "ln1_g", "ln1_b",
        "router_g_w", "router_g_b", "router_e_w", "router_e_b", "moe_w_gate", "moe_w_up", "moe_w_down",
        "ln2_g", "ln2_b"]
_OUTS = [(1, 512, 1024), (1, 32, 1024), (1, 1, 4, 64, 128), (1, 1, 128, 2, 64), (1, 1, 128, 2, 64),
         (1, 1, 4, 64, 128), (1, 1, 128, 2, 64), (1, 1, 128, 2, 64)]


def kernel(**inputs):
    import numpy as _np
    import concourse.bacc as _bacc
    from concourse import mybir as _mybir
    from concourse.bass_utils import run_bass_kernel_spmd as _run

    nc = _bacc.Bacc("TRN2", target_bir_lowering=False, num_devices=1)
    arrays, args = {}, []
    for name in _INS:
        a = _np.ascontiguousarray(inputs[name])
        arrays[f"in_{name}_dram"] = a
        args.append(nc.dram_tensor(f"in_{name}_dram", a.shape, _mybir.dt.from_np(a.dtype), kind="ExternalInput").ap())
    for i, shape in enumerate(_OUTS):
        args.append(nc.dram_tensor(f"out_{i}_dram", shape, _mybir.dt.float32, kind="ExternalOutput").ap())
    hymba_stream_step(nc, *args)
    r = _run(nc, [arrays], core_ids=[0])
    return tuple(r.results[0][f"out_{i}_dram"] for i in range(len(_OUTS)))
```

```python
import concourse.bass as bass
from concourse import mybir
from contextlib import ExitStack


def hymba_stream_step(nc, x_prompt, x_sample, c_prompt, c_sample, state_gla, cache_swa_k, cache_swa_v,
                      ada_w, ada_b, w_in, gla_a2_w, gla_a2_b, gla_norm_w, swa_sinks, w_o, ln1_g, ln1_b,
                      router_g_w, router_g_b, router_e_w, router_e_b, moe_w_gate, moe_w_up, moe_w_down,
                      ln2_g, ln2_b,
                      y_prompt, y_sample, state_prompt, k_prompt, v_prompt, state_sample, k_sample, v_sample):
    f32, i32 = mybir.dt.float32, mybir.dt.int32
    f32r = mybir.dt.float32r
    ALU = mybir.AluOpType
    ACT = mybir.ActivationFunctionType
    AX = mybir.AxisListType

    P = 128
    D = x_prompt.shape[2]
    KD = D // P
    LP, LS = x_prompt.shape[1], x_sample.shape[1]
    T = LP + LS
    NP = LP // P
    NT = NP + 1
    ROWS = [P] * NP + [LS]
    CH = 64
    NCH = LP // CH
    H, DK, DV = state_gla.shape[2:]
    HD = cache_swa_k.shape[4]
    NQ = swa_sinks.shape[1]
    WIN = cache_swa_k.shape[2]
    KW = WIN + P
    NG, NE = router_g_w.shape[2], router_e_w.shape[3]
    E = NG * NE
    FF = moe_w_gate.shape[4]
    NF = FF // P
    ALPHA = 2.0 ** 0.25
    EPS = 1e-5
    O_GQ, O_GK, O_GV, O_GR, O_GA = 0, H * DK, 2 * H * DK, 2 * H * DK + H * DV, 2 * H * DK + 2 * H * DV
    RANK = gla_a2_w.shape[1]
    O_SQ = O_GA + RANK
    O_SK = O_SQ + NQ * HD
    O_SV = O_SK + 2 * HD
    UC = 256

    PAIRS = 2 * T
    NOV = PAIRS // (P + 1)
    OVT = (T - 1) // P
    NBLK = E + NOV
    KSTEP = 1024
    EMPTY = 4096

    mod_d = nc.dram_tensor("mod_scratch", [2, 6 * D], f32).ap()
    h2_d = nc.dram_tensor("h2_scratch", [T, D], f32).ap()
    tbl_d = nc.dram_tensor("slot_table", [NBLK * P, 1], f32).ap()
    yb_d = nc.dram_tensor("expert_rows", [2 * KSTEP, D], f32).ap()

    def cols(w, c, n):
        return w[:, c:c + n].rearrange("(k p) n -> p k n", p=P)

    NR = 6
    NR1 = NR - 1
    units = []
    NA1 = 2 * D // UC
    NA = 6 * D // UC
    for u in range(NA1):
        units.append(("ada", u))
    WIN_UNITS = ["gq", "gk", "sq0", "sq1", "kv", "gv0", "gv1", "gr0", "gr1"]
    for w in WIN_UNITS:
        units.append((w, 0))
    NA2 = 5 * D // UC
    for u in range(NA1, NA2):
        units.append(("ada", u))
    for u in range(KD // 2):
        units.append(("wo", u))
    for u in range(NA2, NA):
        units.append(("ada", u))
    N0 = len(units)
    number = {u: n for n, u in enumerate(units)}

    ctx = ExitStack()
    with ctx:
        def sb(name, shape, dt=f32):
            return ctx.enter_context(nc.sbuf_tensor(name, shape, dt))

        def sem(name):
            return ctx.enter_context(nc.semaphore(name))

        bank = [ctx.enter_context(nc.psum_tensor(f"bank{i}", [P, 512], f32)) for i in range(8)]

        def place_r(name, shape):
            with nc.sbuf_tensor(name, shape, f32r) as t:
                return t

        ring_r = place_r("ring_r", [P, NR, KD * UC])
        ring = sb("ring", [P, NR, KD * UC])
        hH = place_r("h_high", [P, KD, T])
        x_tok = sb("x_tok", [P, NT, D])
        biasH = sb("biasH", [P, NQ, KW])
        ln2 = biasH[:, :, :].rearrange("p h n -> p (h n)").rearrange("p (a n) -> p a n", a=2)
        skT = sb("skT", [P, LP + WIN + LS])
        gaT = sb("gaT", [RANK, T])
        svt = sb("svt", [P, NT + 1, 2 * HD])
        skt = sb("skt", [P, 2, 2 * HD])
        S_r = place_r("S_r", [P, (NCH + 3) * 2 * DV])
        S = sb("S", [P, NCH + 3, 2, DV])
        gend = sb("gend", [P, 2, NCH + 1])
        modrt = sb("modrt", [P, 2 * D])
        modst = modrt[0:2, :]
        adab = sb("adab", [NA, UC])
        crow = sb("crow", [2 * KD, P])
        cT = sb("cT", [P, 2 * KD])
        cx = sb("cx", [P, 2 * KD])
        csT = sb("csT", [P, 2 * KD])
        shsc = sb("shsc", [P, 4 * KD])
        wga = sb("wga", [P, KD, RANK])
        a2w = sb("a2w", [RANK, H * DK])
        a2b = sb("a2b", [P, H * DK])
        nw = sb("nw", [P, DV])
        sinks = sb("sinks", [P, NQ])
        rw = sb("rw", [P, KD, NG + E])
        rb = sb("rb", [P, NG + E])
        kc = sb("kc", [P, 2 * HD])
        ident = sb("ident", [P, P])
        tri = sb("tri", [P, P])
        tup = sb("tup", [P, P])
        before = sb("before", [P, P])
        ones = sb("ones", [P, P])
        dist = sb("dist", [P, KW])
        epst = sb("epst", [P, 1])
        iow = sb("iow", [P, 40])
        fl = sb("fl", [P, NBLK])
        small = sb("small", [P, 80])
        stat = sb("stat", [P, 2, 16])
        lg = sb("lg", [P, NT, NG + E])
        rt = modrt[:, 0:10 * NT * E].rearrange("p (i n) -> p i n", i=10)
        rs = sb("rs", [P, 12, NT])
        ov = sb("ov", [P, 6, E])
        wts = sb("wts", [P, 2, NT])
        posi = sb("posi", [P, 2, NT], i32)
        tokv = sb("tokv", [P, 2, NT])
        trow = sb("trow", [NBLK, P])
        srci = sb("srci", [P, NBLK], i32)
        dsti = sb("dsti", [P, NBLK], i32)
        cnti = sb("cnti", [1, E], i32)
        ovi = sb("ovi", [1, 2 + NOV], i32)

        early = ExitStack()

        def early_sb(name, shape):
            return early.enter_context(nc.sbuf_tensor(name, shape, f32))

        hL = place_r("h_low", [P, KD, T])
        areaA = early_sb("areaA", [P, KD, T])
        hT, mixT = areaA, areaA
        areaB = early_sb("areaB", [P, 8 * T * 2])
        GW = 2 * T

        def area_b(i, n=1):
            return areaB[:, i * GW:(i + n) * GW]
        gq, gk, bc, eb, ebn, ed = (area_b(i).rearrange("p (a t) -> p a t", a=2) for i in range(6))
        sqT = area_b(6, 2).rearrange("p (a t) -> p a t", a=4)
        mixS = sqT
        areaC_r = place_r("areaC_r", [P, 9 * D + 256])
        areaC = early_sb("areaC", [P, 9 * D + 256])
        gv = areaC[:, 0:NT * H * DV].rearrange("p (j n) -> p j n", j=NT)
        wga_r = areaC_r[:, 9 * D:9 * D + 2 * KD * RANK].rearrange("p (i k n) -> p i k n", i=2, k=KD)
        wH = [ring_r[:, NR - 1, :], S_r[:, 2 * DV:2 * DV + KD * UC]]
        gt2st = areaC[0:2, 7 * D:8 * D]
        grg = areaC[:, NT * 512:2 * NT * 512].rearrange("p (j n) -> p j n", j=NT)
        PT = areaC[:, 7 * D:9 * D].rearrange("p (h b q) -> p h b q", h=NQ, b=2)
        z = areaC[:, 5 * D:5 * D + NT * 256].rearrange("p (j n) -> p j n", j=NT)
        zt = areaC[:, 7 * D:7 * D + NT * 256].rearrange("p (j n) -> p j n", j=NT)
        h2Tt = areaC[:, 0:D].rearrange("p (k t) -> p k t", k=KD)
        ytmp = areaC[:, D:2 * D]
        ln1 = areaC[:, 2 * D:4 * D].rearrange("p (a n) -> p a n", a=2)
        h2 = areaC[:, 5 * D:7 * D].rearrange("p (a n) -> p a n", a=2)
        osb = areaC[:, 5 * D:6 * D].rearrange("p (a n) -> p a n", a=2)
        gex = areaC[:, 6 * D:7 * D].rearrange("p (a n) -> p a n", a=2)
        kdT = areaC[:, 7 * D:7 * D + 4 * P].rearrange("p (a n) -> p a n", a=2)
        og = areaC[:, 7 * D + 4 * P:7 * D + 8 * P]
        At = areaC[:, 8 * D + 256:9 * D + 256].rearrange("p (a h t) -> p a h t", a=2, h=H)
        Ssc = [t.rearrange("p (h n) -> p h n", h=NQ) for t in (areaC[:, 5 * D:7 * D], modrt[:, :])]
        modP = [area_b(5)[:, 0:D], area_b(0)[:, 0:D], area_b(2)[:, 0:D], modrt[:, 0:D]]
        modS = [area_b(1)[:, 0:D], area_b(3)[:, 0:D], area_b(4)[:, 0:D], modrt[:, D:2 * D]]
        early.close()
        wsplit = sb("wsplit", [P, 3, 2, KD * UC], f32r)
        xg = sb("xg", [P, 2, D])
        xh = sb("xh", [P, 2, KD, P], f32r)
        xl = sb("xl", [P, 2, KD, P], f32r)
        ye = sb("ye", [P, 2, D])
        hid = sb("hid", [P, 2, FF])
        sgl = sb("sgl", [P, 2, FF])
        hh = sb("hh", [P, 2, NF, P], f32r)
        hl = sb("hl", [P, 2, NF, P], f32r)

        s_c, s_x, s_adab, s_misc, s_misc2 = sem("c_loaded"), sem("x_loaded"), sem("adab_loaded"), sem("misc_loaded"), sem("router_loaded")
        full = [sem(f"ring_full{i}") for i in range(NR)]
        pe_mod = sem("mod_units_done")
        wo_used, pe_g = sem("wo_units_used"), sem("gate_done")
        dv = sem("dve_chain")
        ac = sem("act_chain")
        pl = sem("pool_chain")
        pe_c, c_ex, cs_ready = sem("c_transposed"), sem("c_exp"), sem("cs_ready")
        pe_xt, xt_ev = sem("x_transposed"), sem("xT_evacuated")
        ada_ev, pe_sc, h_ready = sem("mod_evacuated"), sem("mod_transposed"), sem("h_ready")
        pe_t, t_ev = sem("proj_T_done"), sem("proj_T_evacuated")
        pe_z, z_ev, z_abs, z_ln, l_ready = sem("gate_psum"), sem("gate_evacuated"), sem("z_abs"), sem("z_ln"), sem("loga_ready")
        b_ready, e_ready, gla_ready = sem("b_ready"), sem("exps_ready"), sem("gla_operands_ready")
        pe_tok, tok_ev = sem("proj_tok_done"), sem("proj_tok_evacuated")
        pe_kd, kd_ev, pe_u, u_ev = sem("kd_transposed"), sem("kd_evacuated"), sem("u_done"), sem("state_updated")
        pe_a, a_ev, pe_o, o_ev, o_sq, og_ready, pe_og, mg_ev = (sem(n) for n in (
            "A_done", "A_masked", "o_done", "o_evacuated", "o_stats", "og_ready", "og_transposed", "mixT_gla"))
        pe_qk, s_ev, m_ready, p_exp, p_ready, pe_pt, pt_ev, pe_pv, pv_ev = (sem(n) for n in (
            "qk_done", "scores_ready", "max_ready", "probs_exp", "probs_ready", "P_transposed", "PT_evacuated",
            "pv_done", "mixT_swa"))
        s_mod, s_modb, s_ln1, s_ln2, s_kc = sem("mod_stored"), sem("mod_rows"), sem("ln1_rows"), sem("ln2_rows"), sem("cache_loaded")
        pe_y, y_ev, v_ready, v_ln, h2_ready, h2_st = (sem(n) for n in (
            "out_proj_done", "out_proj_read", "var_ready", "rstd_ready", "h2_ready", "h2_stored"))
        h2_st = [h2_st, sem("h2_stored1")]
        pe_ht, ht_ev, pe_rt, rt_ev = sem("h2_transposed"), sem("h2T_evacuated"), sem("logits_done"), sem("logits_read")
        r_ex0, r_ex, oh_ready, pe_rank, pos_ready = (sem(n) for n in (
            "router_diffs", "router_exps", "onehots_ready", "ranks_done", "slots_ready"))
        s_tbl0, s_scat, s_trow, pe_tbl, tbl_ready, ov_ready = (sem(n) for n in (
            "table_empty", "table_filled", "table_loaded", "table_transposed", "table_ready", "overflow_ready"))
        s_g = [sem("rows_gathered0"), sem("rows_gathered1")]
        s_sc = [sem("rows_scattered0"), sem("rows_scattered1")]
        pe_xe, xe_a, pe_gu, sg_done, hid_done, pe_hT, hT_ev, pe_dn, y_a, y_d = (sem(n) for n in (
            "xe_transposed", "xe_high", "gate_up_done", "silu_done", "hid_done",
            "hid_transposed", "hidT_evacuated", "down_done", "ye_act", "ye_dve"))
        o_w = sem("overflow_weights")
        s_fin = [sem(f"final_rows{j}") for j in range(NT)]
        f_a, f_v, f_l, f_o = sem("final_scaled"), sem("final_var"), sem("final_rstd"), sem("final_out")
        f_g = sem("final_gained")
        f_s, f_m = sem("experts_summed"), sem("sum_modulated")
        s_out, s_kv = sem("outputs_stored"), sem("caches_stored")
        moe_over = sem("moe_over")
        at_zero = sem("A_zeroed")
        gt2_ev = sem("gt2_evacuated")
        h_high, h_low, ga_high = sem("h_high_parts"), sem("h_low_parts"), sem("ga_high")
        iw_h, iw_l = sem("proj_weights_high"), sem("proj_weights_low")
        wh_ready, wl_ready = sem("weights_high"), sem("weights_low")
        xe_l, hT_l = sem("xe_low"), sem("hidT_low")
        s_gt1, s_gt2 = sem("gt1_rows"), sem("gt2_rows")

        block = ctx.enter_context(nc.Block())

        def tok(j):
            return slice(P * j, P * j + ROWS[j])

        def place(n):
            return n % NR1 if n < N0 else n % NR

        def slot(n):
            return ring[:, place(n), :]

        def unit_src(kind, u):
            if kind == "ada":
                return [(slice(0, KD * UC), cols(ada_w[0], u * UC, UC))]
            if kind == "wo":
                half = D * 2
                if u < KD // 4:
                    return [(None, w_o[0, 2 * P * u:2 * P * (u + 1), :].rearrange("(k p) n -> p k n", p=P))]
                i0 = 2 * (u - KD // 4)
                return [(g, w_o[0, H * DV + g * 4 * HD + i0 * HD:H * DV + g * 4 * HD + (i0 + 2) * HD, :]
                         .rearrange("(k p) n -> p k n", p=HD)) for g in range(2)]
            if kind in ("sq0", "sq1"):
                a = O_SQ + (0 if kind == "sq0" else 2 * HD)
                return [(2 * i + g, cols(w_in[0], a + g * 4 * HD + i * HD, HD)) for i in range(2) for g in range(2)]
            c = {"gq": O_GQ, "gk": O_GK, "kv": O_SK, "gv0": O_GV, "gv1": O_GV + UC, "gr0": O_GR, "gr1": O_GR + UC}[kind]
            return [(None, cols(w_in[0], c, UC))]

        NDMA = [len(unit_src(*u)) for u in units]

        def full_count(n):
            return sum(16 * NDMA[m] for m in range(n % NR1, n + 1, NR1))

        FULL0 = [0] * NR
        for n in range(N0):
            FULL0[place(n)] += 16 * NDMA[n]

        def expert_count(n):
            first = N0 + (n - N0) % NR
            return FULL0[place(n)] + 16 * ((n - first) // NR + 1)

        W3 = [moe_w_gate, moe_w_up, moe_w_down]

        def low_count(e, r):
            if r == 2:
                return 3 * e + 5 if e < E - 1 else 3 * E
            return 3 * e + r if e >= 1 else r + 1

        def expert_src(e, r):
            w = W3[r][0].rearrange("g e a b -> (g e) a b")
            w = w[e] if isinstance(e, int) else w[bass.ds(e, 1)].rearrange("o a b -> (o a) b")
            return w.rearrange("(k p) n -> p k n", p=P)

        def slot_view(n, kd):
            return slot(n).rearrange("p (k n) -> p k n", k=kd)

        LAST = {"gq": (pe_t, 3), "gk": (pe_t, 5), "sq0": (pe_t, 7), "sq1": (pe_t, 9), "kv": (pe_tok, NT),
                "gv0": (pe_tok, 2 * NT), "gv1": (pe_tok, 3 * NT), "gr0": (pe_tok, 4 * NT), "gr1": (pe_tok, 5 * NT)}

        def freed(n):
            kind, u = units[n]
            if kind == "ada":
                return pe_mod, u + 1
            if kind == "wo":
                return (wo_used, u + 1) if u < KD // 2 - 1 else (pe_y, NT)
            return LAST[kind]

        ADA_STATE = [NA1 + j for j in range(NT)]
        ADA_GLA = [NA1 + NT + j for j in range(NT + 2)]
        assert ADA_GLA[-1] == NA2 - 1 and NA - NA2 == 4

        TOK = [(kind, j) for kind in ("kv", "gv0", "gv1", "gr0", "gr1") for j in range(NT)]
        def t_cut(tb):
            return LP if tb == 9 else T // 2

        SPLIT_AT = {-1: 6, 1: 7, 2: 8}
        places = [(j, f) for j in range(NT + 1) for f in range(4) if (j, f) not in ((0, 2), (0, 3), (NT, 0), (NT, 1))]
        TOK_AT = dict(zip(places, range(NT, len(TOK))))

        def at(base, step, i):
            return base if i is None else i * step + base

        @block.sync
        def _(sp):
            sp.dma_start(crow[0:KD, :], c_prompt[0, :].rearrange("(k p) -> k p", p=P)).then_inc(s_c, 16)
            sp.dma_start(crow[KD:2 * KD, :], c_sample[0, :].rearrange("(k p) -> k p", p=P)).then_inc(s_c, 16)
            sp.dma_start(adab[:, :], ada_b[0, :].rearrange("(u n) -> u n", n=UC)).then_inc(s_adab, 16)
            for n, (kind, u) in enumerate(units):
                if n == 2:
                    sp.dma_start(x_tok[:, 0:NP, :], x_prompt[0].rearrange("(j p) n -> p j n", p=P)).then_inc(s_x, 16)
                    sp.dma_start(x_tok[0:LS, NP, :], x_sample[0]).then_inc(s_x, 16)
                if n == number[("wo", 0)]:
                    sp.wait_ge(pe_tok, len(TOK))
                    sp.dma_start(x_tok[:, 0:NP, :], x_prompt[0].rearrange("(j p) n -> p j n", p=P)).then_inc(s_x, 16)
                    sp.dma_start(x_tok[0:LS, NP, :], x_sample[0]).then_inc(s_x, 16)
                if n >= NR1:
                    sp.wait_ge(*freed(n - NR1))
                for g, src in unit_src(kind, u):
                    if kind == "wo":
                        v = slot_view(n, 2)
                        dst = v if g is None else v[g * HD:(g + 1) * HD, :, :]
                    elif kind in ("sq0", "sq1"):
                        dst = slot_view(n, KD)[:, :, g * HD:(g + 1) * HD]
                    else:
                        dst = slot_view(n, KD)
                    sp.dma_start(dst, src).then_inc(full[place(n)], 16)

            def load(e, r, slot_n):
                sp.dma_start(slot_view(slot_n, KD if r < 2 else NF), expert_src(e, r)).then_inc(full[place(slot_n)], 16)

            def load_first(e, r):
                n = N0 + 3 * e + r
                if e < 2:
                    former = [m for m in range(N0) if m % NR1 == place(n)]
                    sp.wait_ge(*(freed(former[-1]) if former else (pe_tok, len(TOK))))
                else:
                    sp.wait_ge(wl_ready, low_count(e - 2, r))
                load(e, r, n)

            for e in range(4):
                load_first(e, 0)
                load_first(e, 1)
                if e >= 1:
                    load_first(e - 1, 2)
            with sp.Fori(2, E // 2) as i:
                for b in range(2):
                    for c, r in ((b, 0), (b, 1), (b - 1, 2)):
                        sp.wait_ge(wl_ready, i * 6 + (low_count(c + 2, r) - 12))
                        load(i * 2 + c, r, N0 + 3 * (c % 2) + r)
            sp.wait_ge(wl_ready, low_count(E - 3, 2))
            load(E - 1, 2, N0 + 3 + 2)

            sp.wait_ge(moe_over, 1)
            sp.wait_ge(ov_ready, 1)
            nov = sp.value_load(ovi[0:1, 0:1], min_val=0, max_val=NOV)
            with sp.If(nov > 0):
                with sp.Fori(0, nov) as i:
                    e = sp.value_load(ovi[0:1, bass.ds(i + 1, 1)], min_val=0, max_val=E - 1)
                    sp.wait_ge(y_d, i + E)
                    for r in range(3):
                        sp.dma_start(ring[:, r, :].rearrange("p (k n) -> p k n", k=KD if r < 2 else NF),
                                     expert_src(e, r)).then_inc(o_w, 16)

            sp.wait_ge(moe_over, 2)
            rows3 = yb_d.rearrange("(k t) n -> t k n", k=2)
            for j in range(NT):
                sp.dma_start(ring[0:ROWS[j], j, :].rearrange("p (k n) -> p k n", k=2),
                             rows3[P * j:P * j + ROWS[j], :, :]).then_inc(s_fin[j], 16)
            for j in range(NT):
                sp.wait_ge(f_o, j + 1)
                dst = y_prompt[0, P * j:P * (j + 1), :] if j < NP else y_sample[0]
                sp.dma_start(dst, x_tok[0:ROWS[j], j, :]).then_inc(s_out, 16)
            sp.wait_ge(s_out, 16 * NT)

        NCONST = 20

        @block.gpsimd
        def _(pool):
            chain = [0]

            def link(ins):
                chain[0] += 1
                ins.then_inc(pl, 1)
                pool.wait_ge(pl, chain[0])

            link(pool.memset(epst[:, :], EPS))
            link(pool.memset(ident[:, :], 0.0))
            link(pool.affine_select(out=ident[:, :], in_=ident[:, :], compare_op=ALU.not_equal, fill=1.0, base=0,
                               pattern=[[-1, P]], channel_multiplier=1))
            link(pool.memset(ones[:, :], 1.0))
            link(pool.memset(tri[:, :], 1.0 / 16.0))
            link(pool.affine_select(out=tri[:, :], in_=tri[:, :], compare_op=ALU.is_ge, fill=0.0, base=0,
                                    pattern=[[1, P]], channel_multiplier=-1))
            link(pool.memset(tri[0:CH, CH:P], 0.0))
            link(pool.memset(tup[:, :], 1.0))
            link(pool.affine_select(out=tup[:, :], in_=tup[:, :], compare_op=ALU.is_ge, fill=0.0, base=-1,
                                    pattern=[[-1, P]], channel_multiplier=1))
            link(pool.memset(tup[CH:P, 0:CH], 0.0))
            link(pool.memset(before[:, :], 1.0))
            link(pool.affine_select(out=before[:, :], in_=before[:, :], compare_op=ALU.is_ge, fill=0.0, base=-1,
                               pattern=[[1, P]], channel_multiplier=-1))
            link(pool.iota(dist[:, :], pattern=[[1, KW]], base=-WIN, channel_multiplier=-1,
                      allow_small_or_imprecise_dtypes=True))
            link(pool.memset(z[:, NP, :], 0.0))
            link(pool.memset(S[:, 0, :, :], 0.0))
            link(pool.memset(lg[:, :, :], 0.0))
            link(pool.iota(ov[:, 0, :], pattern=[[P, E]], base=0, channel_multiplier=0,
                      allow_small_or_imprecise_dtypes=True))
            link(pool.iota(iow[:, 0:E], pattern=[[-1, E]], base=E, channel_multiplier=0,
                      allow_small_or_imprecise_dtypes=True))
            for k in range(2):
                link(pool.iota(tokv[:, k, :], pattern=[[P, NT]], base=k * KSTEP, channel_multiplier=1,
                          allow_small_or_imprecise_dtypes=True))
            link(pool.memset(fl[:, :], float(EMPTY)))
            pool.dma_start(tbl_d.rearrange("(p b) o -> p (b o)", p=P), fl[:, :]).then_inc(s_tbl0, 16)

            pool.wait_ge(tok_ev, NT)
            pool.dma_start(k_prompt[0, 0].rearrange("t h d -> t (h d)"), skt[:, 0, :]).then_inc(s_kv, 16)
            pool.dma_start(v_prompt[0, 0].rearrange("t h d -> t (h d)"), svt[:, NP - 1, :]).then_inc(s_kv, 16)
            for dst, old, new in ((k_sample, kc[LS:P, :], skt[0:LS, 1, :]), (v_sample, svt[LS:P, NP, :], svt[0:LS, NP + 1, :])):
                d = dst[0, 0].rearrange("t h d -> t (h d)")
                pool.dma_start(d[0:WIN - LS, :], old).then_inc(s_kv, 16)
                pool.dma_start(d[WIN - LS:WIN, :], new).then_inc(s_kv, 16)
            pool.wait_ge(pe_pv, NT)
            pool.memset(At[:, :, :, :], 0.0).then_inc(at_zero, 1)
            pool.wait_ge(s_ev, 4 * NT)
            pool.dma_start(ln2[:, 0, :], ln2_g.to_broadcast([P, D])).then_inc(s_ln2, 16)
            pool.dma_start(ln2[:, 1, :], ln2_b.to_broadcast([P, D])).then_inc(s_ln2, 16)
            pool.wait_ge(u_ev, NT)
            for dst, n in ((state_prompt, NCH), (state_sample, NCH + 2)):
                pool.dma_start(dst[0, 0].rearrange("(a h) k v -> (h k) a v", a=2), S[:, n, :, :]).then_inc(s_kv, 16)
            pool.wait_ge(s_kv, 16 * 8)
            def mod_rows(a, loaded):
                c = slice((a + 2) * D, (a + 3) * D)
                pool.dma_start(modP[a], mod_d[0:1, c].to_broadcast([P, D])).then_inc(loaded, 16)
                pool.dma_start(modS[a][0:LS, :], mod_d[1:2, c].to_broadcast([LS, D])).then_inc(loaded, 16)

            pool.wait_ge(ada_ev, NA1 * 2)
            pool.dma_start(mod_d[:, 2 * D:4 * D], modst[:, :]).then_inc(s_mod, 16)
            pool.wait_ge(s_mod, 16)
            mod_rows(0, s_gt1)
            pool.wait_ge(ada_ev, NA2)
            pool.dma_start(mod_d[:, 4 * D:5 * D], modst[:, 0:D]).then_inc(s_mod, 16)
            pool.wait_ge(s_mod, 32)
            pool.wait_ge(pe_o, NT)
            mod_rows(1, s_modb)
            mod_rows(2, s_modb)
            pool.wait_ge(og_ready, NT)
            pool.dma_start(ln1[:, 0, :], ln1_g.to_broadcast([P, D])).then_inc(s_ln1, 16)
            pool.dma_start(ln1[:, 1, :], ln1_b.to_broadcast([P, D])).then_inc(s_ln1, 16)

            pool.wait_ge(gt2_ev, NA - NA2)
            pool.dma_start(mod_d[:, 5 * D:6 * D], gt2st[:, :]).then_inc(s_mod, 16)
            pool.wait_ge(pos_ready, 1)
            pool.wait_ge(s_tbl0, 16)
            for k in range(2):
                for j in range(NT):
                    pool.indirect_dma_start(
                        out=tbl_d[:, :], out_offset=bass.IndirectOffsetOnAxis(ap=posi[0:ROWS[j], k, j:j + 1], axis=0),
                        in_=tokv[0:ROWS[j], k, j:j + 1], in_offset=None,
                        bounds_check=NBLK * P - 1, oob_is_err=False).then_inc(s_scat, 16)
            pool.wait_ge(s_scat, 16 * 2 * NT)
            pool.dma_start(trow[:, :], tbl_d.rearrange("(b p) o -> b (p o)", p=P)).then_inc(s_trow, 16)
            pool.wait_ge(pe_y, NT)
            pool.wait_ge(pe_rt, NT)
            pool.wait_ge(h2_st[0], 16 * ((NT + 1) // 2))
            pool.wait_ge(h2_st[1], 16 * (NT // 2))
            link(pool.memset(xg[:, :, :], 0.0))
            pool.wait_ge(s_mod, 48)
            pool.wait_ge(tbl_ready, 1)

            def move_rows(b, move, done):
                if b >= E:
                    move(P).then_inc(done, 16)
                    return
                rows = pool.value_load(cnti[0:1, b:b + 1], min_val=0, max_val=T)
                with pool.If(rows < 33):
                    move(32).then_inc(done, 16)
                with pool.If(rows > 32):
                    with pool.If(rows < 65):
                        move(64).then_inc(done, 16)
                with pool.If(rows > 64):
                    move(P).then_inc(done, 16)

            def gather(b, a):
                move_rows(b, lambda n: pool.indirect_dma_start(
                    out=xg[0:n, a, :], out_offset=None, in_=h2_d[:, :],
                    in_offset=bass.IndirectOffsetOnAxis(ap=srci[0:n, b:b + 1], axis=0),
                    bounds_check=T - 1, oob_is_err=False), s_g[a])

            def scatter(b, a):
                pool.wait_ge(y_a, b + 1)
                pool.wait_ge(y_d, b + 1)
                move_rows(b, lambda n: pool.indirect_dma_start(
                    out=yb_d[:, :], out_offset=bass.IndirectOffsetOnAxis(ap=dsti[0:n, b:b + 1], axis=0),
                    in_=ye[0:n, a, :], in_offset=None,
                    bounds_check=2 * KSTEP - 1, oob_is_err=False), s_sc[a])

            gather(0, 0)
            gather(1, 1)
            pool.wait_ge(ov_ready, 1)
            mod_rows(3, s_gt2)
            for e in range(E + 2):
                if e + 2 < E:
                    pool.wait_ge(pe_xe, e + 1)
                    gather(e + 2, e % 2)
                if e >= 2:
                    scatter(e - 2, e % 2)
            pool.wait_ge(s_sc[0], 16 * (E // 2))
            pool.wait_ge(s_sc[1], 16 * (E // 2))
            pool.wait_ge(wl_ready, 3 * E)
            pool.engine_nop().then_inc(moe_over, 1)
            pool.wait_ge(ov_ready, 1)
            nov = pool.value_load(ovi[0:1, 0:1], min_val=0, max_val=NOV)
            with pool.If(nov > 0):
                for b in range(NOV):
                    with pool.If(nov > b):
                        gather(E + b, 0)
                        scatter(E + b, 0)
                        pool.wait_ge(s_sc[0], 16 * (E // 2 + b + 1))
            pool.engine_nop().then_inc(moe_over, 1)
            pool.wait_ge(s_gt2, 32)
            for j in range(NT + 2):
                if j < NT:
                    r = ROWS[j]
                    y = ring[0:r, j, 0:D]
                    pool.wait_ge(f_s, j + 1)
                    pool.tensor_tensor(y, y, (modP if j < NP else modS)[3][0:r, :], ALU.mult).then_inc(f_m, 1)
                if j >= 2:
                    x = x_tok[0:ROWS[j - 2], j - 2, :]
                    pool.wait_ge(f_g, j - 1)
                    pool.tensor_tensor(x, x, ln2[0:ROWS[j - 2], 1, :], ALU.add).then_inc(f_o, 1)

        @block.scalar
        def _(act):
            chain = [0]

            def link(ins):
                chain[0] += 1
                ins.then_inc(ac, 1)
                act.wait_ge(ac, chain[0])

            act.wait_ge(pl, NCONST)
            act.wait_ge(pe_c, 1)
            act.activation(cx[:, :], bank[0][:, 0:2 * KD], ACT.Exp, scale=-1.0).then_inc(c_ex, 1)
            act.dma_start(wga[:, :, :], cols(w_in[0], O_GA, RANK)).then_inc(s_misc, 16)
            act.dma_start(a2w[:, :], gla_a2_w[0]).then_inc(s_misc, 16)
            act.dma_start(a2b[:, :], gla_a2_b.to_broadcast([P, H * DK])).then_inc(s_misc, 16)
            act.dma_start(nw[:, :], gla_norm_w.to_broadcast([P, DV])).then_inc(s_misc, 16)
            act.dma_start(sinks[:, :], swa_sinks.to_broadcast([P, NQ])).then_inc(s_misc, 16)
            act.dma_start(kc[:, :], cache_swa_k[0, 0].rearrange("t h d -> t (h d)")).then_inc(s_kc, 16)
            act.dma_start(svt[:, NP, :], cache_swa_v[0, 0].rearrange("t h d -> t (h d)")).then_inc(s_misc, 16)
            act.dma_start(S[:, NCH + 1, :, :], state_gla[0, 0].rearrange("(a h) k v -> (h k) a v", a=2)).then_inc(s_misc, 16)
            act.dma_start(rw[:, :, 0:NG], cols(router_g_w[0], 0, NG)).then_inc(s_misc2, 16)
            for g in range(NG):
                act.dma_start(rw[:, :, NG + g * NE:NG + (g + 1) * NE], cols(router_e_w[0, g], 0, NE)).then_inc(s_misc2, 16)
            act.dma_start(rb[:, 0:NG], router_g_b.to_broadcast([P, NG])).then_inc(s_misc2, 16)
            act.dma_start(rb[:, NG:NG + E], router_e_b.rearrange("o g e -> o (g e)").to_broadcast([P, E])).then_inc(s_misc2, 16)
            for q in range(2 * NT):
                j, half = q // 2, q % 2
                act.wait_ge(pe_xt, q + 1)
                r = ROWS[j]
                act.activation(hT[:, 4 * half:4 * half + 4, tok(j)],
                               bank[1 + q % 2][:, 0:4 * r].rearrange("p (k t) -> p k t", k=4), ACT.Copy).then_inc(xt_ev, 1)
            dests = [gaT] + [gq[:, 0], gq[:, 1], gk[:, 0], gk[:, 1]] + [sqT[:, i] for i in range(4)] + [skT]

            def evac_t(tb):
                act.wait_ge(pe_t, tb + 1)
                d = dests[tb]
                m = RANK if tb == 0 else P
                s = DK ** -0.5 if tb in (1, 2) else 1.0
                c = t_cut(tb)
                off = c + (WIN if tb == 9 else 0)
                act.activation(d[0:m, 0:c], bank[1 + tb % 2][0:m, 0:c], ACT.Copy, scale=s).then_inc(t_ev, 1)
                act.activation(d[0:m, off:off + T - c], bank[5 + tb % 2][0:m, 0:T - c], ACT.Copy, scale=s).then_inc(t_ev, 1)

            act.wait_ge(s_misc, 16 * 7)
            act.activation(wga_r[:, 0, :, :], wga[:, :, :], ACT.Copy).then_inc(ga_high, 1)
            for k in range(KD):
                act.wait_ge(h_ready, 2 * (k + 1))
                act.activation(hH[:, k, :], hT[:, k, :], ACT.Copy).then_inc(h_high, 1)

            def high_unit(q):
                n = NA1 + q
                act.wait_ge(full[place(n)], full_count(n))
                if q >= 2:
                    act.wait_ge(*freed(n - 2))
                act.activation(wH[q % 2], slot(n), ACT.Copy).then_inc(iw_h, 1)

            high_unit(0)
            high_unit(1)
            for tb in range(3):
                evac_t(tb)
            high_unit(2)
            evac_t(3)
            act.wait_ge(z_abs, 1)
            link(act.activation(zt, zt, ACT.Exp, scale=-1.0))
            act.activation(zt, zt, ACT.Ln, bias=1.0).then_inc(z_ln, 1)
            evac_t(4)
            high_unit(3)
            evac_t(5)
            evac_t(6)
            high_unit(4)
            act.wait_ge(b_ready, 2)
            act.activation(eb, bc, ACT.Exp).then_inc(e_ready, 1)
            act.activation(ebn, bc, ACT.Exp, scale=-1.0).then_inc(e_ready, 1)
            act.activation(ed, ed, ACT.Exp).then_inc(e_ready, 1)
            evac_t(7)
            evac_t(8)
            high_unit(5)
            evac_t(9)
            act.wait_ge(pe_t, 11)
            act.activation(skT[:, LP:LP + WIN], bank[1][:, 0:WIN], ACT.Copy).then_inc(t_ev, 1)

            def win(j):
                return (P, KW) if j == 0 else (0, KW) if j < NP else (0, WIN + LS)

            def probs(j):
                r = ROWS[j]
                lo, hi = win(j)
                act.wait_ge(m_ready, j + 1)
                c = 16 + 32 * (j % 2)
                for h in range(NQ):
                    sc = Ssc[j % 2][0:r, h, 0:hi - lo]
                    act.activation(sc, sc, ACT.Exp, bias=small[0:r, c + 8 + h:c + 9 + h],
                                   accum_out=small[0:r, c + 16 + h:c + 17 + h]).then_inc(p_exp, 1)
                act.activation(small[0:r, c + 24:c + 32], small[0:r, c + 24:c + 32], ACT.Exp).then_inc(p_exp, 1)

            def evac_pt(j):
                r = ROWS[j]
                nb = 1 if j == 0 else 2
                for f in range(4):
                    act.wait_ge(pe_pt, 4 * j + f + 1)
                    if f == 0:
                        act.wait_ge(pe_pv, j)
                    src = bank[5 + f % 2][:, 0:2 * nb * r].rearrange("p (h b q) -> p h b q", h=2, b=nb)
                    if j < NP:
                        act.activation(PT[:, 2 * f:2 * f + 2, 0:nb, 0:r], src, ACT.Copy).then_inc(pt_ev, 1)
                    else:
                        link(act.activation(PT[:, 2 * f:2 * f + 2, 0, 0:r], src[:, :, 0, :], ACT.Copy))
                        act.activation(PT[0:LS, 2 * f:2 * f + 2, 1, 0:r], src[0:LS, :, 1, :], ACT.Copy).then_inc(pt_ev, 1)

            def evac_pv(j):
                act.wait_ge(pe_pv, j + 1)
                act.activation(mixS[:, :, tok(j)], bank[7][:, 0:4 * ROWS[j]].rearrange("p (k t) -> p k t", k=4),
                               ACT.Copy).then_inc(pv_ev, 1)

            high_unit(SPLIT_AT[-1])
            for j in range(NT + 1):
                if j >= 1:
                    evac_pt(j - 1)
                if j < NT:
                    probs(j)
                if j >= 1:
                    evac_pv(j - 1)
                if j in SPLIT_AT:
                    high_unit(SPLIT_AT[j])

            for j in range(NT):
                act.wait_ge(pe_kd, j + 1)
                if j >= 2:
                    act.wait_ge(pe_u, j - 1)
                act.activation(kdT[0:ROWS[j], j % 2, :], bank[0][0:ROWS[j], 0:2 * P], ACT.Copy).then_inc(kd_ev, 1)

            def mix_stats(j):
                r = ROWS[j]
                act.wait_ge(pe_o, j + 1)
                if j >= 2:
                    act.wait_ge(og_ready, j - 1)
                o4 = osb[0:r, j % 2, :].rearrange("p (a b v) -> p a b v", a=2, b=2)
                for par in range(2):
                    act.activation(o4[:, :, par, :], bank[3 + par][0:r, 0:2 * DV].rearrange("p (a v) -> p a v", a=2),
                                   ACT.Copy).then_inc(o_ev, 1)
                act.wait_ge(o_ev, 2 * (j + 1))
                for h in range(H):
                    link(act.activation(gex[0:r, j % 2, h * DV:(h + 1) * DV], osb[0:r, j % 2, h * DV:(h + 1) * DV], ACT.Square,
                                        accum_out=small[0:r, 8 * (j % 2) + h:8 * (j % 2) + h + 1]))
                ss = small[0:r, 8 * (j % 2):8 * (j % 2) + H]
                link(act.activation(ss, ss, ACT.Ln, scale=1.0 / DV, bias=epst[0:r, 0:1]))
                link(act.activation(ss, ss, ACT.Exp, scale=-0.5))
                act.wait_ge(tok_ev, 25)
                act.activation(gex[0:r, j % 2, :], grg[0:r, j, :], ACT.Exp, scale=-1.0).then_inc(o_sq, 1)

            def evac_og(j):
                act.wait_ge(pe_og, j + 1)
                act.activation(mixT[:, 0:4, tok(j)], bank[5][:, 0:4 * ROWS[j]].rearrange("p (k t) -> p k t", k=4),
                               ACT.Copy).then_inc(mg_ev, 1)

            for j in range(NT + 3):
                if j >= 3:
                    evac_og(j - 3)
                if 1 <= j <= NT:
                    mix_stats(j - 1)

            def rstd(j):
                act.wait_ge(v_ready, j + 1)
                v = stat[0:ROWS[j], j % 2, 13:14]
                link(act.activation(v, v, ACT.Ln, bias=epst[0:ROWS[j], 0:1]))
                act.activation(v, v, ACT.Exp, scale=-0.5).then_inc(v_ln, 1)

            def evac_h2(j):
                r = ROWS[j]
                act.wait_ge(h2_ready, j + 1)
                act.dma_start(h2_d[P * j:P * j + r, :], h2[0:r, j % 2, :]).then_inc(h2_st[j % 2], 16)
                for half in range(2):
                    act.wait_ge(pe_ht, 2 * j + half + 1)
                    if half == 0:
                        act.wait_ge(pe_rt, j)
                    act.activation(h2Tt[:, 4 * half:4 * half + 4, 0:r],
                                   bank[5 + half][:, 0:4 * r].rearrange("p (k t) -> p k t", k=4), ACT.Copy).then_inc(ht_ev, 1)

            def evac_gt2(i):
                act.wait_ge(pe_mod, NA2 + i + 1)
                act.activation(gt2st[:, i * UC:(i + 1) * UC], bank[3 + i % 2][0:2, 0:UC], ACT.Copy).then_inc(gt2_ev, 1)

            for j in range(NT + 1):
                if j >= 1:
                    evac_h2(j - 1)
                if j < NT:
                    rstd(j)
                if j >= NT - 1:
                    evac_gt2(2 * (j - NT + 1))
                    evac_gt2(2 * (j - NT + 1) + 1)
            act.wait_ge(r_ex0, 1)
            link(act.activation(rt[:, 0, 0:NT * NG], rt[:, 0, 0:NT * NG], ACT.Exp))
            act.activation(rs[:, 5, :], rs[:, 5, :], ACT.Exp).then_inc(r_ex, 1)

            def high_w(r, src, used):
                if used is not None:
                    act.wait_ge(*used)
                act.activation(wsplit[:, r, 0, :], src, ACT.Copy).then_inc(wh_ready, 1)

            def expert_w(e, r, i):
                n = N0 + 3 * e + r
                act.wait_ge(full[place(n)], at(expert_count(n), 16, i))
                high_w(r, slot(n), ((pe_g, pe_gu, pe_dn)[r], at(e, 2, i)) if e >= 1 or i is not None else None)

            def high_x(a, w):
                act.wait_ge(pe_xe, w)
                for half in range(2):
                    act.activation(xh[:, a, 4 * half:4 * half + 4, :], bank[half][:, :].rearrange("p (k t) -> p k t", k=4),
                                   ACT.Copy).then_inc(xe_a, 1)

            def silu(a, w):
                act.wait_ge(pe_gu, w)
                act.activation(sgl[:, a, :], bank[2 + a][:, 0:FF], ACT.Silu).then_inc(sg_done, 1)

            def high_h(a, w):
                act.wait_ge(pe_hT, w)
                act.activation(hh[:, a, :, :], bank[4][:, 0:FF].rearrange("p (k t) -> p k t", k=NF), ACT.Copy).then_inc(hT_ev, 1)

            def evac_y(a, w, free):
                act.wait_ge(pe_dn, w)
                if free is not None:
                    act.wait_ge(s_sc[a], free)
                act.activation(ye[:, a, 0:512], bank[5][:, :], ACT.Copy).then_inc(y_a, 1)

            def step(e, i, last=False):
                a, b = e % 2, (e - 1) % 2
                high_h(b, at(e, 2, i))
                if not last:
                    high_x(b, at(e + 2, 2, i))
                    expert_w(e + 1, 0, i)
                silu(a, at(e + 1, 2, i))
                if not last:
                    expert_w(e + 1, 1, i)
                evac_y(b, at(e, 2, i), at(16 * ((e - 1) // 2), 16, i) if e >= 3 or i is not None else None)
                expert_w(e, 2, i)

            act.wait_ge(pe_y, NT)
            act.wait_ge(h2_ready, NT)
            expert_w(0, 0, None)
            expert_w(0, 1, None)
            act.wait_ge(tbl_ready, 1)
            high_x(0, 1)
            high_x(1, 2)
            expert_w(1, 0, None)
            silu(0, 1)
            expert_w(1, 1, None)
            expert_w(0, 2, None)
            step(1, None)
            step(2, None)
            with act.Fori(1, E // 2 - 1) as i:
                step(1, i)
                step(2, i)
            step(E - 1, None, last=True)
            high_h(1, E)
            evac_y(1, E, 16 * (E // 2 - 1))
            act.wait_ge(ov_ready, 1)
            nov = act.value_load(ovi[0:1, 0:1], min_val=0, max_val=NOV)
            with act.If(nov > 0):
                with act.Fori(0, nov) as i:
                    act.wait_ge(o_w, i * 48 + 48)
                    act.wait_ge(pe_dn, i + E)
                    for r in range(3):
                        high_w(r, ring[:, r, :], None)
                    high_x(0, i + E + 1)
                    silu(0, i + E + 1)
                    high_h(0, i + E + 1)
                    evac_y(0, i + E + 1, i * 16 + 16 * (E // 2))

            def scale_first(j):
                r = ROWS[j]
                act.wait_ge(s_fin[j], 16)
                act.activation(ring[0:r, j, 0:D], ring[0:r, j, 0:D], ACT.Copy, scale=wts[0:r, 0, j:j + 1]).then_inc(f_a, 1)

            def normalise(j):
                r = ROWS[j]
                act.wait_ge(f_v, j + 1)
                mean, v = stat[0:r, j % 2, 12:13], stat[0:r, j % 2, 13:14]
                link(act.activation(v, v, ACT.Ln, bias=epst[0:r, 0:1]))
                link(act.activation(v, v, ACT.Exp, scale=-0.5))
                link(act.activation(mean, mean, ACT.Copy, scale=v))
                link(act.mul(mean, mean, -1.0))
                act.activation(x_tok[0:r, j, :], x_tok[0:r, j, :], ACT.Identity, scale=v, bias=mean).then_inc(f_l, 1)

            scale_first(0)
            scale_first(1)
            for j in range(NT):
                if j + 2 < NT:
                    scale_first(j + 2)
                normalise(j)

        @block.tensor
        def _(pe):
            pe.wait_ge(pl, NCONST)
            pe.wait_ge(s_c, 32)
            pe.transpose(bank[0][:, 0:2 * KD], crow[:, :], ident[0:2 * KD, 0:2 * KD]).then_inc(pe_c, 1)
            pe.wait_ge(cs_ready, 1)
            pe.wait_ge(s_adab, 16)
            cs3 = csT[:, :].rearrange("p (b k) -> p b k", b=2)

            def wait_unit(n):
                pe.wait_ge(full[place(n)], full_count(n))

            def ada(u, bk):
                n = number[("ada", u)]
                wait_unit(n)
                w = slot_view(n, KD)
                pe.matmul(bank[bk][0:2, 0:UC], ident[0:NA, u:u + 1].to_broadcast([NA, 2]), adab[:, :], start=True, stop=False)
                for k in range(KD):
                    mm = pe.matmul(bank[bk][0:2, 0:UC], cs3[:, :, k], w[:, k, :], start=False, stop=(k == KD - 1))
                mm.then_inc(pe_mod, 1)

            ada(0, 3)
            ada(1, 4)
            pe.wait_ge(s_x, 32)
            for q in range(2 * NT):
                j, half = q // 2, q % 2
                r = ROWS[j]
                if q >= 2:
                    pe.wait_ge(xt_ev, q - 1)
                for k in range(4):
                    kk = 4 * half + k
                    mm = pe.transpose(bank[1 + q % 2][:, k * r:(k + 1) * r], x_tok[0:r, j, kk * P:(kk + 1) * P], ident[0:r, 0:r])
                mm.then_inc(pe_xt, 1)
            for u in range(2, NA1):
                pe.wait_ge(ada_ev, u - 1)
                ada(u, 3 + u % 2)
            pe.wait_ge(ada_ev, NA1)
            for i in range(2 * KD):
                mm = pe.transpose(bank[0][:, 32 + 2 * i:34 + 2 * i], modst[:, i * P:(i + 1) * P], ident[0:2, 0:2])
            mm.then_inc(pe_sc, 1)

            PARTS = ((0, 0), (0, 1), (1, 0))
            hHL = (hH, hL)

            def unit_parts(q):
                return wH[q % 2].rearrange("p (k n) -> p k n", k=KD), ring_r[:, place(NA1 + q), :].rearrange("p (k n) -> p k n", k=KD)

            def proj_t(tb, w, cs):
                m = RANK if tb == 0 else P
                if tb >= 2:
                    pe.wait_ge(t_ev, 2 * (tb - 1))
                for bk, ts in ((1, slice(0, t_cut(tb))), (5, slice(t_cut(tb), T))):
                    for ph, pw in PARTS:
                        for k in range(KD):
                            mm = pe.matmul(bank[bk + tb % 2][0:m, 0:ts.stop - ts.start], w[pw][:, k, cs], hHL[ph][:, k, ts],
                                           start=(ph + pw == 0 and k == 0), stop=(ph == 1 and k == KD - 1))
                return mm

            pe.wait_ge(s_misc, 16 * 7)
            pe.wait_ge(h_low, KD + 1)
            proj_t(0, (wga_r[:, 0, :, :], wga_r[:, 1, :, :]), slice(0, RANK)).then_inc(pe_t, 1)
            tb = 1
            for q, kind in enumerate(("gq", "gk")):
                pe.wait_ge(iw_l, q + 1)
                for b in range(2):
                    proj_t(tb, unit_parts(q), slice(b * P, (b + 1) * P)).then_inc(pe_t, 1)
                    tb += 1
                if kind == "gq":
                    pe.wait_ge(t_ev, 2)
                    for j in range(NT):
                        if j >= 2:
                            pe.wait_ge(z_ev, j - 1)
                        pe.matmul(bank[7 if j % 2 == 0 else 0][0:ROWS[j], 0:H * DK], gaT[:, tok(j)], a2w[:, :],
                                  start=True, stop=True).then_inc(pe_z, 1)
            pe.wait_ge(l_ready, 1)
            for j in range(NT):
                r = ROWS[j]
                pe.wait_ge(z_ev, 5 + j - 1 if j >= 1 else 5)
                for half in range(2):
                    mm = pe.matmul(bank[7 if j % 2 == 0 else 0][:, half * r:(half + 1) * r], z[0:r, j, half * P:(half + 1) * P],
                                   tri[0:r, 0:r], start=True, stop=True)
                mm.then_inc(pe_z, 1)
            for q in (2, 3):
                pe.wait_ge(iw_l, q + 1)
                for b in range(2):
                    proj_t(tb, unit_parts(q), slice(b * P, (b + 1) * P)).then_inc(pe_t, 1)
                    tb += 1
            pe.wait_ge(iw_l, 5)
            proj_t(tb, unit_parts(4), slice(0, 2 * HD)).then_inc(pe_t, 1)
            pe.wait_ge(s_kc, 16)
            pe.wait_ge(t_ev, 18)
            pe.transpose(bank[1][:, 0:WIN], kc[:, :], ident[:, :]).then_inc(pe_t, 1)

            def proj_tok(m):
                kind, j = TOK[m]
                q = 4 + m // NT
                pe.wait_ge(iw_l, q + 1)
                w = unit_parts(q)
                r = ROWS[j]
                c0 = 0 if kind != "kv" or j >= NP - 1 else 2 * HD
                if m >= 2:
                    pe.wait_ge(tok_ev, m - 1)
                for ph, pw in PARTS:
                    for k in range(KD):
                        mm = pe.matmul(bank[3 + m % 2][0:r, 0:UC - c0], hHL[ph][:, k, tok(j)], w[pw][:, k, c0:UC],
                                       start=(ph + pw == 0 and k == 0), stop=(ph == 1 and k == KD - 1))
                mm.then_inc(pe_tok, 1)

            def fill(j, f):
                if (j, f) in TOK_AT:
                    proj_tok(TOK_AT[(j, f)])

            for m in range(NT):
                proj_tok(m)

            def qk(j, g):
                r = ROWS[j]
                k0, k1 = (0, P) if j == 0 else (P * (j - 1), P * (j + 1)) if j < NP else (LP, LP + WIN + LS)
                n = k1 - k0
                for par in range(2):
                    f = 4 * j + 2 * g + par
                    if f >= 2:
                        pe.wait_ge(s_ev, f - 1)
                    q0 = par * HD
                    for a in range(2):
                        mm = pe.matmul(bank[1 + par][0:r, a * KW:a * KW + n], sqT[q0:q0 + HD, 2 * g + a, tok(j)],
                                       skT[q0:q0 + HD, k0:k1], start=True, stop=True)
                    mm.then_inc(pe_qk, 1)

            def key_blocks(j):
                return [(0, P)] if j == 0 else [(0, P), (P, P)] if j < NP else [(0, P), (P, LS)]

            def pt(j, fs):
                r = ROWS[j]
                pe.wait_ge(p_ready, j + 1)
                nb = len(key_blocks(j))
                for f in fs:
                    if 4 * j + f >= 2:
                        pe.wait_ge(pt_ev, 4 * j + f - 1)
                    for h in range(2):
                        for b, (kb, kn) in enumerate(key_blocks(j)):
                            c = (h * nb + b) * r
                            mm = pe.transpose(bank[5 + f % 2][0:kn, c:c + r], Ssc[j % 2][0:r, 2 * f + h, kb:kb + kn], ident[0:r, 0:r])
                    mm.then_inc(pe_pt, 1)

            def pv(j):
                r = ROWS[j]
                pe.wait_ge(pt_ev, 4 * (j + 1))
                if j >= 1:
                    pe.wait_ge(pv_ev, j)
                tiles = [0] if j == 0 else [j - 1, j] if j < NP else [NP, NP + 1]
                for i in range(4):
                    for g in range(2):
                        for b, (kb, kn) in enumerate(key_blocks(j)):
                            mm = pe.matmul(bank[7][g * HD:(g + 1) * HD, i * r:(i + 1) * r], svt[0:kn, tiles[b], g * HD:(g + 1) * HD],
                                           PT[0:kn, 4 * g + i, b, 0:r], start=(b == 0), stop=(b == len(tiles) - 1))
                mm.then_inc(pe_pv, 1)

            pe.wait_ge(t_ev, 21)
            for j in range(NT + 1):
                if j < NT:
                    qk(j, 0)
                fill(j, 0)
                if j < NT:
                    qk(j, 1)
                fill(j, 1)
                if j >= 1:
                    pt(j - 1, (0, 1))
                fill(j, 2)
                if j >= 1:
                    pt(j - 1, (2, 3))
                fill(j, 3)
                if j >= 1:
                    pv(j - 1)

            pe.wait_ge(gla_ready, 1)
            pe.wait_ge(pv_ev, NT)
            for j in range(NT + 1):
                if j < NT:
                    r = ROWS[j]
                    pe.wait_ge(kd_ev, j) if j >= 1 else pe.wait_ge(z_ev, 10)
                    for half in range(2):
                        mm = pe.transpose(bank[0][0:r, half * P:(half + 1) * P], ed[:, half, tok(j)], ident[:, :])
                    mm.then_inc(pe_kd, 1)
                if j >= 1:
                    i = j - 1
                    pe.wait_ge(kd_ev, i + 1)
                    pe.wait_ge(tok_ev, 15)
                    if i >= 1:
                        pe.wait_ge(u_ev, i)
                    for c in range(2 if i < NP else 1):
                        r0 = c * CH
                        r1 = r0 + min(CH, ROWS[i])
                        for h in range(H):
                            mm = pe.matmul(bank[6 + c][(h % 2) * DK:(h % 2 + 1) * DK, (h // 2) * DV:(h // 2 + 1) * DV],
                                           kdT[r0:r1, i % 2, h * DK:(h + 1) * DK], gv[r0:r1, i, h * DV:(h + 1) * DV],
                                           start=True, stop=True)
                    mm.then_inc(pe_u, 1)
                if j < NT:
                    u = ADA_STATE[j]
                    pe.wait_ge(tok_ev, 25) if j < 2 else pe.wait_ge(ada_ev, u - 1)
                    ada(u, 3 + u % 2)

            def gla_scores(j):
                r = ROWS[j]
                if j >= 1:
                    pe.wait_ge(a_ev, j)
                for par in range(2):
                    q0 = par * DK
                    for a in range(2):
                        for up in range(2):
                            ks, qs = (ebn, eb) if up == 0 else (bc, gq)
                            mm = pe.matmul(bank[1 + par][0:r, (2 * up + a) * P:(2 * up + a) * P + r],
                                           ks[q0:q0 + DK, a, tok(j)], qs[q0:q0 + DK, a, tok(j)], start=True, stop=True)
                mm.then_inc(pe_a, 1)

            def gla_out(j):
                r = ROWS[j]
                pe.wait_ge(a_ev, j + 1)
                pe.wait_ge(u_ev, j + 1)
                if j >= 1:
                    pe.wait_ge(o_sq, j)
                else:
                    pe.wait_ge(ada_ev, NA1 + NT)
                for par in range(2):
                    for a in range(2):
                        h = 2 * a + par
                        out = bank[3 + par][:, a * DV:(a + 1) * DV]
                        pe.matmul(out[0:r, :], At[0:r, j % 2, h, 0:r], gv[0:r, j, h * DV:(h + 1) * DV], start=True, stop=False)
                        for c in range(2 if j < NP else 1):
                            n = 2 * j + c if j < NP else NCH + 1
                            c0, cn = c * CH, min(CH, r)
                            mm = pe.matmul(out[c0:c0 + cn, :], eb[par * DK:(par + 1) * DK, a, P * j + c0:P * j + c0 + cn],
                                           S[par * DK:(par + 1) * DK, n, a, :], start=False, stop=True)
                mm.then_inc(pe_o, 1)

            def gla_turn(j):
                r = ROWS[j]
                pe.wait_ge(og_ready, j + 1)
                if j >= 1:
                    pe.wait_ge(mg_ev, j)
                for k in range(4):
                    mm = pe.transpose(bank[5][:, k * r:(k + 1) * r], og[0:r, k * P:(k + 1) * P], ident[0:r, 0:r])
                mm.then_inc(pe_og, 1)

            pe.wait_ge(kd_ev, NT)
            pe.wait_ge(u_ev, NT)
            def out_proj(j):
                r = ROWS[j]
                pe.wait_ge(mg_ev, j + 1)
                if j == 0:
                    pe.wait_ge(pv_ev, NT)
                if j == 1:
                    pe.wait_ge(o_ev, 2 * NT)
                if j >= 2:
                    pe.wait_ge(y_ev, 2 * (j - 1))
                for u in range(KD // 2):
                    n = number[("wo", u)]
                    wait_unit(n)
                    v = slot_view(n, 2)
                    for kk in range(2):
                        k = 2 * u + kk
                        for half in range(2):
                            mix = mixT[:, k, tok(j)] if k < H else mixS[:, k - H, tok(j)]
                            mm = pe.matmul(bank[1 + 2 * (j % 2) + half][0:r, :], mix, v[:, kk, half * 512:(half + 1) * 512],
                                           start=(k == 0), stop=(k == KD - 1))
                    if j == NT - 1 and u < KD // 2 - 1:
                        mm.then_inc(wo_used, 1)
                mm.then_inc(pe_y, 1)

            for j in range(NT + 3):
                if j < NT:
                    gla_scores(j)
                if j == NT + 2:
                    out_proj(0)
                if j >= 3:
                    gla_turn(j - 3)
                if 2 <= j < NT + 2:
                    pe.wait_ge(ada_ev, ADA_GLA[j] - 1)
                if j < NT + 2:
                    ada(ADA_GLA[j], 6 * (j % 2))
                if 1 <= j <= NT:
                    gla_out(j - 1)

            def route(j):
                r = ROWS[j]
                pe.wait_ge(h2_ready, j + 1)
                for half in range(2):
                    if j >= 1:
                        pe.wait_ge(ht_ev, 2 * j)
                    for k in range(4):
                        kk = 4 * half + k
                        mm = pe.transpose(bank[5 + half][:, k * r:(k + 1) * r], h2[0:r, j % 2, kk * P:(kk + 1) * P], ident[0:r, 0:r])
                    mm.then_inc(pe_ht, 1)
                pe.wait_ge(ht_ev, 2 * (j + 1))
                if j >= 1:
                    pe.wait_ge(rt_ev, j)
                for k in range(KD):
                    mm = pe.matmul(bank[7][0:r, 0:NG + E], h2Tt[:, k, 0:r], rw[:, k, :], start=(k == 0), stop=(k == KD - 1))
                mm.then_inc(pe_rt, 1)

            pe.wait_ge(s_misc2, 16 * (NG + 3))
            for j in range(1, NT):
                out_proj(j)
                if j == 1:
                    pe.wait_ge(mg_ev, NT)
                route(j - 1)
            pe.wait_ge(y_ev, 2 * (NT - 1))
            ada(NA2, 3)
            ada(NA2 + 1, 4)
            pe.wait_ge(gt2_ev, 1)
            ada(NA2 + 2, 3)
            route(NT - 1)
            pe.wait_ge(gt2_ev, 2)
            ada(NA2 + 3, 4)

            pe.wait_ge(oh_ready, 1)
            M = rt[:, 3, :].rearrange("p (j e) -> p j e", j=NT)
            for j in range(NT):
                for i in range(j + 1):
                    lhs = before if i == j else ones
                    mm = pe.matmul(bank[0][:, j * E:(j + 1) * E], lhs[0:ROWS[i], :], M[0:ROWS[i], i, :], start=(i == 0), stop=(i == j))
            for i in range(NT):
                mm = pe.matmul(bank[0][:, NT * E:(NT + 1) * E], ones[0:ROWS[i], :], M[0:ROWS[i], i, :], start=(i == 0), stop=(i == NT - 1))
            mm.then_inc(pe_rank, 1)
            pe.wait_ge(s_trow, 16)
            pe.transpose(bank[7][:, 0:NBLK], trow[:, :], ident[0:NBLK, 0:NBLK]).then_inc(pe_tbl, 1)

            def turn_x(a, gw):
                pe.wait_ge(s_g[a], gw)
                for k in range(KD):
                    mm = pe.transpose(bank[k // 4][:, (k % 4) * P:(k % 4 + 1) * P], xg[:, a, k * P:(k + 1) * P], ident[:, :])
                mm.then_inc(pe_xe, 1)

            def wview(r, part, kd):
                return wsplit[:, r, part, :].rearrange("p (k n) -> p k n", k=kd)

            def product(r, a, lows):
                pe.wait_ge(wl_ready, lows)
                out, done = ((0, pe_g), (FF, pe_gu))[r]
                for px, pw in PARTS:
                    x, w = (xh, xl)[px], wview(r, pw, KD)
                    for k in range(KD):
                        mm = pe.matmul(bank[2 + a][:, out:out + FF], x[:, a, k, :], w[:, k, :],
                                       start=(px + pw == 0 and k == 0), stop=(px == 1 and k == KD - 1))
                mm.then_inc(done, 1)

            def turn_h(a):
                for k in range(NF):
                    mm = pe.transpose(bank[4][:, k * P:(k + 1) * P], hid[:, a, k * P:(k + 1) * P], ident[:, :])
                mm.then_inc(pe_hT, 1)

            def down(a, lows):
                pe.wait_ge(wl_ready, lows)
                for px, pw in PARTS:
                    h, w = (hh, hl)[px], wview(2, pw, NF)
                    for k in range(NF):
                        for half in range(2):
                            mm = pe.matmul(bank[5 + half][:, :], h[:, a, k, :], w[:, k, half * 512:(half + 1) * 512],
                                           start=(px + pw == 0 and k == 0), stop=(px == 1 and k == NF - 1))
                mm.then_inc(pe_dn, 1)

            def expert_gate(e, i):
                pe.wait_ge(xe_l, at(2 * (e + 1), 4, i))
                if e >= 2 or i is not None:
                    pe.wait_ge(hid_done, at(e - 1, 2, i))
                product(0, e % 2, at(low_count(e, 0), 6, i))

            def expert_up(e, i):
                product(1, e % 2, at(low_count(e, 1), 6, i))

            def expert_turn(e, i):
                pe.wait_ge(hid_done, at(e + 1, 2, i))
                if e >= 1:
                    pe.wait_ge(hT_l, at(e, 2, i))
                turn_h(e % 2)

            def rows_turn(e, i):
                pe.wait_ge(xe_l, at(2 * e, 4, i))
                turn_x(e % 2, at(16 * (e // 2 + 1), 16, i))

            def expert_down(e, i):
                pe.wait_ge(hT_l, at(e + 1, 2, i))
                if e >= 1 or i is not None:
                    pe.wait_ge(y_a, at(e, 2, i))
                    pe.wait_ge(y_d, at(e, 2, i))
                down(e % 2, at(low_count(e, 2), 6, i))

            def step(e, i):
                expert_gate(e, i)
                expert_turn(e - 1, i)
                rows_turn(e + 1, i)
                expert_up(e, i)
                expert_down(e - 1, i)

            pe.wait_ge(tbl_ready, 1)
            turn_x(0, 16)
            expert_gate(0, None)
            rows_turn(1, None)
            expert_up(0, None)
            step(1, None)
            step(2, None)
            with pe.Fori(1, E // 2 - 1) as i:
                step(1, i)
                step(2, i)
            expert_gate(E - 1, None)
            expert_turn(E - 2, None)
            expert_up(E - 1, None)
            expert_down(E - 2, None)
            expert_turn(E - 1, None)
            expert_down(E - 1, None)
            pe.wait_ge(ov_ready, 1)
            nov = pe.value_load(ovi[0:1, 0:1], min_val=0, max_val=NOV)
            with pe.If(nov > 0):
                with pe.Fori(0, nov) as i:
                    turn_x(0, i * 16 + 16 * (E // 2) + 16)
                    pe.wait_ge(xe_l, i * 2 + 2 * E + 2)
                    product(0, 0, i * 3 + 3 * E + 1)
                    product(1, 0, i * 3 + 3 * E + 2)
                    pe.wait_ge(hid_done, i + E + 1)
                    turn_h(0)
                    pe.wait_ge(hT_l, i + E + 1)
                    down(0, i * 3 + 3 * E + 3)

        @block.vector
        def _(dve):
            chain = [0]

            def link(ins):
                chain[0] += 1
                ins.then_inc(dv, 1)
                dve.wait_ge(dv, chain[0])

            def bcast(ap, shape):
                return ap.broadcast_to(shape)

            dve.wait_ge(pl, NCONST)
            link(dve.scalar_tensor_tensor(dist[:, :], dist[:, :], -1.0, dist[:, :], ALU.mult, ALU.max))
            link(dve.memset(dist[0:CH, WIN + CH:KW], 1e32))
            link(dve.memset(dist[CH:P, 0:CH], 1e32))
            for h in range(NQ):
                dve.tensor_scalar(biasH[:, h, :], dist[:, :], -(2.0 ** (-(8.0 / NQ) * (h + 1))), None, ALU.mult)
            dve.wait_ge(c_ex, 1)
            link(dve.tensor_scalar(cx[:, :], cx[:, :], 1.0, None, ALU.add))
            link(dve.reciprocal(cx[:, :], cx[:, :]))
            dve.tensor_tensor(csT[:, :], bank[0][:, 0:2 * KD], cx[:, :], ALU.mult).then_inc(cs_ready, 1)

            def mod_evac(u, bk):
                dve.wait_ge(pe_mod, u + 1)
                if u >= 2 * NA1:
                    dve.wait_ge(s_mod, 16)
                dve.tensor_copy(modst[:, (u % NA1) * UC:(u % NA1 + 1) * UC], bank[bk][0:2, 0:UC]).then_inc(ada_ev, 1)

            for u in range(NA1):
                mod_evac(u, 3 + u % 2)
            dve.wait_ge(pe_sc, 1)
            link(dve.tensor_copy(shsc[:, 0:2 * KD], bank[0][:, 32:32 + 2 * KD]))
            link(dve.tensor_scalar(shsc[:, 2 * KD:4 * KD], bank[0][:, 32 + 2 * KD:32 + 4 * KD], 1.0, None, ALU.add))
            dve.wait_ge(xt_ev, 2 * NT)
            for k in range(KD):
                for b, cs in ((0, slice(0, LP)), (1, slice(LP, T))):
                    dve.tensor_scalar(hT[:, k, cs], hT[:, k, cs], shsc[:, 2 * KD + 2 * k + b:2 * KD + 2 * k + b + 1],
                                      shsc[:, 2 * k + b:2 * k + b + 1], ALU.mult, ALU.add).then_inc(h_ready, 1)
            dve.wait_ge(ga_high, 1)
            dve.tensor_tensor(wga_r[:, 1, :, :], wga[:, :, :], wga_r[:, 0, :, :].bitcast(f32), ALU.subtract).then_inc(h_low, 1)
            for k in range(KD):
                dve.wait_ge(h_high, k + 1)
                dve.tensor_tensor(hL[:, k, :], hT[:, k, :], hH[:, k, :].bitcast(f32), ALU.subtract).then_inc(h_low, 1)

            def low_unit(q):
                dve.wait_ge(iw_h, q + 1)
                dve.tensor_tensor(ring_r[:, place(NA1 + q), :], slot(NA1 + q), wH[q % 2].bitcast(f32), ALU.subtract).then_inc(iw_l, 1)

            low_unit(0)
            low_unit(1)
            dve.wait_ge(s_misc, 16 * 7)
            for j in range(NT):
                r = ROWS[j]
                dve.wait_ge(pe_z, j + 1)
                dve.tensor_tensor(z[0:r, j, :], bank[7 if j % 2 == 0 else 0][0:r, 0:H * DK], a2b[0:r, :], ALU.add).then_inc(z_ev, 1)
            low_unit(2)
            dve.wait_ge(z_ev, NT)
            dve.scalar_tensor_tensor(zt, z, -1.0, z, ALU.mult, ALU.max).then_inc(z_abs, 1)
            dve.wait_ge(z_ln, 1)
            dve.scalar_tensor_tensor(z, z, 0.0, zt, ALU.min, ALU.subtract).then_inc(l_ready, 1)
            for j in range(NT):
                r = ROWS[j]
                dve.wait_ge(pe_z, NT + j + 1)
                dve.tensor_copy(bc[:, :, tok(j)], bank[7 if j % 2 == 0 else 0][:, 0:2 * r].rearrange("p (a t) -> p a t", a=2)).then_inc(z_ev, 1)
            low_unit(3)
            dve.wait_ge(z_ev, 2 * NT)
            for a in range(2):
                bp = bc[:, a, 0:LP].rearrange("p (n t) -> p n t", t=CH)
                link(dve.tensor_tensor(ed[:, a, 0:LP].rearrange("p (n t) -> p n t", t=CH),
                                       bcast(bp[:, :, CH - 1:CH], [P, NCH, CH]), bp, ALU.subtract))
                dve.tensor_tensor(ed[:, a, LP:T], bcast(bc[:, a, T - 1:T], [P, LS]), bc[:, a, LP:T], ALU.subtract).then_inc(b_ready, 1)
            low_unit(4)
            dve.wait_ge(e_ready, 3)
            dve.wait_ge(t_ev, 10)
            for a in range(2):
                dve.tensor_copy(gend[:, a, 0:NCH], eb[:, a, 0:LP].rearrange("p (n t) -> p n t", t=CH)[:, :, CH - 1])
                link(dve.tensor_copy(gend[:, a, NCH:NCH + 1], eb[:, a, T - 1:T]))
            link(dve.tensor_tensor(bc, gk, eb, ALU.mult))
            link(dve.tensor_tensor(eb, gq, eb, ALU.mult))
            link(dve.tensor_tensor(gq, gq, ebn, ALU.mult))
            link(dve.tensor_tensor(ebn, gk, ebn, ALU.mult))
            dve.tensor_tensor(ed, gk, ed, ALU.mult).then_inc(gla_ready, 1)
            def evac_tok(m):
                kind, j = TOK[m]
                r = ROWS[j]
                dve.wait_ge(pe_tok, m + 1)
                src = bank[3 + m % 2]
                if kind == "kv":
                    i = NP + 1 if j == NP else j
                    if j >= NP - 1:
                        link(dve.tensor_copy(skt[0:r, j - NP + 1, :], src[0:r, 0:2 * HD]))
                        dve.tensor_copy(svt[0:r, i, :], src[0:r, 2 * HD:4 * HD]).then_inc(tok_ev, 1)
                    else:
                        dve.tensor_copy(svt[0:r, i, :], src[0:r, 0:2 * HD]).then_inc(tok_ev, 1)
                else:
                    dst = gv if kind in ("gv0", "gv1") else grg
                    c = UC * int(kind[-1])
                    dve.tensor_copy(dst[0:r, j, c:c + UC], src[0:r, 0:UC]).then_inc(tok_ev, 1)

            def fill(j, f):
                if (j, f) in TOK_AT:
                    evac_tok(TOK_AT[(j, f)])

            low_unit(5)
            for m in range(NT):
                evac_tok(m)

            def stats_of(j):
                return (small[0:ROWS[j], 16 + 32 * (j % 2) + 8 * i:24 + 32 * (j % 2) + 8 * i] for i in range(4))

            def key_window(j):
                return (P, KW) if j == 0 else (0, KW) if j < NP else (0, WIN + LS)

            def scores(j, g):
                r = ROWS[j]
                w0, w1 = key_window(j)
                n = w1 - w0
                sc = Ssc[j % 2]
                if j >= 2 and g == 0:
                    dve.wait_ge(pe_pt, 4 * (j - 1))
                for par in range(2):
                    dve.wait_ge(pe_qk, 4 * j + 2 * g + par + 1)
                    h0 = 4 * par + 2 * g
                    dve.scalar_tensor_tensor(sc[0:r, h0:h0 + 2, 0:n],
                                             bank[1 + par][0:r, :].rearrange("p (a n) -> p a n", a=2)[:, :, 0:n],
                                             HD ** -0.5, biasH[0:r, h0:h0 + 2, w0:w1], ALU.mult, ALU.add).then_inc(s_ev, 1)

            def maxima(j):
                r = ROWS[j]
                w0, w1 = key_window(j)
                dve.wait_ge(s_ev, 4 * (j + 1))
                mx, nm, rsum, es = stats_of(j)
                link(dve.tensor_reduce(mx, Ssc[j % 2][0:r, :, 0:w1 - w0], AX.X, ALU.max))
                link(dve.tensor_tensor(mx, mx, sinks[0:r, :], ALU.max))
                link(dve.tensor_tensor(es, sinks[0:r, :], mx, ALU.subtract))
                dve.tensor_scalar(nm, mx, -1.0, None, ALU.mult).then_inc(m_ready, 1)

            def normalise(j):
                r = ROWS[j]
                n = P if j == 0 else KW if j < NP else WIN + LS
                mx, nm, rsum, es = stats_of(j)
                sc = Ssc[j % 2][0:r, :, 0:n]
                dve.wait_ge(p_exp, (NQ + 1) * (j + 1))
                link(dve.tensor_tensor(rsum, rsum, es, ALU.add))
                link(dve.reciprocal(rsum, rsum))
                dve.tensor_tensor(sc, sc, bcast(rsum.unsqueeze(2), [r, NQ, n]), ALU.mult).then_inc(p_ready, 1)

            low_unit(SPLIT_AT[-1])
            for j in range(NT + 1):
                if j < NT:
                    scores(j, 0)
                fill(j, 0)
                if j < NT:
                    scores(j, 1)
                if j >= 1:
                    normalise(j - 1)
                fill(j, 1)
                if j < NT:
                    maxima(j)
                fill(j, 2)
                fill(j, 3)
                if j in SPLIT_AT:
                    low_unit(SPLIT_AT[j])

            for j in range(NT):
                mod_evac(ADA_STATE[j], 3 + ADA_STATE[j] % 2)
                dve.wait_ge(pe_u, j + 1)
                for c in range(2 if j < NP else 1):
                    n = 2 * j + c
                    s0, s1 = (n, n + 1) if j < NP else (NCH + 1, NCH + 2)
                    for a in range(2):
                        last = dve.scalar_tensor_tensor(S[:, s1, a, :], S[:, s0, a, :], gend[:, a, n:n + 1],
                                                        bank[6 + c][:, a * DV:(a + 1) * DV], ALU.mult, ALU.add)
                        if a == 0 or c == 0 and j < NP:
                            link(last)
                        else:
                            last.then_inc(u_ev, 1)
                            dve.wait_ge(u_ev, j + 1)

            def mask(j):
                r = ROWS[j]
                dve.wait_ge(pe_a, j + 1)
                if j >= 2:
                    dve.wait_ge(pe_o, j - 1)
                for par in range(2):
                    a4 = At[0:r, j % 2, :, 0:r].rearrange("p (a b) t -> p a b t", b=2)[:, :, par, :]
                    for up, mk in ((0, tri), (1, tup)):
                        src = bank[1 + par][0:r, 2 * up * P:2 * (up + 1) * P].rearrange("p (a t) -> p a t", a=2)[:, :, 0:r]
                        last = dve.copy_predicated(a4, bcast(mk[0:r, 0:r].bitcast(i32).unsqueeze(1), [r, 2, r]), src)
                        if up == 0 or par == 0:
                            link(last)
                last.then_inc(a_ev, 1)

            def gated(j):
                r = ROWS[j]
                dve.wait_ge(o_sq, j + 1)
                gx = gex[0:r, j % 2, :]
                o = osb[0:r, j % 2, :]
                link(dve.tensor_scalar(gx, gx, 1.0, None, ALU.add))
                link(dve.reciprocal(gx, gx))
                link(dve.tensor_tensor(gx, gx, grg[0:r, j, :], ALU.mult))
                h3 = [r, H, DV]
                gx3, o3 = gx.rearrange("p (h v) -> p h v", h=H), o.rearrange("p (h v) -> p h v", h=H)
                link(dve.tensor_tensor(gx3, gx3, bcast(nw[0:r, :].unsqueeze(1), h3), ALU.mult))
                link(dve.tensor_tensor(o3, o3, bcast(small[0:r, 8 * (j % 2):8 * (j % 2) + H].unsqueeze(2), h3), ALU.mult))
                if j >= 1:
                    dve.wait_ge(pe_og, j)
                dve.tensor_tensor(og[0:r, :], o, gx, ALU.mult).then_inc(og_ready, 1)

            dve.wait_ge(at_zero, 1)
            for j in range(NT + 2):
                if j < NT:
                    mask(j)
                if j >= 2:
                    gated(j - 2)
                mod_evac(ADA_GLA[j], 6 * (j % 2))

            dve.wait_ge(s_gt1, 32)
            dve.wait_ge(s_x, 64)

            def ln_stats(x, j, done):
                r = ROWS[j]
                st = stat[0:r, j % 2, :]
                link(dve.bn_stats(st[:, 0:6], x[:, 0:512]))
                link(dve.bn_stats(st[:, 6:12], x[:, 512:D]))
                dve.bn_aggr(st[:, 12:14], st[:, 0:12]).then_inc(done, 1)

            def ln_finish(x, j, rows):
                r = ROWS[j]
                st = stat[0:r, j % 2, :]
                link(dve.tensor_scalar(x, x, st[:, 12:13], st[:, 13:14], ALU.subtract, ALU.mult))
                link(dve.tensor_tensor(x, x, rows[0:r, 0, :], ALU.mult))

            def logits(j):
                r = ROWS[j]
                dve.wait_ge(pe_rt, j + 1)
                dve.tensor_tensor(lg[0:r, j, :], bank[7][0:r, 0:NG + E], rb[0:r, :], ALU.add).then_inc(rt_ev, 1)

            def residual(j):
                r = ROWS[j]
                md = modP if j < NP else modS
                x = x_tok[0:r, j, :]
                dve.wait_ge(pe_y, j + 1)
                for half in range(2):
                    c = slice(512 * half, 512 * (half + 1))
                    dve.tensor_tensor(ytmp[0:r, c], bank[1 + 2 * (j % 2) + half][0:r, :], md[0][0:r, c], ALU.mult).then_inc(y_ev, 1)
                dve.wait_ge(y_ev, 2 * (j + 1))
                link(dve.scalar_tensor_tensor(x, x, ALPHA, ytmp[0:r, :], ALU.mult, ALU.add))
                ln_stats(x, j, v_ready)

            def modulated(j):
                r = ROWS[j]
                md = modP if j < NP else modS
                x = x_tok[0:r, j, :]
                dve.wait_ge(v_ln, j + 1)
                if j == 0:
                    dve.wait_ge(s_ln1, 32)
                    dve.wait_ge(s_modb, 64)
                ln_finish(x, j, ln1)
                link(dve.tensor_tensor(x, x, ln1[0:r, 1, :], ALU.add))
                if j >= 2:
                    dve.wait_ge(h2_st[j % 2], 16 * (j // 2))
                    dve.wait_ge(pe_ht, 2 * (j - 1))
                link(dve.scalar_tensor_tensor(h2[0:r, j % 2, :], md[2][0:r, :], 1.0, x, ALU.add, ALU.mult))
                dve.tensor_tensor(h2[0:r, j % 2, :], h2[0:r, j % 2, :], md[1][0:r, :], ALU.add).then_inc(h2_ready, 1)

            for j in range(NT + 1):
                if j < NT:
                    residual(j)
                    modulated(j)
                if j >= 1:
                    logits(j - 1)

            R5, R4 = [P, NT, E], [P, NT, NG]
            g, ex = lg[:, :, 0:NG], lg[:, :, NG:NG + E]

            def q5(i):
                return rt[:, i, :].rearrange("p (j e) -> p j e", j=NT)

            def q4(i):
                return rt[:, i, 0:NT * NG].rearrange("p (j e) -> p j e", j=NT)

            def over(i, shape):
                return bcast(rs[:, i, :].unsqueeze(2), shape)

            def first_max(v, mxi, eq, out, n, shape):
                link(dve.tensor_tensor(eq, v, over(mxi, shape), ALU.is_equal))
                link(dve.tensor_tensor(eq, eq, bcast(iow[:, 0:n].unsqueeze(1), shape), ALU.mult))
                link(dve.tensor_reduce(rs[:, 9, :], eq, AX.X, ALU.max))
                link(dve.tensor_tensor(out, eq, over(9, shape), ALU.is_equal))

            dve.wait_ge(rt_ev, NT)
            link(dve.tensor_reduce(rs[:, 0, :], g, AX.X, ALU.max))
            link(dve.tensor_tensor(q4(0), g, over(0, R4), ALU.subtract))
            first_max(g, 0, q4(1), q4(2), NG, R4)
            link(dve.tensor_scalar(q4(2), q4(2), 1e30, -1e30, ALU.mult, ALU.add))
            link(dve.tensor_tensor(ex.rearrange("p j (g e) -> p j g e", g=NG), ex.rearrange("p j (g e) -> p j g e", g=NG),
                                   bcast(q4(2).unsqueeze(3), [P, NT, NG, NE]), ALU.add))
            link(dve.tensor_reduce(rs[:, 3, :], ex, AX.X, ALU.max))
            first_max(ex, 3, q5(6), q5(4), E, R5)
            link(dve.scalar_tensor_tensor(q5(6), q5(4), -2e30, ex, ALU.mult, ALU.add))
            link(dve.tensor_reduce(rs[:, 4, :], q5(6), AX.X, ALU.max))
            first_max(q5(6), 4, q5(7), q5(5), E, R5)
            dve.tensor_tensor(q5(3), q5(4), q5(5), ALU.add).then_inc(oh_ready, 1)
            dve.tensor_tensor(rs[:, 5, :], rs[:, 4, :], rs[:, 3, :], ALU.subtract).then_inc(r_ex0, 1)

            dve.wait_ge(pe_rank, 1)
            cnt = bank[0][:, NT * E:(NT + 1) * E]
            link(dve.tensor_copy(cnti[:, :], cnt[0:1, :]))
            link(dve.tensor_scalar(ov[:, 1, :], cnt, float(P), None, ALU.is_gt))
            for m in range(2, OVT + 1):
                link(dve.scalar_tensor_tensor(ov[:, 1, :], cnt, float(m * P), ov[:, 1, :], ALU.is_gt, ALU.add))
            link(dve.tensor_copy(ov[:, 2, :], ov[:, 1, :]))
            a, sh = 2, 1
            while sh < E:
                link(dve.tensor_copy(ov[:, 5 - a, 0:sh], ov[:, a, 0:sh]))
                link(dve.tensor_tensor(ov[:, 5 - a, sh:E], ov[:, a, sh:E], ov[:, a, 0:E - sh], ALU.add))
                a, sh = 5 - a, 2 * sh
            link(dve.tensor_tensor(ov[:, 4, :], ov[:, a, :], ov[:, 1, :], ALU.subtract))
            link(dve.tensor_scalar(ov[:, 4, :], ov[:, 4, :], float(P), float(E * P - P), ALU.mult, ALU.add))
            link(dve.tensor_tensor(ov[:, 4, :], ov[:, 4, :], ov[:, 0, :], ALU.subtract))
            rank = bank[0][:, 0:NT * E].rearrange("p (j e) -> p j e", j=NT)
            link(dve.scalar_tensor_tensor(q5(6), rank, float(P), bcast(ov[:, 4, :].unsqueeze(1), R5), ALU.is_ge, ALU.mult))
            link(dve.tensor_tensor(q5(7), rank, bcast(ov[:, 0, :].unsqueeze(1), R5), ALU.add))
            link(dve.tensor_tensor(q5(6), q5(6), q5(7), ALU.add))
            for k in range(2):
                link(dve.tensor_tensor(q5(7), q5(6), q5(4 + k), ALU.mult))
                link(dve.tensor_reduce(rs[:, 6 + k, :], q5(7), AX.X, ALU.add))
                last = dve.tensor_copy(posi[:, k, :], rs[:, 6 + k, :])
                if k == 0:
                    link(last)
            last.then_inc(pos_ready, 1)
            dve.wait_ge(r_ex, 1)
            link(dve.tensor_reduce(rs[:, 1, :], q4(0), AX.X, ALU.add))
            link(dve.tensor_scalar(rs[:, 2, :], rs[:, 5, :], 1.0, None, ALU.add))
            link(dve.tensor_tensor(rs[:, 1, :], rs[:, 1, :], rs[:, 2, :], ALU.mult))
            link(dve.reciprocal(wts[:, 0, :], rs[:, 1, :]))
            link(dve.tensor_tensor(wts[:, 1, :], wts[:, 0, :], rs[:, 5, :], ALU.mult))
            link(dve.tensor_copy(ovi[0:1, 0:1], ov[0:1, a, E - 1:E]))
            for b in range(NOV):
                link(dve.tensor_scalar(ov[0:1, 1, :], ov[0:1, a, :], float(b), None, ALU.is_le))
                link(dve.tensor_reduce(rs[0:1, 8, 0:1], ov[0:1, 1, :], AX.X, ALU.add))
                link(dve.tensor_scalar(rs[0:1, 8, 0:1], rs[0:1, 8, 0:1], float(E - 1), None, ALU.min))
                last = dve.tensor_copy(ovi[0:1, b + 1:b + 2], rs[0:1, 8, 0:1])
                if b < NOV - 1:
                    link(last)
            last.then_inc(ov_ready, 1)
            def low_w(r, src, w):
                dve.wait_ge(wh_ready, w)
                dve.tensor_tensor(wsplit[:, r, 1, :], src, wsplit[:, r, 0, :].bitcast(f32), ALU.subtract).then_inc(wl_ready, 1)

            def expert_w(e, r, i):
                low_w(r, slot(N0 + 3 * e + r), at(low_count(e, r), 6, i))

            expert_w(0, 0, None)
            expert_w(0, 1, None)
            dve.wait_ge(pe_tbl, 1)
            ent = bank[7][:, 0:NBLK]
            link(dve.tensor_copy(dsti[:, :], ent))
            link(dve.tensor_scalar(fl[:, :], ent, float(KSTEP), -float(KSTEP), ALU.is_ge, ALU.mult))
            dve.tensor_tensor(srci[:, :], ent, fl[:, :], ALU.add).then_inc(tbl_ready, 1)

            def low_x(a, w):
                for half in range(2):
                    dve.wait_ge(xe_a, w + half)
                    k = slice(4 * half, 4 * half + 4)
                    dve.tensor_tensor(xl[:, a, k, :], bank[half][:, :].rearrange("p (k t) -> p k t", k=4),
                                      xh[:, a, k, :].bitcast(f32), ALU.subtract).then_inc(xe_l, 1)

            def hidden(a, w):
                dve.wait_ge(sg_done, w)
                dve.tensor_tensor(hid[:, a, :], bank[2 + a][:, FF:2 * FF], sgl[:, a, :], ALU.mult).then_inc(hid_done, 1)

            def low_h(a, w):
                dve.wait_ge(hT_ev, w)
                dve.tensor_tensor(hl[:, a, :, :], bank[4][:, 0:FF].rearrange("p (k t) -> p k t", k=NF),
                                  hh[:, a, :, :].bitcast(f32), ALU.subtract).then_inc(hT_l, 1)

            def evac_y(a, w, free):
                dve.wait_ge(pe_dn, w)
                if free is not None:
                    dve.wait_ge(s_sc[a], free)
                dve.tensor_copy(ye[:, a, 512:D], bank[6][:, :]).then_inc(y_d, 1)

            def step(e, i, last=False):
                x, b = e % 2, (e - 1) % 2
                low_h(b, at(e, 2, i))
                if not last:
                    low_x(b, at(2 * (e + 1) + 1, 4, i))
                    expert_w(e + 1, 0, i)
                hidden(x, at(e + 1, 2, i))
                if not last:
                    expert_w(e + 1, 1, i)
                evac_y(b, at(e, 2, i), at(16 * ((e - 1) // 2), 16, i) if e >= 3 or i is not None else None)
                expert_w(e, 2, i)

            low_x(0, 1)
            low_x(1, 3)
            expert_w(1, 0, None)
            hidden(0, 1)
            expert_w(1, 1, None)
            expert_w(0, 2, None)
            step(1, None)
            step(2, None)
            with dve.Fori(1, E // 2 - 1) as i:
                step(1, i)
                step(2, i)
            step(E - 1, None, last=True)
            low_h(1, E)
            evac_y(1, E, 16 * (E // 2 - 1))
            nov = dve.value_load(ovi[0:1, 0:1], min_val=0, max_val=NOV)
            with dve.If(nov > 0):
                with dve.Fori(0, nov) as i:
                    for r in range(3):
                        low_w(r, ring[:, r, :], i * 3 + (3 * E + r + 1))
                    low_x(0, i * 2 + 2 * E + 1)
                    hidden(0, i + E + 1)
                    low_h(0, i + E + 1)
                    evac_y(0, i + E + 1, i * 16 + 16 * (E // 2))

            dve.wait_ge(s_ln2, 32)
            dve.wait_ge(s_gt2, 32)
            def summed(j):
                r = ROWS[j]
                y = ring[0:r, j, 0:D]
                dve.wait_ge(f_a, j + 1)
                dve.scalar_tensor_tensor(y, ring[0:r, j, D:2 * D], wts[0:r, 1, j:j + 1], y, ALU.mult, ALU.add).then_inc(f_s, 1)

            def final_residual(j):
                r = ROWS[j]
                x = x_tok[0:r, j, :]
                dve.wait_ge(f_m, j + 1)
                link(dve.scalar_tensor_tensor(x, x, ALPHA, ring[0:r, j, 0:D], ALU.mult, ALU.add))
                if j >= 2:
                    dve.wait_ge(f_l, j - 1)
                ln_stats(x, j, f_v)

            def gained(j):
                x = x_tok[0:ROWS[j], j, :]
                dve.wait_ge(f_l, j + 1)
                dve.tensor_tensor(x, x, ln2[0:ROWS[j], 0, :], ALU.mult).then_inc(f_g, 1)

            summed(0)
            for j in range(NT + 1):
                if j + 1 < NT:
                    summed(j + 1)
                if j < NT:
                    final_residual(j)
                if j >= 1:
                    gained(j - 1)


_INS = ["x_prompt", "x_sample", "c_prompt", "c_sample", "state_gla", "cache_swa_k", "cache_swa_v",
        "ada_w", "ada_b", "w_in", "gla_a2_w", "gla_a2_b", "gla_norm_w", "swa_sinks", "w_o", "ln1_g", "ln1_b",
        "router_g_w", "router_g_b", "router_e_w", "router_e_b", "moe_w_gate", "moe_w_up", "moe_w_down",
        "ln2_g", "ln2_b"]
_OUTS = [(1, 512, 1024), (1, 32, 1024), (1, 1, 4, 64, 128), (1, 1, 128, 2, 64), (1, 1, 128, 2, 64),
         (1, 1, 4, 64, 128), (1, 1, 128, 2, 64), (1, 1, 128, 2, 64)]


def kernel(**inputs):
    import numpy as _np
    import concourse.bacc as _bacc
    from concourse import mybir as _mybir
    from concourse.bass_utils import run_bass_kernel_spmd as _run

    nc = _bacc.Bacc("TRN2", target_bir_lowering=False, num_devices=1)
    arrays, args = {}, []
    for name in _INS:
        a = _np.ascontiguousarray(inputs[name])
        arrays[f"in_{name}_dram"] = a
        args.append(nc.dram_tensor(f"in_{name}_dram", a.shape, _mybir.dt.from_np(a.dtype), kind="ExternalInput").ap())
    for i, shape in enumerate(_OUTS):
        args.append(nc.dram_tensor(f"out_{i}_dram", shape, _mybir.dt.float32, kind="ExternalOutput").ap())
    hymba_stream_step(nc, *args)
    r = _run(nc, [arrays], core_ids=[0])
    return tuple(r.results[0][f"out_{i}_dram"] for i in range(len(_OUTS)))
```
